# Optimizing a Trainium2 kernel written in Bass

```python
import jax, jax.numpy as jnp
from jax import lax
import numpy as np

D_MODEL = 1024
BATCH = 1
SEQ = 128
DEPTH = 2
DEC_BATCH = 1
DEC_SEQ = 512
PAST_LEN = 128

GRID_W = 64
N_MIXERS = 2
N_REC_LAYERS = (DEPTH + 1) // 2
N_ATTN_LAYERS = DEPTH // 2
N_MOD = 6
EPS = 1e-6
NEG_INF = -1e30
REC_HEADS = 8
REC_DK = D_MODEL // REC_HEADS
REC_DV = D_MODEL // REC_HEADS
REC_CHUNK = 64
ATTN_HEADS = 16
ATTN_KV_HEADS = 4
ATTN_GROUPS = ATTN_HEADS // ATTN_KV_HEADS
HEAD_DIM = D_MODEL // ATTN_HEADS
WINDOW = 128
ATTN_SCALE = HEAD_DIM ** -0.5
ROPE_BASE = 10000.0
PEER_HEADS = 8
PEER_NKEYS = 128
PEER_EXPERTS = PEER_NKEYS * PEER_NKEYS
PEER_TOPK = 16
PEER_DQ = 256
PEER_DQ_HALF = PEER_DQ // 2
PEER_TOKEN_BLOCK = 128

kernel_name = 'hgrn2_swa_peer_diffusion_step'

def _rms_norm(x, w):
    xf = x.astype(jnp.float32)
    y = xf * lax.rsqrt(jnp.mean(xf * xf, axis=-1, keepdims=True) + EPS)
    return (y * w.astype(jnp.float32)).astype(x.dtype)

def _modulate(h, shift, scale):
    return h * (1 + scale) + shift

def _rope_2d(x):
    L = x.shape[1]
    rows = L // GRID_W
    row = jnp.repeat(jnp.arange(rows), GRID_W).astype(jnp.float32)
    col = (jnp.arange(L) % GRID_W).astype(jnp.float32)
    half = HEAD_DIM // 2
    nf = half // 2
    freqs = ROPE_BASE ** (-jnp.arange(nf, dtype=jnp.float32) / nf)

    def rot(xa, pos):
        ang = pos[:, None] * freqs[None, :]
        cos = jnp.cos(ang)[None, :, None, :]
        sin = jnp.sin(ang)[None, :, None, :]
        x1, x2 = xa[..., :nf], xa[..., nf:]
        return jnp.concatenate([x1 * cos - x2 * sin, x1 * sin + x2 * cos], axis=-1)

    xf = x.astype(jnp.float32)
    return jnp.concatenate([rot(xf[..., :half], row), rot(xf[..., half:], col)], axis=-1).astype(x.dtype)

def _gla_scan(q, k, v, logf, s0):
    B, L, H, _ = q.shape
    n = L // REC_CHUNK

    def chunks(t):
        return jnp.moveaxis(t.reshape(B, n, REC_CHUNK, H, t.shape[-1]), 1, 0)

    causal = jnp.tril(jnp.ones((REC_CHUNK, REC_CHUNK), dtype=bool))[None, :, :, None, None]

    def step(S, inp):
        qc, kc, vc, gc = inp
        b = jnp.cumsum(gc, axis=1)
        o_inter = jnp.einsum('bthk,bhkv->bthv', qc * jnp.exp(b), S)
        decay = jnp.exp(jnp.where(causal, b[:, :, None] - b[:, None, :], -jnp.inf))
        scores = jnp.einsum('btshk,bshk->bhts', qc[:, :, None] * decay, kc)
        o_intra = jnp.einsum('bhts,bshv->bthv', scores, vc)
        b_end = b[:, -1]
        S_new = jnp.exp(b_end)[..., None] * S + jnp.einsum('bshk,bshv->bhkv', kc * jnp.exp(b_end[:, None] - b), vc)
        return S_new, o_inter + o_intra

    S_fin, o = lax.scan(step, s0, (chunks(q), chunks(k), chunks(v), chunks(logf)))
    return jnp.moveaxis(o, 0, 1).reshape(B, L, H, -1), S_fin

def _rec_project(h, w_in, lb):
    B, L, _ = h.shape
    z = (h @ w_in).astype(jnp.float32)
    q, f_fwd, f_bwd, i, g = jnp.split(z, 5, axis=-1)
    heads = lambda t: t.reshape(B, L, REC_HEADS, -1)

    def forget(fz, lbd):
        log_f = jnp.logaddexp(jnp.log(lbd), jnp.log1p(-lbd) + jax.nn.log_sigmoid(fz))
        k = (1.0 - lbd) * jax.nn.sigmoid(-fz)
        return heads(k), heads(log_f)

    return heads(jax.nn.silu(q)), heads(i), forget(f_fwd, lb[0]), forget(f_bwd, lb[1]), heads(g)

def _bidir_scan(q, v, fwd, bwd, s0_fwd, s0_bwd):
    flip = lambda t: jnp.flip(t, axis=1)
    o_f, s_f = _gla_scan(q, fwd[0], v, fwd[1], s0_fwd)
    o_b, s_b = _gla_scan(flip(q), flip(bwd[0]), flip(v), flip(bwd[1]), s0_bwd)
    return o_f + flip(o_b), s_f, s_b

def _rec_mixer(hp, hs, s0_lat, w_in, lb, gn_w, w_out):
    def readout(o, g, dtype):
        B, L = o.shape[:2]
        y = _rms_norm(o, gn_w) * jax.nn.silu(g)
        return y.reshape(B, L, D_MODEL).astype(dtype) @ w_out

    q, v, fwd, bwd, g = _rec_project(hp, w_in, lb)
    zeros = jnp.zeros((hp.shape[0], REC_HEADS, REC_DK, REC_DV), jnp.float32)
    o, s_f, s_b = _bidir_scan(q, v, fwd, bwd, zeros, zeros)
    y_ctx = readout(o, g, hp.dtype)
    s0 = s0_lat.astype(jnp.float32)
    q, v, fwd, bwd, g = _rec_project(hs, w_in, lb)
    o, _, _ = _bidir_scan(q, v, fwd, bwd, s0[:, 0], s0[:, 1])
    y_lat = readout(o, g, hs.dtype)
    state = jnp.stack([s_f, s_b], axis=1).astype(hp.dtype)
    return y_ctx, y_lat, state

def _attn_project(h, w_qkv, qn_w, kn_w):
    B, L, _ = h.shape
    z = h @ w_qkv
    q, k, v = jnp.split(z, [ATTN_HEADS * HEAD_DIM, (ATTN_HEADS + ATTN_KV_HEADS) * HEAD_DIM], axis=-1)
    q = _rms_norm(q.reshape(B, L, ATTN_HEADS, HEAD_DIM), qn_w)
    k = _rms_norm(k.reshape(B, L, ATTN_KV_HEADS, HEAD_DIM), kn_w)
    return q, k, v.reshape(B, L, ATTN_KV_HEADS, HEAD_DIM)

def _softmax_with_sink(parts, sink):
    lead = parts[0].shape[:-1]
    sink_col = jnp.broadcast_to(sink.astype(jnp.float32).reshape(1, ATTN_KV_HEADS, ATTN_GROUPS, 1, 1), lead + (1,))
    p = jax.nn.softmax(jnp.concatenate(parts + [sink_col], axis=-1), axis=-1)
    out, start = [], 0
    for part in parts:
        out.append(p[..., start:start + part.shape[-1]])
        start += part.shape[-1]
    return out

def _ctx_attention(q, k, v, sink):
    B, L = q.shape[:2]
    qg = q.reshape(B, L, ATTN_KV_HEADS, ATTN_GROUPS, HEAD_DIM)
    s = jnp.einsum('blkgd,bskd->bkgls', qg, k, preferred_element_type=jnp.float32) * ATTN_SCALE
    (p,) = _softmax_with_sink([s], sink)
    o = jnp.einsum('bkgls,bskd->blkgd', p.astype(v.dtype), v)
    return o.reshape(B, L, ATTN_HEADS * HEAD_DIM)

def _latent_attention(q, k, v, k_ctx, v_ctx, sink):
    B, L = q.shape[:2]
    n = L // WINDOW
    qg = q.reshape(B, L, ATTN_KV_HEADS, ATTN_GROUPS, HEAD_DIM)
    pad = ((0, 0), (WINDOW, WINDOW), (0, 0), (0, 0))
    kp = jnp.pad(k, pad)
    vp = jnp.pad(v, pad)
    offs_q = jnp.arange(WINDOW)
    offs_k = jnp.arange(3 * WINDOW) - WINDOW

    def block(j):
        start = j * WINDOW
        qb = lax.dynamic_slice_in_dim(qg, start, WINDOW, axis=1)
        kb = lax.dynamic_slice_in_dim(kp, start, 3 * WINDOW, axis=1)
        vb = lax.dynamic_slice_in_dim(vp, start, 3 * WINDOW, axis=1)
        qpos = start + offs_q
        kpos = start + offs_k
        valid = (kpos[None, :] >= 0) & (kpos[None, :] < L) & (jnp.abs(qpos[:, None] - kpos[None, :]) <= WINDOW)
        s_loc = jnp.einsum('bqkgd,bskd->bkgqs', qb, kb, preferred_element_type=jnp.float32) * ATTN_SCALE
        s_loc = jnp.where(valid, s_loc, NEG_INF)
        s_ctx = jnp.einsum('bqkgd,bskd->bkgqs', qb, k_ctx, preferred_element_type=jnp.float32) * ATTN_SCALE
        p_loc, p_ctx = _softmax_with_sink([s_loc, s_ctx], sink)
        return (jnp.einsum('bkgqs,bskd->bqkgd', p_loc.astype(vb.dtype), vb)
                + jnp.einsum('bkgqs,bskd->bqkgd', p_ctx.astype(v_ctx.dtype), v_ctx))

    o = lax.map(block, jnp.arange(n))
    return jnp.moveaxis(o, 0, 1).reshape(B, L, ATTN_HEADS * HEAD_DIM)

def _attn_mixer(hp, hs, k_cache, v_cache, w_qkv, qn_w, kn_w, sink, w_out):
    qp, kp, vp = _attn_project(hp, w_qkv, qn_w, kn_w)
    y_ctx = _ctx_attention(qp, kp, vp, sink) @ w_out
    qs, ks, vs = _attn_project(hs, w_qkv, qn_w, kn_w)
    qs, ks = _rope_2d(qs), _rope_2d(ks)
    y_lat = _latent_attention(qs, ks, vs, k_cache, v_cache, sink) @ w_out
    return y_ctx, y_lat, kp, vp

def _peer(x, w_q, sub_keys, u, v):
    T = x.shape[0]
    q = (x @ w_q).reshape(T, PEER_HEADS, 2, PEER_DQ_HALF)
    s = jnp.einsum('thpd,hpnd->thpn', q, sub_keys, preferred_element_type=jnp.float32)
    s1, i1 = lax.top_k(s[:, :, 0], PEER_TOPK)
    s2, i2 = lax.top_k(s[:, :, 1], PEER_TOPK)
    cand = (s1[..., :, None] + s2[..., None, :]).reshape(T, PEER_HEADS, PEER_TOPK * PEER_TOPK)
    cidx = (i1[..., :, None] * PEER_NKEYS + i2[..., None, :]).reshape(T, PEER_HEADS, PEER_TOPK * PEER_TOPK)
    best, pos = lax.top_k(cand, PEER_TOPK)
    eidx = jnp.take_along_axis(cidx, pos, axis=-1)
    gate = jax.nn.softmax(best, axis=-1)
    nb = T // PEER_TOKEN_BLOCK
    xs = x.reshape(nb, PEER_TOKEN_BLOCK, D_MODEL)
    ids = eidx.reshape(nb, PEER_TOKEN_BLOCK, PEER_HEADS * PEER_TOPK)
    gs = gate.reshape(nb, PEER_TOKEN_BLOCK, PEER_HEADS * PEER_TOPK).astype(x.dtype)

    def block(args):
        xb, ib, gb = args
        hb = jax.nn.gelu(jnp.einsum('tkd,td->tk', u[ib], xb), approximate=False)
        return jnp.einsum('tk,tkd->td', gb * hb, v[ib])

    return lax.map(block, (xs, ids, gs)).reshape(T, D_MODEL)

def setup_inputs(seed: int = 0) -> dict:
    key = jax.random.key(seed)
    ks = jax.random.split(key, 23)
    D = D_MODEL
    nrm = lambda k, shape, s: jax.random.normal(k, shape, jnp.float32) * s
    return {
        'x_prompt': nrm(ks[0], (BATCH, SEQ, D), 1.0),
        'x_sample': nrm(ks[1], (DEC_BATCH, DEC_SEQ, D), 1.0),
        'c': nrm(ks[2], (DEC_BATCH, D), 1.0),
        'state_rec': nrm(ks[3], (DEC_BATCH, N_REC_LAYERS, 2, REC_HEADS, REC_DK, REC_DV), 0.5),
        'cache_k': nrm(ks[4], (DEC_BATCH, N_ATTN_LAYERS, PAST_LEN, ATTN_KV_HEADS, HEAD_DIM), 1.0),
        'cache_v': nrm(ks[5], (DEC_BATCH, N_ATTN_LAYERS, PAST_LEN, ATTN_KV_HEADS, HEAD_DIM), 1.0),
        'c_ctx': nrm(ks[6], (D,), 1.0),
        'norm_w': 1.0 + nrm(ks[7], (DEPTH, 2, D), 0.02),
        'ada_w': nrm(ks[8], (DEPTH, D, N_MOD * D), 0.5 * D ** -0.5),
        'ada_b': nrm(ks[9], (DEPTH, N_MOD * D), 0.02),
        'rec_w_in': nrm(ks[10], (N_REC_LAYERS, D, 5 * D), D ** -0.5),
        'rec_lb': nrm(ks[11], (N_REC_LAYERS, 2, REC_HEADS * REC_DK), 0.5),
        'rec_gn_w': 1.0 + nrm(ks[12], (N_REC_LAYERS, REC_DV), 0.02),
        'rec_w_out': nrm(ks[13], (N_REC_LAYERS, D, D), D ** -0.5),
        'attn_w_qkv': nrm(ks[14], (N_ATTN_LAYERS, D, (ATTN_HEADS + 2 * ATTN_KV_HEADS) * HEAD_DIM), D ** -0.5),
        'attn_qn_w': 1.0 + nrm(ks[15], (N_ATTN_LAYERS, HEAD_DIM), 0.02),
        'attn_kn_w': 1.0 + nrm(ks[16], (N_ATTN_LAYERS, HEAD_DIM), 0.02),
        'attn_sink': nrm(ks[17], (N_ATTN_LAYERS, ATTN_HEADS), 1.0),
        'attn_w_out': nrm(ks[18], (N_ATTN_LAYERS, ATTN_HEADS * HEAD_DIM, D), (ATTN_HEADS * HEAD_DIM) ** -0.5),
        'peer_w_q': nrm(ks[19], (DEPTH, D, PEER_HEADS * PEER_DQ), D ** -0.5),
        'peer_keys': nrm(ks[20], (DEPTH, PEER_HEADS, 2, PEER_NKEYS, PEER_DQ_HALF), PEER_DQ_HALF ** -0.5),
        'peer_u': nrm(ks[21], (DEPTH, PEER_EXPERTS, D), D ** -0.5),
        'peer_v': nrm(ks[22], (DEPTH, PEER_EXPERTS, D), PEER_HEADS ** -0.5),
    }

def reference(x_prompt, x_sample, c, state_rec, cache_k, cache_v, c_ctx, norm_w, ada_w, ada_b,
              rec_w_in, rec_lb, rec_gn_w, rec_w_out, attn_w_qkv, attn_qn_w, attn_kn_w, attn_sink,
              attn_w_out, peer_w_q, peer_keys, peer_u, peer_v):
    lb_p = jax.nn.softmax(rec_lb.astype(jnp.float32), axis=0)
    lb_cs = jnp.cumsum(lb_p, axis=0)
    lower_bounds = lb_cs - lb_cs[0]

    xp, xs = x_prompt, x_sample
    Bp, Lp = xp.shape[:2]
    Bs, Ls = xs.shape[:2]
    cond_ctx = jax.nn.silu(c_ctx)[None, :]
    cond_lat = jax.nn.silu(c)
    new_rec, new_k, new_v = [], [], []
    for i in range(DEPTH):
        mod_p = (cond_ctx @ ada_w[i] + ada_b[i]).reshape(1, N_MOD, 1, D_MODEL)
        mod_s = (cond_lat @ ada_w[i] + ada_b[i]).reshape(Bs, N_MOD, 1, D_MODEL)
        hp = _modulate(_rms_norm(xp, norm_w[i, 0]), mod_p[:, 0], mod_p[:, 1])
        hs = _modulate(_rms_norm(xs, norm_w[i, 0]), mod_s[:, 0], mod_s[:, 1])
        r = i // N_MIXERS
        if i % N_MIXERS == 0:
            yp, ys, st = _rec_mixer(hp, hs, state_rec[:, r], rec_w_in[r], lower_bounds[r],
                                    rec_gn_w[r], rec_w_out[r])
            new_rec.append(st)
        else:
            yp, ys, kc, vc = _attn_mixer(hp, hs, cache_k[:, r], cache_v[:, r], attn_w_qkv[r],
                                         attn_qn_w[r], attn_kn_w[r], attn_sink[r], attn_w_out[r])
            new_k.append(kc)
            new_v.append(vc)
        xp = xp + mod_p[:, 2] * yp
        xs = xs + mod_s[:, 2] * ys
        hp = _modulate(_rms_norm(xp, norm_w[i, 1]), mod_p[:, 3], mod_p[:, 4])
        hs = _modulate(_rms_norm(xs, norm_w[i, 1]), mod_s[:, 3], mod_s[:, 4])
        tokens = jnp.concatenate([hp.reshape(-1, D_MODEL), hs.reshape(-1, D_MODEL)], axis=0)
        f = _peer(tokens, peer_w_q[i], peer_keys[i], peer_u[i], peer_v[i])
        xp = xp + mod_p[:, 5] * f[:Bp * Lp].reshape(Bp, Lp, D_MODEL)
        xs = xs + mod_s[:, 5] * f[Bp * Lp:].reshape(Bs, Ls, D_MODEL)
    new_state_rec = jnp.stack(new_rec, axis=1)
    new_cache_k = jnp.stack(new_k, axis=1)
    new_cache_v = jnp.stack(new_v, axis=1)
    return (xp, xs, new_state_rec, new_cache_k, new_cache_v)


_drawn_inputs = setup_inputs


def setup_inputs(seed=0):
    import zlib

    import numpy as np

    out = dict(_drawn_inputs(seed))
    spreads = {}
    factors = {'state_rec': 8.0,
     'cache_k': 3.689,
     'cache_v': 2.963,
     'rec_gn_w': 8.0,
     'attn_qn_w': 8.0,
     'attn_sink': 64.0}
    for name, (base, spread) in spreads.items():
        noise = np.random.default_rng([zlib.crc32(name.encode()), seed]).standard_normal(out[name].shape)
        drawn = base * np.exp(spread * noise) if base else spread * noise
        out[name] = __import__('jax').numpy.asarray(drawn.astype(out[name].dtype))
    for name, factor in factors.items():
        out[name] = (out[name] * factor).astype(out[name].dtype)
    return out
```

```python
from contextlib import ExitStack

import numpy as np

import concourse.bass as bass
from concourse import mybir

P = 128
D = 1024
KD = D // P
CTX, LAT = 128, 512
T = CTX + LAT
NT = T // P
NMOD = 6
RH = 8
AH, AKV, HD = 16, 4, 64
HALFT = T // 2
BANK = 512
C0 = BANK - CTX
EPS = 1e-6
NEG = -1e30
LEVELS = 7
PH, NK, TK = 8, 128, 16
SCALE = HD ** -0.5

F32 = mybir.dt.float32
BF16 = mybir.dt.bfloat16
U32 = mybir.dt.uint32
I32 = mybir.dt.int32
ALU = mybir.AluOpType
ACT = mybir.ActivationFunctionType
AX = mybir.AxisListType.X
ds = bass.ds


def segments():
    return ((slice(0, CTX), slice(C0, BANK)), (slice(CTX, T), slice(BANK, BANK + LAT)))


def modulation(nc, cst, ada_w, adab_in, modT, tag):
    with nc.cleanup_on_exit(), ExitStack() as ctx:
        sb = lambda n, s, d=F32: ctx.enter_context(nc.sbuf_tensor(n + tag, s, d))
        sem = lambda n: nc.alloc_semaphore(n + tag)
        wst = sb("ada_wst", [P, 2, 4, KD, P])
        adab = sb("ada_bias", [P, NMOD * KD, 2])
        ps = [ctx.enter_context(nc.psum_tensor(f"ada_ps{s}" + tag, [P, 4, 2], F32)) for s in range(2)]
        w_in = [sem(f"ada_w_in{s}") for s in range(2)]
        w_free = sem("ada_w_free")
        b_in = sem("ada_b_in")
        prod = sem("ada_prod")
        psum_free = sem("ada_psum_free")
        block = ctx.enter_context(nc.Block())

        @block.sync
        def _(sp):
            sp.dma_start(adab[:], adab_in).then_inc(b_in, 16)
            with sp.Fori(0, 6) as i:
                for s in range(2):
                    sp.wait_ge(w_free, 2 * i + s + 1)
                    sp.dma_start(wst[:, s], ada_w[2 * i + s]).then_inc(w_in[s], 16)

        @block.tensor
        def _(pe):
            pe.sem_inc(w_free, 2)
            with pe.Fori(0, 6) as i:
                for s in range(2):
                    pe.wait_ge(w_in[s], 16 * i + 16)
                    pe.wait_ge(psum_free, 2 * i + s + 1)
                    for m in range(4):
                        for k in range(KD):
                            last = nc.tensor.matmul(ps[s][:, m, :], wst[:, s, m, k, :], cst.cond[:, k, :],
                                                    start=(k == 0), stop=(k == KD - 1))
                    last.then_inc(prod, 1)
                    pe.wait_ge(prod, 2 * i + s + 1)
                    pe.sem_inc(w_free, 1)

        @block.vector
        def _(dve):
            dve.sem_inc(psum_free, 2)
            dve.wait_ge(b_in, 16)
            with dve.Fori(0, 6) as i:
                for s in range(2):
                    dve.wait_ge(prod, 2 * i + s + 1)
                    at = ds(8 * i + 4 * s, 4)
                    nc.vector.tensor_tensor(modT[:, at, :], ps[s][:], adab[:, at, :], ALU.add).then_inc(psum_free, 1)


class Norm:

    def __init__(self, nc, ctx, cst, tag, modT, which, sq, hT, sum_ps):
        sem = lambda n: nc.alloc_semaphore(n + tag)
        self.nc, self.cst, self.modT, self.which = nc, cst, modT, which
        self.sq, self.hT, self.sum_ps = sq, hT, sum_ps
        self.rstd = ctx.enter_context(nc.sbuf_tensor("rstd" + tag, [P, T], F32))
        self.gain = ctx.enter_context(nc.sbuf_tensor("gain" + tag, [P, KD, 2], F32))
        self.squares = sem("norm_squares")
        self.sums = sem("norm_sums")
        self.inv = sem("norm_inv")
        self.root = sem("norm_root")
        self.ready = sem("norm_ready")

    def act(self, act):
        nc = self.nc
        nc.scalar.activation(self.sq[:], self.cst.XT[:], ACT.Square).then_inc(self.squares, 1)
        act.wait_ge(self.inv, 1)
        nc.scalar.activation(self.rstd[:], self.rstd[:], ACT.Sqrt).then_inc(self.root, 1)

    def pe(self, pe):
        nc = self.nc
        pe.wait_ge(self.squares, 1)
        for tok, col in segments():
            for k in range(KD):
                last = nc.tensor.matmul(self.sum_ps[:, col], self.cst.ones[:], self.sq[:, k, tok],
                                        start=(k == 0), stop=(k == KD - 1))
        last.then_inc(self.sums, 1)

    def dve(self, dve):
        nc, n0 = self.nc, 3 * self.which * KD
        shift, scale = self.modT[:, n0:n0 + KD, :], self.modT[:, n0 + KD:n0 + 2 * KD, :]
        nc.vector.scalar_tensor_tensor(self.gain[:], scale, 1.0, self.cst.normw[:, self.which],
                                       op0=ALU.add, op1=ALU.mult)
        dve.wait_ge(self.sums, 1)
        nc.vector.tensor_scalar(self.rstd[:], self.sum_ps[:, C0:C0 + T], 1.0 / D, EPS, ALU.mult, ALU.add)
        dve.drain()
        nc.vector.reciprocal(self.rstd[:], self.rstd[:]).then_inc(self.inv, 1)
        dve.wait_ge(self.root, 1)
        nc.vector.tensor_tensor(self.hT[:], self.cst.XT[:],
                                self.rstd[:].unsqueeze(1).to_broadcast([P, KD, T]), ALU.mult)
        dve.drain()
        for k in range(KD):
            for c, tok in ((0, slice(0, CTX)), (1, slice(CTX, T))):
                last = nc.vector.tensor_scalar(self.hT[:, k, tok], self.hT[:, k, tok], self.gain[:, k, c:c + 1],
                                               shift[:, k, c:c + 1], ALU.mult, ALU.add)
        dve.drain().then_inc(self.ready, 1)


def out_projection(nc, cst, w_out, yT, modT, tag):
    with nc.cleanup_on_exit(), ExitStack() as ctx:
        sem = lambda n: nc.alloc_semaphore(n + tag)
        wst = ctx.enter_context(nc.sbuf_tensor("wo_st" + tag, [P, 4, KD, P], F32))
        ps = [ctx.enter_context(nc.psum_tensor(f"wo_ps{s}" + tag, [P, 2 * BANK], F32)) for s in range(2)]
        w_in = [sem(f"wo_in{s}") for s in range(4)]
        w_free, prod, psum_free = sem("wo_free"), sem("wo_prod"), sem("wo_psum_free")
        block = ctx.enter_context(nc.Block())

        @block.sync
        def _(sp):
            for m in range(KD):
                if m >= 4:
                    sp.wait_ge(prod, m - 3)
                sp.dma_start(wst[:, m % 4], w_out[m]).then_inc(w_in[m % 4], 16)

        @block.tensor
        def _(pe):
            for m in range(KD):
                pe.wait_ge(w_in[m % 4], 16 * (m // 4 + 1))
                if m >= 2:
                    pe.wait_ge(psum_free, m - 1)
                for k in range(KD):
                    for tok, col in segments():
                        last = nc.tensor.matmul(ps[m % 2][:, col], wst[:, m % 4, k, :], yT[:, k, tok],
                                                start=(k == 0), stop=(k == KD - 1))
                last.then_inc(prod, 1)

        @block.vector
        def _(dve):
            for m in range(KD):
                dve.wait_ge(prod, m + 1)
                for c, (tok, col) in enumerate(segments()):
                    last = nc.vector.scalar_tensor_tensor(cst.XT[:, m, tok], ps[m % 2][:, col],
                                                          modT[:, 2 * KD + m, c:c + 1], cst.XT[:, m, tok],
                                                          op0=ALU.mult, op1=ALU.add)
                last.then_inc(psum_free, 1)


def rec_mixer(nc, cst, modT, w_in_d, gn_in, masks_in, st_in, st_out, yT):
    Q_, FF_, FB_, G_, V_ = range(5)
    with nc.cleanup_on_exit(), ExitStack() as ctx:
        sb = lambda n, s, d=F32: ctx.enter_context(nc.sbuf_tensor(n, s, d))
        sem = lambda n: nc.alloc_semaphore(n)
        hT = sb("rec_hT", [P, KD, T])
        ms = sb("rec_ms", [P, RH, T])
        wst = sb("rec_wst", [P, 5, KD, P])
        masks = sb("rec_masks", [P, 2 * LEVELS, P], I32)
        gn = sb("rec_gn", [P, 1])
        z = [{n: sb(f"rec_{n}{s}", [P, T]) for n in ("q", "g", "f0", "f1", "k0", "k1", "v")} for s in range(2)]
        ksum = sb("rec_ksum", [P, T])
        ql = [sb(f"rec_ql{i}", [P, T]) for i in range(3)]
        kl = [sb(f"rec_kl{i}", [P, T]) for i in range(3)]
        qf = [sb(f"rec_qf{d}", [P, T]) for d in range(2)]
        kf = [sb(f"rec_kf{d}", [P, T]) for d in range(2)]
        tot = [sb(f"rec_tot{d}", [P, 2 * T]) for d in range(2)]
        acc = sb("rec_acc", [P, T])
        kt = [sb(f"rec_kt{d}", [P, NT, P]) for d in range(2)]
        st = sb("rec_st", [P, 2, 4, P])
        sto = sb("rec_sto", [P, 2, P])
        oT = sb("rec_oT", [P, T])
        osq = sb("rec_osq", [P, T])
        psA = [ctx.enter_context(nc.psum_tensor(f"rec_psA{s}", [P, 2 * BANK], F32)) for s in range(2)]
        psB = [ctx.enter_context(nc.psum_tensor(f"rec_psB{s}", [P, 2 * BANK], F32)) for s in range(2)]
        norm = Norm(nc, ctx, cst, "_rec", modT, 0, yT, hT, psA[0])
        small_in = sem("rec_small_in")
        wsem = [sem(f"rec_w_in{n}") for n in range(5)]
        proj = sem("rec_proj")
        psa_read = sem("rec_psa_read")
        zsem = sem("rec_z")
        zfree = sem("rec_zfree")
        lvl = sem("rec_lvl")
        full = sem("rec_full")
        psb_read = sem("rec_psb_read")
        accr = sem("rec_accr")
        ktr = sem("rec_ktr")
        st_ld = sem("rec_st_ld")
        st_rdy = sem("rec_st_rdy")
        st_sv = sem("rec_st_sv")
        osr = sem("rec_osr")
        otr = sem("rec_otr")
        seen = sem("rec_seen")
        fin = sem("rec_fin")
        NB = 20
        TR0, UU, OO, NN = 15, 17, 18, 19
        block = ctx.enter_context(nc.Block())

        @block.sync
        def _(sp):
            sp.dma_start(masks[:], masks_in).then_inc(small_in, 16)
            sp.dma_start(gn[:], gn_in).then_inc(small_in, 16)

            def head(h, first):
                for n in range(5):
                    if not first:
                        sp.wait_ge(proj, 5 * h + n - 4)
                    sp.dma_start(wst[:, n], w_in_d[h, n]).then_inc(wsem[n], 16)
                if not first:
                    sp.wait_ge(full, NB * h)
                    sp.wait_ge(accr, h)
                for d in range(2):
                    sp.dma_start(st[:, d, 0, :], st_in[d, h]).then_inc(st_ld, 16)

            def store(h):
                sp.wait_ge(st_rdy, h + 1)
                for d in range(2):
                    sp.dma_start(st_out[d, h], sto[:, d, :]).then_inc(st_sv, 16)

            head(0, True)
            with sp.Fori(1, RH) as h:
                head(h, False)
                store(h - 1)
            store(RH - 1)
            sp.wait_ge(st_sv, 32 * RH)

        @block.tensor
        def _(pe):
            norm.pe(pe)
            pe.wait_ge(norm.ready, 1)

            def project(h, n):
                pe.wait_ge(wsem[n], 16 * h + 16)
                pe.wait_ge(psa_read, 5 * h + max(n, 1))
                ps = psA[n % 2]
                if n == V_:
                    for t in range(NT):
                        for k in range(KD):
                            last = nc.tensor.matmul(ps[:, C0 + P * t:C0 + P * t + P], hT[:, k, P * t:P * t + P],
                                                    wst[:, n, k, :], start=(k == 0), stop=(k == KD - 1))
                else:
                    for k in range(KD):
                        for tok, col in segments():
                            last = nc.tensor.matmul(ps[:, col], wst[:, n, k, :], hT[:, k, tok],
                                                    start=(k == 0), stop=(k == KD - 1))
                last.then_inc(proj, 1)

            def tiles(n, h, lhs, rhs, which=range(NT)):
                ps = psB[n % 2]
                for t in which:
                    a = slice(P * t, P * t + P)
                    last = nc.tensor.matmul(ps[:, C0 + P * t:C0 + P * t + P], lhs[:, a], rhs[:, a],
                                            start=True, stop=True)
                last.then_inc(full, 1)

            def head(h, s, nxt):
                zz = z[s]
                todo = [0, 1, 2, 3, 4] if nxt is not None else []
                for n in range(15):
                    if n % 3 == 0 and todo:
                        project(nxt, todo.pop(0))
                    pe.wait_ge(psb_read, NB * h + n + 1)
                    pe.wait_ge(lvl, 15 * h + n + 1)
                    if n == 0:
                        tiles(0, h, ksum, zz["q"])
                        continue
                    d, l = divmod(n - 1, LEVELS)
                    i = (n - 1) % 3
                    tiles(n, h, zz[f"k{d}"] if l == 0 else kl[i], ql[i])
                for d in range(2):
                    n = TR0 + d
                    pe.wait_ge(psb_read, NB * h + n + 1)
                    pe.wait_ge(accr, 3 * h + d + 1)
                    for t in range(NT):
                        last = nc.tensor.transpose(psB[n % 2][:, C0 + P * t:C0 + P * t + P],
                                                   kf[d][:, P * t:P * t + P], cst.ident[:])
                    last.then_inc(full, 1)
                n = UU
                pe.wait_ge(psb_read, NB * h + n + 1)
                pe.wait_ge(ktr, 2 * h + 2)
                for d in range(2):
                    for j in range(4):
                        t = (0 if j == 3 else j + 1) if d == 0 else (0 if j == 3 else 4 - j)
                        last = nc.tensor.matmul(psB[n % 2][:, BANK * d + P * j:BANK * d + P * j + P],
                                                kt[d][:, t, :], zz["v"][:, P * t:P * t + P], start=True, stop=True)
                last.then_inc(full, 1)
                n = OO
                pe.wait_ge(psb_read, NB * h + n + 1)
                pe.wait_ge(accr, 3 * h + 3)
                for t in range(NT):
                    a, o = slice(P * t, P * t + P), psB[n % 2][:, C0 + P * t:C0 + P * t + P]
                    last = nc.tensor.matmul(o, zz["v"][:, a], acc[:, a], start=True, stop=(t == 0))
                    if t > 0:
                        nc.tensor.matmul(o, st[:, 0, t - 1, :], qf[0][:, a], start=False, stop=False)
                        last = nc.tensor.matmul(o, st[:, 1, 4 - t, :], qf[1][:, a], start=False, stop=True)
                last.then_inc(full, 1)
                n = NN
                pe.wait_ge(psb_read, NB * h + n + 1)
                pe.wait_ge(osr, h + 1)
                for tok, col in segments():
                    last = nc.tensor.matmul(psB[n % 2][:, col], cst.ones[:], osq[:, tok], start=True, stop=True)
                last.then_inc(full, 1)

            for n in range(5):
                project(0, n)
            with pe.Fori(0, RH // 2 - 1) as i:
                head(2 * i, 0, 2 * i + 1)
                head(2 * i + 1, 1, 2 * i + 2)
            head(RH - 2, 0, RH - 1)
            head(RH - 1, 1, None)

        @block.scalar
        def _(act):
            norm.act(act)
            act.sem_inc(psa_read, 1)

            def evacuate(h, s):
                zz = z[s]
                act.wait_ge(zfree, h + 1)
                for n in range(5):
                    act.wait_ge(proj, 5 * h + n + 1)
                    src = psA[n % 2][:, C0:C0 + T]
                    if n in (Q_, G_):
                        dst = zz["q" if n == Q_ else "g"]
                        nc.scalar.activation(dst[:], src, ACT.Silu)
                    elif n in (FF_, FB_):
                        nc.scalar.activation(zz[f"f{n - FF_}"][:], src, ACT.Sigmoid)
                        nc.scalar.activation(zz[f"k{n - FF_}"][:], src, ACT.Sigmoid, scale=-1.0)
                    else:
                        nc.scalar.activation(zz["v"][:], src, ACT.Copy)
                    act.drain().then_inc(psa_read, 1)
                act.sem_inc(zsem, 1)

            def squares(h):
                act.wait_ge(otr, h + 1)
                nc.scalar.activation(osq[:], oT[:], ACT.Square).then_inc(osr, 1)

            evacuate(0, 0)
            with act.Fori(0, RH // 2 - 1) as i:
                evacuate(2 * i + 1, 1)
                squares(2 * i)
                evacuate(2 * i + 2, 0)
                squares(2 * i + 1)
            evacuate(RH - 1, 1)
            squares(RH - 2)
            squares(RH - 1)
            act.wait_ge(fin, 1)
            nc.scalar.activation(ms[:], ms[:], ACT.Sqrt).then_inc(fin, 1)

        @block.vector
        def _(dve):
            norm.dve(dve)
            dve.sem_inc(zfree, 2)
            dve.sem_inc(psb_read, 2)
            dve.wait_ge(small_in, 32)

            def build(h, s, n):
                zz = z[s]
                d, l = divmod(n - 1, LEVELS)
                i, H = (n - 1) % 3, 1 << l
                nb = T // H
                at = 2 * T - 2 * nb
                q_src, k_src = (ql[(i - 1) % 3], kl[(i - 1) % 3]) if l > 0 else (zz["q"], None)
                if n >= 4:
                    dve.wait_ge(full, NB * h + n - 2)
                if l == 0:
                    nc.vector.tensor_tensor(ql[i][:], zz["q"][:], zz[f"f{d}"][:], ALU.mult)
                else:
                    grow(d, l, q_src, ql[i], zz[f"k{d}"] if l == 1 else k_src, kl[i], zz)
                dve.drain().then_inc(lvl, 1)

            def grow(d, l, q_src, q_dst, k_src, k_dst, zz):
                H = 1 << l
                h2, nb = H // 2, T // H
                prev = zz[f"f{d}"][:] if l == 1 else tot[d][:, 2 * T - 4 * nb:2 * T - 2 * nb]
                pair = prev.rearrange("p (b e) -> p b e", e=2)
                if l < LEVELS:
                    nc.vector.tensor_tensor(tot[d][:, 2 * T - 2 * nb:2 * T - nb], pair[:, :, 0], pair[:, :, 1], ALU.mult)
                else:
                    nc.vector.tensor_tensor(tot[d][:, 2 * T - 2 * nb:2 * T - nb], pair[:, :, 0], pair[:, :, 1], ALU.mult)
                for src, dst, e in ((q_src, q_dst, 1 - d), (k_src, k_dst, d)):
                    sv = src[:].rearrange("p (b e x) -> p b e x", e=2, x=h2)
                    dv = dst[:].rearrange("p (b e x) -> p b e x", e=2, x=h2)
                    other = pair[:, :, 1 - e].unsqueeze(2).to_broadcast([P, nb, h2])
                    nc.vector.tensor_tensor(dv[:, :, e, :], sv[:, :, e, :], other, ALU.mult)
                    nc.vector.tensor_copy(dv[:, :, 1 - e, :], sv[:, :, 1 - e, :])

            def take(h, n):
                dve.wait_ge(full, NB * h + n + 1)
                dve.sem_inc(seen, 1)
                src = psB[n % 2][:, C0:C0 + T].rearrange("p (t x) -> p t x", x=P)
                dst = acc[:].rearrange("p (t x) -> p t x", x=P)
                if n == 0:
                    nc.vector.tensor_copy(dst, src).then_inc(psb_read, 1)
                else:
                    nc.vector.copy_predicated(dst, masks[:, n - 1, :].unsqueeze(1).to_broadcast([P, NT, P]),
                                              src).then_inc(psb_read, 1)
                dve.drain()

            def head(h, s, last):
                zz = z[s]
                dve.wait_ge(zsem, h + 1)
                nc.vector.tensor_tensor(ksum[:], zz["k0"][:], zz["k1"][:], ALU.add)
                dve.drain().then_inc(lvl, 1)
                for n in range(1, 15):
                    build(h, s, n)
                    take(h, n - 1)
                    if n % LEVELS == 0:
                        d = n // LEVELS - 1
                        i = (n - 1) % 3
                        grow(d, LEVELS, ql[i], qf[d], kl[i], kf[d], zz)
                        dve.drain().then_inc(accr, 1)
                take(h, 14)
                for d in range(2):
                    n = TR0 + d
                    dve.wait_ge(full, NB * h + n + 1)
                    nc.vector.tensor_copy(kt[d][:].rearrange("p t x -> p (t x)"),
                                          psB[n % 2][:, C0:C0 + T]).then_inc(psb_read, 1)
                    dve.drain().then_inc(ktr, 1)
                dve.wait_ge(full, NB * h + UU + 1)
                dve.wait_ge(st_ld, 32 * h + 32)
                if not (isinstance(h, int) and h == 0):
                    dve.wait_ge(st_sv, 32 * h)
                for d in range(2):
                    nc.vector.tensor_copy(sto[:, d, :], psB[UU % 2][:, BANK * d + 3 * P:BANK * d + 4 * P])
                for j in range(3):
                    for d in range(2):
                        t = j + 1 if d == 0 else 4 - j
                        decay = tot[d][:, 2 * T - 2 * NT + t:2 * T - 2 * NT + t + 1]
                        nc.vector.scalar_tensor_tensor(st[:, d, j + 1, :], st[:, d, j, :], decay,
                                                       psB[UU % 2][:, BANK * d + P * j:BANK * d + P * j + P],
                                                       op0=ALU.mult, op1=ALU.add)
                    dve.drain()
                dve.sem_inc(psb_read, 1)
                dve.sem_inc(st_rdy, 1)
                dve.sem_inc(accr, 1)
                dve.wait_ge(full, NB * h + OO + 1)
                nc.vector.tensor_copy(oT[:], psB[OO % 2][:, C0:C0 + T])
                nc.vector.tensor_tensor(yT[:, ds(h, 1), :].rearrange("p a t -> p (a t)"),
                                        psB[OO % 2][:, C0:C0 + T], zz["g"][:], ALU.mult)
                dve.drain()
                dve.sem_inc(otr, 1)
                dve.sem_inc(psb_read, 1)
                dve.sem_inc(zfree, 1)
                dve.wait_ge(full, NB * h + NN + 1)
                nc.vector.tensor_scalar(ms[:, ds(h, 1), :].rearrange("p a t -> p (a t)"),
                                        psB[NN % 2][:, C0:C0 + T], 1.0 / P, EPS, ALU.mult, ALU.add)
                dve.drain().then_inc(psb_read, 1)

            head(0, 0, False)
            head(1, 1, False)
            with dve.Fori(1, RH // 2) as i:
                head(2 * i, 0, False)
                head(2 * i + 1, 1, False)
            nc.vector.reciprocal(ms[:], ms[:]).then_inc(fin, 1)
            dve.wait_ge(fin, 2)
            nc.vector.scalar_tensor_tensor(yT[:], yT[:], gn[:, 0:1], ms[:], op0=ALU.mult, op1=ALU.mult)


def peer_scores(nc, cst, modT, wqk, h_hi, h_lo, vals, idxs, tag):
    NS = 2 * PH
    with nc.cleanup_on_exit(), ExitStack() as ctx:
        sb = lambda n, s, d=F32: ctx.enter_context(nc.sbuf_tensor(n + tag, s, d))
        sem = lambda n: nc.alloc_semaphore(n + tag)
        hT, sq = sb("ps_hT", [P, KD, T]), sb("ps_sq", [P, KD, T])
        wst = [sb(f"ps_wst{s}", [P, KD + 1, P]) for s in range(2)]
        qT = [sb(f"ps_qT{s}", [P, T]) for s in range(2)]
        sc = [sb(f"ps_sc{s}", [P, NT, P]) for s in range(2)]
        sc2 = sb("ps_sc2", [P, NT, P])
        v8, i8 = sb("ps_v8", [P, NT, TK]), sb("ps_i8", [P, NT, TK], U32)
        psA = [ctx.enter_context(nc.psum_tensor(f"ps_psA{s}" + tag, [P, 2 * BANK], F32)) for s in range(2)]
        psB = [ctx.enter_context(nc.psum_tensor(f"ps_psB{s}" + tag, [P, 2 * BANK], F32)) for s in range(2)]
        norm = Norm(nc, ctx, cst, "_ps" + tag, modT, 1, sq, hT, psA[0])
        w_in = [sem(f"ps_w_in{s}") for s in range(2)]
        qpr, qcp = sem("ps_qpr"), sem("ps_qcp")
        spr, scp = sem("ps_spr"), sem("ps_scp")
        top = sem("ps_top")
        qfree, sfree = sem("ps_qfree"), sem("ps_sfree")
        seen = sem("ps_seen")
        split = sem("ps_split")
        block = ctx.enter_context(nc.Block())

        @block.sync
        def _(sp):
            for s in range(2):
                sp.dma_start(wst[s][:], wqk[s]).then_inc(w_in[s], 16)
            with sp.Fori(1, NS // 2) as i:
                for s in range(2):
                    sp.wait_ge(spr, 2 * i + s - 1)
                    sp.dma_start(wst[s][:], wqk[2 * i + s]).then_inc(w_in[s], 16)

        @block.tensor
        def _(pe):
            norm.pe(pe)
            pe.wait_ge(norm.ready, 1)

            def query(i, s):
                n = 2 * i + s
                pe.wait_ge(w_in[s], 16 * i + 16)
                pe.wait_ge(qfree, n + 1)
                for k in range(KD):
                    for tok, col in segments():
                        last = nc.tensor.matmul(psA[s][:, col], wst[s][:, k, :], hT[:, k, tok],
                                                start=(k == 0), stop=(k == KD - 1))
                last.then_inc(qpr, 1)

            def score(i, s):
                n = 2 * i + s
                pe.wait_ge(qcp, n + 1)
                pe.wait_ge(sfree, n + 1)
                for t in range(NT):
                    last = nc.tensor.matmul(psB[s][:, C0 + P * t:C0 + P * t + P], qT[s][:, P * t:P * t + P],
                                            wst[s][:, KD, :], start=True, stop=True)
                last.then_inc(spr, 1)

            query(0, 0)
            query(0, 1)
            with pe.Fori(0, NS // 2 - 1) as i:
                score(i, 0)
                query(i + 1, 0)
                score(i, 1)
                query(i + 1, 1)
            score(NS // 2 - 1, 0)
            score(NS // 2 - 1, 1)

        @block.scalar
        def _(act):
            norm.act(act)
            act.sem_inc(qfree, 2)
            act.sem_inc(sfree, 2)
            act.wait_ge(norm.ready, 1)
            nc.scalar.activation(h_hi[:], hT[:], ACT.Copy).then_inc(split, 1)
            with act.Fori(0, NS // 2) as i:
                for s in range(2):
                    n = 2 * i + s
                    act.wait_ge(qpr, n + 1)
                    nc.scalar.activation(qT[s][:], psA[s][:, C0:C0 + T], ACT.Copy)
                    act.drain()
                    act.sem_inc(qcp, 1)
                    act.sem_inc(qfree, 1)
                    act.wait_ge(spr, n + 1)
                    act.wait_ge(top, n + 1)
                    nc.scalar.activation(sc[s][:].rearrange("p t x -> p (t x)"), psB[s][:, C0:C0 + T], ACT.Copy)
                    act.drain()
                    act.sem_inc(scp, 1)
                    act.sem_inc(sfree, 1)

        @block.vector
        def _(dve):
            norm.dve(dve)
            dve.sem_inc(top, 2)
            dve.wait_ge(split, 1)
            nc.vector.tensor_tensor(h_lo[:], hT[:], h_hi[:], ALU.subtract)
            with dve.Fori(0, NS // 2) as i:
                for s in range(2):
                    n = 2 * i + s
                    dve.wait_ge(scp, n + 1)
                    dve.sem_inc(seen, 1)
                    for t in range(NT):
                        nc.vector.max(v8[:, t, 0:8], sc[s][:, t, :])
                    dve.drain()
                    for t in range(NT):
                        nc.vector.max_index(i8[:, t, 0:8], v8[:, t, 0:8], sc[s][:, t, :])
                        nc.vector.match_replace(sc2[:, t, :], v8[:, t, 0:8], sc[s][:, t, :], -3e38)
                    dve.drain().then_inc(top, 1)
                    for t in range(NT):
                        nc.vector.max(v8[:, t, 8:16], sc2[:, t, :])
                    dve.drain()
                    for t in range(NT):
                        nc.vector.max_index(i8[:, t, 8:16], v8[:, t, 8:16], sc2[:, t, :])
                    dve.drain()
                    nc.vector.tensor_copy(vals[:, :, ds(n, 1), :].rearrange("p t a k -> p t (a k)"), v8[:])
                    nc.vector.tensor_copy(idxs[:, :, ds(n, 1), :].rearrange("p t a k -> p t (a k)"), i8[:])
                    dve.drain()


def peer_select(nc, cst, vals, idxs, picks, tag):
    W = PH * TK
    with nc.cleanup_on_exit(), ExitStack() as ctx:
        sb = lambda n, s, d=F32: ctx.enter_context(nc.sbuf_tensor(n + tag, s, d))
        sem = lambda n: nc.alloc_semaphore(n + tag)
        vt, it = sb("sl_vt", [P, 2 * PH, TK]), sb("sl_it", [P, 2 * PH, TK])
        cand, cand2 = sb("sl_cand", [P, PH, TK, TK]), sb("sl_cand2", [P, PH, TK * TK])
        best, pos = sb("sl_best", [P, PH, TK]), sb("sl_pos", [P, PH, TK], U32)
        half = sb("sl_half", [P, 2, W], U32)
        halff = sb("sl_halff", [P, 2, W])
        eq = [sb(f"sl_eq{s}", [P, W, TK]) for s in range(2)]
        row = sb("sl_row", [P, 3, W])
        den = sb("sl_den", [P, PH])
        ps = ctx.enter_context(nc.psum_tensor("sl_ps" + tag, [P, 3, W], F32))
        ex_in, ex_out, rows, trs, seen = (sem(n) for n in ("sl_ex_in", "sl_ex_out", "sl_rows", "sl_trs", "sl_seen"))
        block = ctx.enter_context(nc.Block())

        @block.scalar
        def _(act):
            with act.Fori(0, NT) as t:
                act.wait_ge(ex_in, t + 1)
                nc.scalar.activation(row[:, 2, :], row[:, 2, :], ACT.Exp).then_inc(ex_out, 1)

        @block.tensor
        def _(pe):
            with pe.Fori(0, NT) as t:
                pe.wait_ge(rows, t + 1)
                for j in range(3):
                    last = nc.tensor.transpose(ps[:, j, :], row[:, j, :], cst.ident[:])
                last.then_inc(trs, 1)

        @block.vector
        def _(dve):
            with dve.Fori(0, NT) as t:
                nc.vector.tensor_copy(vt[:], vals[:, ds(t, 1)].rearrange("p o a k -> p (o a) k"))
                nc.vector.tensor_copy(it[:], idxs[:, ds(t, 1)].rearrange("p o a k -> p (o a) k"))
                dve.drain()
                nc.vector.tensor_tensor(cand[:], vt[:, 0:PH, :].unsqueeze(3).to_broadcast([P, PH, TK, TK]),
                                        vt[:, PH:, :].unsqueeze(2).to_broadcast([P, PH, TK, TK]), ALU.add)
                dve.drain()
                c = cand[:].rearrange("p h a b -> p h (a b)")
                for h in range(PH):
                    nc.vector.max(best[:, h, 0:8], c[:, h, :])
                dve.drain()
                for h in range(PH):
                    nc.vector.max_index(pos[:, h, 0:8], best[:, h, 0:8], c[:, h, :])
                    nc.vector.match_replace(cand2[:, h, :], best[:, h, 0:8], c[:, h, :], -3e38)
                dve.drain()
                for h in range(PH):
                    nc.vector.max(best[:, h, 8:16], cand2[:, h, :])
                dve.drain()
                for h in range(PH):
                    nc.vector.max_index(pos[:, h, 8:16], best[:, h, 8:16], cand2[:, h, :])
                nc.vector.tensor_tensor(row[:, 2, :].rearrange("p (h k) -> p h k", k=TK), best[:],
                                        best[:, :, 0:1].to_broadcast([P, PH, TK]), ALU.subtract)
                dve.drain().then_inc(ex_in, 1)
                pf = pos[:].rearrange("p h k -> p (h k)")
                nc.vector.tensor_scalar(half[:, 0, :], pf, 4, None, ALU.logical_shift_right)
                nc.vector.tensor_scalar(half[:, 1, :], pf, 15, None, ALU.bitwise_and)
                dve.drain()
                nc.vector.tensor_copy(halff[:], half[:])
                dve.drain()
                for j in range(2):
                    nc.vector.tensor_tensor(eq[j][:], halff[:, j, :].unsqueeze(2).to_broadcast([P, W, TK]),
                                            cst.iota[:, 0:TK].unsqueeze(1).to_broadcast([P, W, TK]), ALU.is_equal)
                dve.drain()
                for j in range(2):
                    e4 = eq[j][:].rearrange("p (h k) a -> p h k a", k=TK)
                    nc.vector.tensor_tensor(e4, e4, it[:, PH * j:PH * j + PH, :].unsqueeze(2)
                                            .to_broadcast([P, PH, TK, TK]), ALU.mult)
                dve.drain()
                for j in range(2):
                    nc.vector.tensor_reduce(row[:, j, :], eq[j][:], AX, ALU.add)
                dve.wait_ge(ex_out, t + 1)
                nc.vector.tensor_reduce(den[:], row[:, 2, :].rearrange("p (h k) -> p h k", k=TK), AX, ALU.add)
                dve.drain()
                nc.vector.reciprocal(den[:], den[:])
                dve.drain()
                nc.vector.tensor_tensor(row[:, 2, :].rearrange("p (h k) -> p h k", k=TK),
                                        row[:, 2, :].rearrange("p (h k) -> p h k", k=TK),
                                        den[:].unsqueeze(2).to_broadcast([P, PH, TK]), ALU.mult)
                dve.drain().then_inc(rows, 1)
                dve.wait_ge(trs, t + 1)
                dve.sem_inc(seen, 1)
                nc.vector.tensor_copy(picks[:, :, ds(P * t, P)], ps[:])
                dve.drain()


def peer_gates(nc, cst, picks, gates, tag):
    TB = 32
    RING = 4
    with nc.cleanup_on_exit(), ExitStack() as ctx:
        sb = lambda n, s, d=F32: ctx.enter_context(nc.sbuf_tensor(n + tag, s, d))
        sem = lambda n: nc.alloc_semaphore(n + tag)
        pk = [sb(f"gt_pk{s}", [P, 3, TB]) for s in range(2)]
        oh1 = [sb(f"gt_oh1{r}", [P, 4, NK]) for r in range(RING)]
        oh2 = [sb(f"gt_oh2{r}", [P, 4, NK]) for r in range(RING)]
        gs = [sb(f"gt_gs{s}", [P, NK, TB]) for s in range(2)]
        ps = [ctx.enter_context(nc.psum_tensor(f"gt_ps{q}" + tag, [P, 8, NK], F32)) for q in range(4)]
        oh = sem("gt_oh")
        mm = sem("gt_mm")
        ev = sem("gt_ev")
        blk = sem("gt_blk")
        sv = [sem(f"gt_sv{s}") for s in range(2)]
        block = ctx.enter_context(nc.Block())
        NBL = T // TB

        @block.vector
        def _(dve):
            with dve.Fori(0, NBL // 2) as i:
                for s in range(2):
                    nc.vector.tensor_copy(pk[s][:], picks[:, :, ds(2 * TB * i + TB * s, TB)])
                    dve.drain()
                    for q in range(TB // 4):
                        r = q % RING
                        dve.wait_ge(mm, 8 * (2 * i + s) + q + 1)
                        for x in range(4):
                            t = 4 * q + x
                            nc.vector.tensor_scalar(oh1[r][:, x, :], cst.iota[:], pk[s][:, 0, t:t + 1], None, ALU.is_equal)
                            nc.vector.tensor_scalar(oh2[r][:, x, :], cst.iota[:], pk[s][:, 1, t:t + 1],
                                                    pk[s][:, 2, t:t + 1], ALU.is_equal, ALU.mult)
                        dve.drain().then_inc(oh, 1)

        @block.tensor
        def _(pe):
            pe.sem_inc(mm, RING)
            with pe.Fori(0, NBL // 2) as i:
                for s in range(2):
                    for q in range(TB // 4):
                        n = 8 * (2 * i + s) + q
                        pe.wait_ge(oh, n + 1)
                        if q % 2 == 0:
                            pe.wait_ge(ev, 4 * (2 * i + s) + q // 2 + 1)
                        for x in range(4):
                            last = nc.tensor.matmul(ps[q // 2][:, 4 * (q % 2) + x, :], oh1[q % RING][:, x, :],
                                                    oh2[q % RING][:, x, :], start=True, stop=True)
                        last.then_inc(mm, 1)

        @block.scalar
        def _(act):
            act.sem_inc(ev, 4)

            def rows(i, s, first):
                if not first:
                    act.wait_ge(sv[s], 16 * i)
                for q in range(4):
                    act.wait_ge(mm, 8 * (2 * i + s) + 2 * q + 2 + RING)
                    nc.scalar.activation(gs[s][:, :, 8 * q:8 * q + 8].rearrange("p j t -> p t j"), ps[q][:],
                                         ACT.Copy).then_inc(ev, 1)
                act.drain().then_inc(blk, 1)

            for s in range(2):
                rows(0, s, True)
            with act.Fori(1, NBL // 2) as i:
                for s in range(2):
                    rows(i, s, False)

        @block.sync
        def _(sp):
            with sp.Fori(0, NBL // 2) as i:
                for s in range(2):
                    sp.wait_ge(blk, 2 * i + s + 1)
                    sp.dma_start(gates[:, ds(2 * i + s, 1)].rearrange("p o j t -> p (o j t)"),
                                 gs[s][:].rearrange("p j t -> p (j t)")).then_inc(sv[s], 16)
            for s in range(2):
                sp.wait_ge(sv[s], 16 * (NBL // 2))


def peer_experts(nc, cst, modT, uT, v, gates, h_hi, h_lo, tag):
    J, TB = 4, 32
    NG = NK // J
    with nc.cleanup_on_exit(), ExitStack() as ctx:
        sb = lambda n, s, d=F32: ctx.enter_context(nc.sbuf_tensor(n + tag, s, d))
        sem = lambda n: nc.alloc_semaphore(n + tag)
        pst = lambda n: ctx.enter_context(nc.psum_tensor(n + tag, [P, 2, BANK], F32))
        facc = sb("ex_facc", [P, KD, T])
        ust = [sb(f"ex_ust{s}", [P, KD, P]) for s in range(2)]
        vst = [sb(f"ex_vst{s}", [P, KD, P]) for s in range(2)]
        gst = [sb(f"ex_gst{s}", [P, T // TB, J, TB]) for s in range(2)]
        u_hi = [sb(f"ex_uhi{s}", [P, KD, P], BF16) for s in range(2)]
        u_lo = [sb(f"ex_ulo{s}", [P, KD, P], BF16) for s in range(2)]
        v_hi = [sb(f"ex_vhi{s}", [P, J, KD, P], BF16) for s in range(2)]
        v_lo = [sb(f"ex_vlo{s}", [P, J, KD, P], BF16) for s in range(2)]
        ge = [sb(f"ex_ge{s}", [P, T]) for s in range(2)]
        gh = sb("ex_gh", [P, T])
        g_hi = [sb(f"ex_ghi{s}", [P, J, T], BF16) for s in range(2)]
        g_lo = [sb(f"ex_glo{s}", [P, J, T], BF16) for s in range(2)]
        psH = [pst(f"ex_psH{s}") for s in range(2)]
        psV = [pst(f"ex_psV{s}") for s in range(2)]
        u_in = [sem(f"ex_u_in{s}") for s in range(2)]
        v_in = [sem(f"ex_v_in{s}") for s in range(2)]
        g_in = [sem(f"ex_g_in{s}") for s in range(2)]
        uh, ul = sem("ex_uh"), sem("ex_ul")
        vh, vl = sem("ex_vh"), sem("ex_vl")
        hp, hg, hr = sem("ex_hp"), sem("ex_hg"), sem("ex_hr")
        vp, vr = sem("ex_vp"), sem("ex_vr")
        block = ctx.enter_context(nc.Block())
        seg = [slice(0, HALFT), slice(HALFT, T)]

        @block.sync
        def _(sp):
            def group(g, first, s):
                if first < 2:
                    pass
                else:
                    sp.wait_ge(hr, J * g - J)
                sp.dma_start(gst[s][:], gates[:, :, ds(J * g, J), :]).then_inc(g_in[s], 16)
                for q in range(J):
                    n = J * g + q
                    if first > 0 or q >= 2:
                        sp.wait_ge(ul, n - 1)
                    sp.dma_start(ust[q % 2][:], uT[n]).then_inc(u_in[q % 2], 16)
                    if first > 0 or q >= 2:
                        sp.wait_ge(vl, n - 1)
                    sp.dma_start(vst[q % 2][:].rearrange("p k x -> p (k x)"), v[n]).then_inc(v_in[q % 2], 16)

            group(0, 0, 0)
            group(1, 1, 1)
            with sp.Fori(1, NG // 2) as i:
                group(2 * i, 2, 0)
                group(2 * i + 1, 2, 1)

        @block.tensor
        def _(pe):
            def hidden(g, q, first):
                n, s = J * g + q, q % 2
                pe.wait_ge(ul, n + 1)
                if first and q < 2:
                    pass
                else:
                    pe.wait_ge(hg, n - 1)
                prods = [(a, b, k) for k in range(KD) for a, b in ((u_hi, h_hi), (u_hi, h_lo), (u_lo, h_hi))]
                for m, (a, b, k) in enumerate(prods):
                    for x in range(2):
                        last = nc.tensor.matmul(psH[s][:, x, 0:HALFT], a[s][:, k, :], b[:, k, seg[x]],
                                                start=(m == 0), stop=(m == len(prods) - 1))
                last.then_inc(hp, 1)

            def output(g, k, s, first):
                if k == 0:
                    pe.wait_ge(hr, J * g + J)
                    pe.wait_ge(vl, J * g + J)
                if not (first and k < 2):
                    pe.wait_ge(vr, KD * g + k - 1)
                prods = [(a, b, q) for q in range(J) for a, b in ((v_hi, g_hi), (v_hi, g_lo), (v_lo, g_hi))]
                for m, (a, b, q) in enumerate(prods):
                    for x in range(2):
                        last = nc.tensor.matmul(psV[k % 2][:, x, 0:HALFT], a[s][:, q, k, :], b[s][:, q, seg[x]],
                                                start=(m == 0), stop=(m == len(prods) - 1))
                last.then_inc(vp, 1)

            def group(g, s, second):
                for q in range(J):
                    hidden(g, q, False)
                    output(g - 1, 2 * q, 1 - s, second)
                    output(g - 1, 2 * q + 1, 1 - s, second)

            for q in range(J):
                hidden(0, q, True)
            group(1, 1, True)
            with pe.Fori(1, NG // 2) as i:
                group(2 * i, 0, False)
                group(2 * i + 1, 1, False)
            for k in range(KD):
                output(NG - 1, k, 1, False)

        @block.scalar
        def _(act):
            def take_u(g, q, first):
                n, s = J * g + q, q % 2
                rnd = (n - s) // 2 if isinstance(n, int) else 2 * g + q // 2
                act.wait_ge(u_in[s], 16 * rnd + 16)
                if not first:
                    act.wait_ge(hp, n - 1)
                nc.scalar.activation(u_hi[s][:], ust[s][:], ACT.Copy).then_inc(uh, 1)

            def take_v(g, q, s, first):
                act.wait_ge(v_in[q % 2], 16 * (2 * g + q // 2) + 16)
                if not first:
                    act.wait_ge(vp, KD * g - KD)
                nc.scalar.activation(v_hi[s][:, q], vst[q % 2][:], ACT.Copy).then_inc(vh, 1)

            def gelu(g, q, first):
                n, s = J * g + q, q % 2
                act.wait_ge(hp, n + 1)
                if not first:
                    act.wait_ge(hr, n - 1)
                nc.scalar.activation(ge[s][:].rearrange("p (a x) -> p a x", a=2), psH[s][:, :, 0:HALFT],
                                     ACT.Gelu).then_inc(hg, 1)

            def group(g, s, first, last):
                for q in range(J):
                    if q < J - 1:
                        take_u(g, q + 1, first == 0 and q < 1)
                    elif not last:
                        take_u(g + 1, 0, False)
                    gelu(g, q, first == 0 and q < 2)
                    take_v(g, q, s, first < 2)

            take_u(0, 0, True)
            group(0, 0, 0, False)
            group(1, 1, 1, False)
            with act.Fori(1, NG // 2 - 1) as i:
                group(2 * i, 0, 2, False)
                group(2 * i + 1, 1, 2, False)
            group(NG - 2, 0, 2, False)
            group(NG - 1, 1, 2, True)

        @block.vector
        def _(dve):
            def take_u(g, q):
                n, s = J * g + q, q % 2
                dve.wait_ge(uh, n + 1)
                nc.vector.tensor_tensor(u_lo[s][:], ust[s][:], u_hi[s][:], ALU.subtract).then_inc(ul, 1)

            def take_v(g, q, s):
                dve.wait_ge(vh, J * g + q + 1)
                nc.vector.tensor_tensor(v_lo[s][:, q], vst[q % 2][:], v_hi[s][:, q], ALU.subtract).then_inc(vl, 1)

            def gate(g, q, s, first):
                n = J * g + q
                if q == 0:
                    dve.wait_ge(g_in[s], 16 * ((g - s) // 2 if isinstance(g, int) else g // 2) + 16)
                dve.wait_ge(hg, n + 1)
                nc.vector.tensor_tensor(gh[:].rearrange("p (b t) -> p b t", t=TB),
                                        ge[q % 2][:].rearrange("p (b t) -> p b t", t=TB), gst[s][:, :, q, :], ALU.mult)
                dve.drain()
                if not first:
                    dve.wait_ge(vp, KD * g - KD)
                nc.vector.tensor_copy(g_hi[s][:, q], gh[:])
                dve.drain()
                nc.vector.tensor_tensor(g_lo[s][:, q], gh[:], g_hi[s][:, q], ALU.subtract)
                dve.drain().then_inc(hr, 1)

            def add_up(g, k):
                dve.wait_ge(vp, KD * g + k + 1)
                dst = facc[:, k, :].rearrange("p (a x) -> p a x", a=2)
                nc.vector.tensor_tensor(dst, psV[k % 2][:, :, 0:HALFT], dst, ALU.add).then_inc(vr, 1)

            def group(g, s, first, last):
                for q in range(J):
                    if q < J - 1:
                        take_u(g, q + 1)
                    elif not last:
                        take_u(g + 1, 0)
                    gate(g, q, s, first < 2)
                    take_v(g, q, s)
                    if first > 0:
                        add_up(g - 1, 2 * q)
                        add_up(g - 1, 2 * q + 1)

            nc.vector.memset(facc[:], 0.0)
            dve.drain()
            take_u(0, 0)
            group(0, 0, 0, False)
            group(1, 1, 1, False)
            with dve.Fori(1, NG // 2 - 1) as i:
                group(2 * i, 0, 2, False)
                group(2 * i + 1, 1, 2, False)
            group(NG - 2, 0, 2, False)
            group(NG - 1, 1, 2, True)
            for k in range(KD):
                add_up(NG - 1, k)
            dve.drain()
            for k in range(KD):
                for c, tok in ((0, slice(0, CTX)), (1, slice(CTX, T))):
                    nc.vector.scalar_tensor_tensor(cst.XT[:, k, tok], facc[:, k, tok], modT[:, 5 * KD + k, c:c + 1],
                                                   cst.XT[:, k, tok], op0=ALU.mult, op1=ALU.add)
            dve.drain()


def peer(nc, cst, modT, wqk, uT, v, gates, tag):
    with ExitStack() as ctx:
        h_hi = ctx.enter_context(nc.sbuf_tensor("h_hi" + tag, [P, KD, T], BF16))
        h_lo = ctx.enter_context(nc.sbuf_tensor("h_lo" + tag, [P, KD, T], BF16))
        with ExitStack() as c1:
            vals = c1.enter_context(nc.sbuf_tensor("vals" + tag, [P, NT, 2 * PH, TK], F32))
            idxs = c1.enter_context(nc.sbuf_tensor("idxs" + tag, [P, NT, 2 * PH, TK], F32))
            picks = c1.enter_context(nc.sbuf_tensor("picks" + tag, [P, 3, T], F32))
            peer_scores(nc, cst, modT, wqk, h_hi, h_lo, vals, idxs, tag)
            peer_select(nc, cst, vals, idxs, picks, tag)
            peer_gates(nc, cst, picks, gates, tag)
        peer_experts(nc, cst, modT, uT, v, gates, h_hi, h_lo, tag)


NQ, NKV = AH * HD // P, AKV * HD // P
KC0 = 2 * P
KCOLS = 2 * P + LAT


def attn_project(nc, cst, modT, a, zT, ktp, vp):
    NZ = NQ + NKV
    with nc.cleanup_on_exit(), ExitStack() as ctx:
        sb = lambda n, s, d=F32: ctx.enter_context(nc.sbuf_tensor(n, s, d))
        sem = lambda n: nc.alloc_semaphore(n)
        hT = sb("ap_hT", [P, KD, T])
        wst = [sb(f"ap_wst{s}", [P, KD, P]) for s in range(2)]
        wv = sb("ap_wv", [P, KD, AKV * HD])
        sqz = [sb(f"ap_sqz{s}", [P, T]) for s in range(2)]
        rs = [sb(f"ap_rs{s}", [P, T]) for s in range(2)]
        turn = sb("ap_turn", [P, LAT])
        cos, sin = sb("ap_cos", [P, LAT]), sb("ap_sin", [P, LAT])
        heads, rot = sb("ap_heads", [P, P]), sb("ap_rot", [P, P])
        gain = sb("ap_gain", [P, NZ])
        vctx = sb("ap_vctx", [P, AKV * HD])
        psA = [ctx.enter_context(nc.psum_tensor(f"ap_psA{s}", [P, 2 * BANK], F32)) for s in range(2)]
        psB = ctx.enter_context(nc.psum_tensor("ap_psB", [P, 2 * BANK], F32))
        psR = [ctx.enter_context(nc.psum_tensor(f"ap_psR{s}", [P, LAT], F32)) for s in range(2)]
        norm = Norm(nc, ctx, cst, "_ap", modT, 0, zT[:, 0:KD, :], hT, psA[0])
        w_in = [sem(f"ap_w_in{s}") for s in range(2)]
        c_in = sem("ap_c_in")
        v_in = sem("ap_v_in")
        cleared = sem("ap_cleared")
        cache_in = sem("ap_cache_in")
        pr = sem("ap_pr")
        zc = sem("ap_zc")
        sm = sem("ap_sm")
        iv = sem("ap_iv")
        rt = sem("ap_rt")
        nz = sem("ap_nz")
        tn = sem("ap_tn")
        ro = sem("ap_ro")
        vpr = sem("ap_vpr")
        outr, outs = sem("ap_outr"), sem("ap_outs")
        def values(t):
            return psA[t // 4][:, 256 * (t % 4):256 * (t % 4) + 256]

        block = ctx.enter_context(nc.Block())

        @block.sync
        def _(sp):
            for s in range(2):
                sp.dma_start(wst[s][:], a["wqk_att"][s]).then_inc(w_in[s], 16)
            for dst, name in ((heads, "heads"), (rot, "rot"), (gain, "qk_gain"), (cos, "cos"), (sin, "sin")):
                sp.dma_start(dst[:], a[name]).then_inc(c_in, 16)
            sp.dma_start(wv[:], a["wv_att"]).then_inc(v_in, 16)
            sp.wait_ge(cleared, 1)
            for p in range(NKV):
                for h in range(2):
                    c = slice(HD * h, HD * h + HD)
                    sp.dma_start(ktp[c, p, h, 0:P], a["cache_k"][c, p, :]).then_inc(cache_in, 16)
                    sp.dma_start(vp[:, p, h, 0, c], a["cache_v"][:, 2 * p + h, :]).then_inc(cache_in, 16)
            with sp.Fori(1, NZ // 2) as i:
                for s in range(2):
                    sp.wait_ge(pr, 2 * i + s - 1)
                    sp.dma_start(wst[s][:], a["wqk_att"][2 * i + s]).then_inc(w_in[s], 16)
            sp.wait_ge(outr, 1)
            sp.dma_start(a["new_k"], zT[:, NQ:NZ, 0:CTX]).then_inc(outs, 16)
            sp.wait_ge(outr, 2)
            sp.dma_start(a["new_v"], vctx[:]).then_inc(outs, 16)
            sp.wait_ge(outs, 32)
            sp.wait_ge(cache_in, 64 * NKV)

        @block.tensor
        def _(pe):
            norm.pe(pe)
            pe.wait_ge(norm.ready, 1)
            pe.wait_ge(c_in, 80)

            def project(n, s):
                rnd = n // 2 if isinstance(n, int) else None
                pe.wait_ge(w_in[s], 16 * rnd + 16)
                proj_rest(n, s)

            def proj_rest(n, s):
                pe.wait_ge(zc, n + 1)
                for k in range(KD):
                    for tok, col in segments():
                        last = nc.tensor.matmul(psA[s][:, col], wst[s][:, k, :], hT[:, k, tok],
                                                start=(k == 0), stop=(k == KD - 1))
                last.then_inc(pr, 1)

            def sums(n, s, first=False):
                pe.wait_ge(zc, n + 3)
                if not first:
                    pe.wait_ge(iv, n)
                for tok, col in segments():
                    last = nc.tensor.matmul(psB[:, col], heads[:], sqz[s][:, tok], start=True, stop=True)
                last.then_inc(sm, 1)

            def turned(n, s):
                pe.wait_ge(nz, n + 1)
                pe.wait_ge(ro, n + 1)
                nc.tensor.matmul(psR[s][:], rot[:], zT[:, ds(n, 1), CTX:T].rearrange("p o t -> p (o t)"),
                                 start=True, stop=True).then_inc(tn, 1)

            project(0, 0)
            project(1, 1)
            sums(0, 0, True)
            with pe.Fori(1, NZ // 2) as i:
                for s in range(2):
                    pe.wait_ge(w_in[s], 16 * i + 16)
                    proj_rest(2 * i + s, s)
                    sums(2 * i + s - 1, 1 - s)
                    turned(2 * i + s - 2, s)
            sums(NZ - 1, 1)
            turned(NZ - 2, 0)
            turned(NZ - 1, 1)
            pe.wait_ge(v_in, 16)
            for t in range(NT):
                for k in range(KD):
                    last = nc.tensor.matmul(values(t), hT[:, k, P * t:P * t + P], wv[:, k, :],
                                            start=(k == 0), stop=(k == KD - 1))
            last.then_inc(vpr, 1)

        @block.scalar
        def _(act):
            norm.act(act)
            act.sem_inc(zc, 2)

            def take(n, s):
                act.wait_ge(pr, n + 1)
                src = psA[s][:, C0:C0 + T]
                nc.scalar.activation(zT[:, ds(n, 1), :].rearrange("p o t -> p (o t)"), src, ACT.Copy)
                nc.scalar.activation(sqz[s][:], src, ACT.Square)
                act.drain().then_inc(zc, 1)

            def root(n, s):
                act.wait_ge(iv, n + 1)
                nc.scalar.activation(rs[s][:], rs[s][:], ACT.Sqrt).then_inc(rt, 1)

            take(0, 0)
            take(1, 1)
            root(0, 0)
            with act.Fori(1, NZ // 2) as i:
                for s in range(2):
                    n = 2 * i + s
                    act.wait_ge(sm, n - 1)
                    take(n, s)
                    root(n - 1, 1 - s)
            root(NZ - 1, 1)

        @block.vector
        def _(dve):
            nc.vector.memset(ktp[:], 0.0)
            nc.vector.memset(vp[:], 0.0)
            dve.drain().then_inc(cleared, 1)
            norm.dve(dve)
            dve.sem_inc(ro, 2)
            dve.wait_ge(c_in, 80)

            def inverse(n, s):
                dve.wait_ge(sm, n + 1)
                nc.vector.tensor_scalar(rs[s][:], psB[:, C0:C0 + T], 1.0 / HD, EPS, ALU.mult, ALU.add)
                dve.drain()
                nc.vector.reciprocal(rs[s][:], rs[s][:])
                dve.drain().then_inc(iv, 1)

            def normalise(n, s):
                z = zT[:, ds(n, 1), :].rearrange("p o t -> p (o t)")
                dve.wait_ge(rt, n + 1)
                nc.vector.scalar_tensor_tensor(z, z, gain[:, ds(n, 1)], rs[s][:], op0=ALU.mult, op1=ALU.mult)
                dve.drain().then_inc(nz, 1)

            def rotate(n, s):
                z = zT[:, ds(n, 1), CTX:T].rearrange("p o t -> p (o t)")
                dve.wait_ge(tn, n + 1)
                nc.vector.tensor_tensor(turn[:], psR[s][:], sin[:], ALU.mult)
                nc.vector.tensor_tensor(z, z, cos[:], ALU.mult)
                dve.drain()
                nc.vector.tensor_tensor(z, z, turn[:], ALU.add)
                dve.drain().then_inc(ro, 1)

            inverse(0, 0)
            normalise(0, 0)
            with dve.Fori(1, NZ // 2) as i:
                for s in range(2):
                    n = 2 * i + s
                    rotate(n - 2, s)
                    inverse(n - 1, 1 - s)
                    normalise(n - 1, 1 - s)
            inverse(NZ - 1, 1)
            normalise(NZ - 1, 1)
            rotate(NZ - 2, 0)
            rotate(NZ - 1, 1)
            dve.sem_inc(outr, 1)
            for p in range(NKV):
                for h in range(2):
                    c = slice(HD * h, HD * h + HD)
                    nc.vector.tensor_copy(ktp[c, p, h, P:KCOLS], zT[c, NQ + p, :])
            dve.wait_ge(vpr, 1)
            nc.vector.tensor_copy(vctx[:], values(0))
            for t in range(NT):
                for p in range(NKV):
                    for h in range(2):
                        o = 2 * HD * p + HD * h
                        nc.vector.tensor_copy(vp[:, p, h, t + 1, HD * h:HD * h + HD], values(t)[:, o:o + HD])
            dve.drain().then_inc(outr, 1)


def attention(nc, cst, a, zT, ktp, vp, yT):
    units = [(c, b, h) for c in range(2) for b in range(NT) for h in range(2)]
    NU = len(units)

    def keys(b):
        if b == 0:
            return [1]
        return [0] + [2 + j for j in range(max(0, b - 2), min(NT - 2, b) + 1)]

    KIND = {0: 1, 1: 0, 2: 1, 3: 1, 4: 2}
    with nc.cleanup_on_exit(), ExitStack() as ctx:
        sb = lambda n, s, d=F32: ctx.enter_context(nc.sbuf_tensor(n, s, d))
        sem = lambda n: nc.alloc_semaphore(n)
        mask = sb("at_mask", [P, 3, 4 * P])
        sink = sb("at_sink", [P, AH])
        qs = [sb(f"at_qs{s}", [P, T]) for s in range(2)]
        ss = [sb(f"at_s{i}", [P, 4 * P]) for i in range(4)]
        pt = [sb(f"at_pt{i}", [P, 4, P]) for i in range(2)]
        nm, den, es = sb("at_nm", [P, NU]), sb("at_den", [P, NU]), sb("at_es", [P, NU])
        mx = sb("at_mx", [P, NU])
        psS = [ctx.enter_context(nc.psum_tensor(f"at_psS{i}", [P, 4 * P], F32)) for i in range(4)]
        psT = [ctx.enter_context(nc.psum_tensor(f"at_psT{i}", [P, 4, P], F32)) for i in range(2)]
        psO = ctx.enter_context(nc.psum_tensor("at_psO", [P, 2 * BANK], F32))
        c_in = sem("at_c_in")
        qr = sem("at_qr")
        sf = sem("at_sf")
        mr = sem("at_mr")
        er = sem("at_er")
        wr = sem("at_wr")
        tf = sem("at_tf")
        tr = sem("at_tr")
        of = sem("at_of")
        orr = sem("at_or")
        block = ctx.enter_context(nc.Block())

        def runs(eng, one):
            for p in range(NKV):
                with eng.Fori(0, 2) as i:
                    one(p, i + 2 * p)

        @block.sync
        def _(sp):
            sp.dma_start(mask[:], a["win_mask"]).then_inc(c_in, 16)
            sp.dma_start(sink[:], a["sinks"]).then_inc(c_in, 16)

        @block.tensor
        def _(pe):
            pe.sem_inc(tf, 4)
            pe.sem_inc(of, 2)

            def one(p, r):
                def score(v):
                    c, b, h = units[v]
                    pe.wait_ge(mr, NU * r + v + 1)
                    q, out = qs[c][:, P * b:P * b + P], psS[v % 4]
                    ks = keys(b)
                    if b == 0:
                        last = nc.tensor.matmul(out[:, 0:P], q, ktp[:, p, h, P:2 * P], start=True, stop=True)
                    else:
                        nc.tensor.matmul(out[:, 0:P], q, ktp[:, p, h, 0:P], start=True, stop=True)
                        n = len(ks) - 1
                        last = nc.tensor.matmul(out[:, P:P + n * P], q, ktp[:, p, h, P * ks[1]:P * ks[1] + n * P],
                                                start=True, stop=True)
                    last.then_inc(sf, 1)

                def turn(v):
                    pe.wait_ge(wr, NU * r + v + 1)
                    pe.wait_ge(tr, NU * r + v + 1)
                    for j in range(len(keys(units[v][1]))):
                        last = nc.tensor.transpose(psT[v % 2][:, j, :], ss[v % 4][:, P * j:P * j + P], cst.ident[:])
                    last.then_inc(tf, 1)

                def output(v):
                    c, b, h = units[v]
                    pe.wait_ge(tr, NU * r + v + 3)
                    if b == 0 and h == 0:
                        pe.wait_ge(orr, 2 * r + c + 1)
                    ks = keys(b)
                    for j, kt in enumerate(ks):
                        last = nc.tensor.matmul(psO[:, C0 + P * b:C0 + P * b + P], vp[:, p, h, kt, :], pt[v % 2][:, j, :],
                                                start=(h == 0 and j == 0), stop=(h == 1 and j == len(ks) - 1))
                    last.then_inc(of, 1)

                pe.wait_ge(qr, r + 1)
                for v in range(NU + 3):
                    if v < NU:
                        score(v)
                    if 2 <= v < NU + 2:
                        turn(v - 2)
                    if v >= 3:
                        output(v - 3)

            runs(pe, one)

        @block.scalar
        def _(act):
            act.sem_inc(tr, 2)
            act.wait_ge(c_in, 32)

            def one(p, r):
                def exps(v):
                    c, b, h = units[v]
                    w = P * len(keys(b))
                    act.wait_ge(mr, NU * r + v + 5)
                    nc.scalar.activation(ss[v % 4][:, 0:w], ss[v % 4][:, 0:w], ACT.Exp, bias=nm[:, v:v + 1],
                                         accum_out=den[:, v:v + 1])
                    nc.scalar.activation(es[:, v:v + 1], sink[:, ds(4 * r + 2 * c + h, 1)], ACT.Exp, bias=nm[:, v:v + 1])
                    act.drain().then_inc(er, 1)

                def move(v):
                    n = len(keys(units[v][1]))
                    act.wait_ge(tf, NU * r + v + 5)
                    act.wait_ge(of, NU * r + v + 1)
                    nc.scalar.activation(pt[v % 2][:, 0:n, :], psT[v % 2][:, 0:n, :], ACT.Copy).then_inc(tr, 1)

                for c in range(2):
                    nc.scalar.activation(qs[c][:], zT[:, ds(2 * r + c, 1), :].rearrange("p o t -> p (o t)"), ACT.Copy)
                act.drain().then_inc(qr, 1)
                for v in range(NU + 2):
                    if v < NU:
                        exps(v)
                    if v >= 2:
                        move(v - 2)

            runs(act, one)

        @block.vector
        def _(dve):
            dve.sem_inc(mr, 4)
            dve.sem_inc(orr, 1)
            dve.wait_ge(c_in, 32)

            def one(p, r):
                def scores(v):
                    c, b, h = units[v]
                    w = P * len(keys(b))
                    m = mask[:, 1, 0:w] if b == 0 else mask[:, KIND[b], 0:w]
                    dve.wait_ge(sf, NU * r + v + 1)
                    dve.wait_ge(tf, NU * r + v + 1)
                    nc.vector.scalar_tensor_tensor(ss[v % 4][:, 0:w], psS[v % 4][:, 0:w], SCALE, m,
                                                   op0=ALU.mult, op1=ALU.add)
                    dve.drain()
                    nc.vector.tensor_reduce(mx[:, v:v + 1], ss[v % 4][:, 0:w], AX, ALU.max)
                    dve.drain()
                    nc.vector.tensor_scalar(nm[:, v:v + 1], mx[:, v:v + 1], sink[:, ds(4 * r + 2 * c + h, 1)], -1.0,
                                            ALU.max, ALU.mult)
                    dve.drain().then_inc(mr, 1)

                def weights(v):
                    w = P * len(keys(units[v][1]))
                    dve.wait_ge(er, NU * r + v + 1)
                    nc.vector.tensor_tensor(den[:, v:v + 1], den[:, v:v + 1], es[:, v:v + 1], ALU.add)
                    dve.drain()
                    nc.vector.reciprocal(den[:, v:v + 1], den[:, v:v + 1])
                    dve.drain()
                    nc.vector.tensor_scalar(ss[v % 4][:, 0:w], ss[v % 4][:, 0:w], den[:, v:v + 1], None, ALU.mult)
                    dve.drain().then_inc(wr, 1)

                def out(c):
                    dve.wait_ge(of, NU * r + 10 * c + 12)
                    nc.vector.tensor_scalar(yT[:, ds(2 * r + c, 1), :].rearrange("p o t -> p (o t)"),
                                            psO[:, C0:C0 + T], 1.0, None, ALU.mult)
                    dve.drain().then_inc(orr, 1)

                for v in range(NU + 1):
                    if v < NU:
                        scores(v)
                    if v >= 1:
                        weights(v - 1)
                    if v == 12:
                        out(0)
                out(1)

            runs(dve, one)


class Const:
    pass


def program(nc, a, stage):
    with ExitStack() as ctx:
        sb = lambda n, s, d=F32: ctx.enter_context(nc.sbuf_tensor(n, s, d))
        cst = Const()
        cst.XT = sb("XT", [P, KD, T])
        cst.cond = sb("cond", [P, KD, 2])
        cst.ones = sb("ones", [P, P])
        cst.ident = sb("ident", [P, P])
        cst.normw = None
        normw = [sb(f"normw{l}", [P, 2, KD, 2]) for l in range(2)]
        cst.iota = sb("iota", [P, P])
        mods = [sb(f"modT{l}", [P, NMOD * KD, 2]) for l in range(2)]
        with ExitStack() as c1:
            ld = c1.enter_context(nc.semaphore("first_in"))
            sil = c1.enter_context(nc.semaphore("first_silu"))
            block = c1.enter_context(nc.Block())

            @block.sync
            def _(sp):
                sp.dma_start(cst.cond[:], a["cond"]).then_inc(ld, 16)
                sp.dma_start(cst.XT[:], a["xT"]).then_inc(ld, 16)
                sp.dma_start(cst.ident[:], a["ident"]).then_inc(ld, 16)
                for l in range(2):
                    sp.dma_start(normw[l][:], a["normw"][l]).then_inc(ld, 16)
                sp.dma_start(cst.iota[:], a["iota"]).then_inc(ld, 16)
                sp.wait_ge(ld, 96)

            @block.scalar
            def _(act):
                act.wait_ge(ld, 96)
                nc.scalar.activation(cst.cond[:], cst.cond[:], ACT.Silu).then_inc(sil, 1)
                act.wait_ge(sil, 1)

            @block.vector
            def _(dve):
                nc.vector.memset(cst.ones[:], 1.0)
                dve.drain()

        for l in range(2 if stage > 2 else 1):
            modulation(nc, cst, a["ada_w"][l], a["ada_b"][l], mods[l], f"_{l}")
        cst.normw = normw[0]
        with ExitStack() as c1:
            yT = c1.enter_context(nc.sbuf_tensor("yT", [P, KD, T], F32))
            rec_mixer(nc, cst, mods[0], a["rec_w_in"], a["rec_gn"], a["masks"], a["state"], a["new_state"], yT)
            out_projection(nc, cst, a["rec_w_out"], yT, mods[0], "_rec")
        if stage >= 2:
            gates = nc.dram_tensor("gates", [P, T // 32, NK, 32], F32, kind="Internal").ap()
            peer(nc, cst, mods[0], a["wqk"][0], a["uT"][0], a["v"][0], gates, "_p0")
        if stage >= 3:
            cst.normw = normw[1]
            with ExitStack() as c1:
                zT = c1.enter_context(nc.sbuf_tensor("zT", [P, NQ + NKV, T], F32))
                ktp = c1.enter_context(nc.sbuf_tensor("ktp", [P, NKV, 2, KCOLS], F32))
                vp = c1.enter_context(nc.sbuf_tensor("vp", [P, NKV, 2, NT + 1, P], F32))
                attn_project(nc, cst, mods[1], a, zT, ktp, vp)
                yT = c1.enter_context(nc.sbuf_tensor("yTa", [P, KD, T], F32))
                attention(nc, cst, a, zT, ktp, vp, yT)
                out_projection(nc, cst, a["att_w_out"], yT, mods[1], "_att")
            peer(nc, cst, mods[1], a["wqk"][1], a["uT"][1], a["v"][1], gates, "_p1")
        with ExitStack() as c1:
            sv = c1.enter_context(nc.semaphore("last_out"))
            block = c1.enter_context(nc.Block())

            @block.sync
            def _(sp):
                sp.dma_start(a["yT"], cst.XT[:]).then_inc(sv, 16)
                sp.wait_ge(sv, 16)


STAGE = 3


def level_masks():
    m = np.zeros((P, 2 * LEVELS, P), np.int32)
    s, t = np.arange(P)[:, None], np.arange(P)[None, :]
    for l in range(LEVELS):
        same = (s >> (l + 1)) == (t >> (l + 1))
        hs, ht = (s >> l) & 1, (t >> l) & 1
        m[:, l, :] = same & (hs == 0) & (ht == 1)
        m[:, LEVELS + l, :] = same & (hs == 1) & (ht == 0)
    return m


def attention_constants():
    p, t = np.arange(P), np.arange(LAT)
    nf, grid = HD // 4, 64
    e, part = p % 32, (p % HD) // 32
    freqs = np.float32(10000.0) ** (-np.arange(nf, dtype=np.float32) / np.float32(nf))
    place = np.where(part[:, None] == 0, t[None, :] // grid, t[None, :] % grid).astype(np.float32)
    angle = place * freqs[e % nf][:, None]
    rot = np.zeros((P, P), np.float32)
    for m in range(P):
        if m % 32 < nf:
            rot[m + nf, m] = -1.0
        else:
            rot[m - nf, m] = 1.0
    q, k = np.arange(P)[:, None], np.arange(P)[None, :]
    left, right, none = np.where(k >= q, 0, NEG), np.where(k <= q, 0, NEG), np.zeros((P, P))
    mask = np.stack([np.concatenate(r, 1) for r in ((none, none, right, none), (none, left, none, right),
                                                    (none, left, none, none))], 1)
    return {"cos": np.cos(angle).astype(np.float32), "sin": np.sin(angle).astype(np.float32), "rot": rot,
            "heads": (p[:, None] // HD == p[None, :] // HD).astype(np.float32), "win_mask": mask.astype(np.float32)}


def kernel(**inputs):
    import concourse.bacc as bacc
    from concourse.bass_utils import run_bass_kernel_spmd

    x = {n: np.asarray(v) for n, v in inputs.items()}
    L = x["ada_w"].shape[0]
    f = np.ascontiguousarray
    tok = np.concatenate([x["x_prompt"][0], x["x_sample"][0]], 0)
    cond = np.stack([x["c_ctx"], x["c"][0]], -1)
    arr = {
        "xT": f(tok.reshape(T, KD, P).transpose(2, 1, 0)),
        "cond": f(cond.reshape(KD, P, 2).transpose(1, 0, 2)),
        "ident": np.eye(P, dtype=np.float32),
        "normw": f(np.repeat(x["norm_w"].reshape(L, 2, KD, P).transpose(0, 3, 1, 2)[..., None], 2, -1)),
        "ada_w": f(x["ada_w"].reshape(L, KD, P, 12, 4, P).transpose(0, 3, 2, 4, 1, 5)),
        "ada_b": f(np.repeat(x["ada_b"].reshape(L, NMOD * KD, P).transpose(0, 2, 1)[..., None], 2, -1)),
        "rec_w_in": f(x["rec_w_in"][0].reshape(KD, P, 5, RH, P)[:, :, [0, 1, 2, 4, 3]].transpose(3, 2, 1, 0, 4)),
        "rec_gn": f(x["rec_gn_w"].reshape(P, 1)),
        "masks": level_masks(),
        "state": f(x["state_rec"][0, 0]),
        "rec_w_out": f(x["rec_w_out"][0].reshape(KD, P, KD, P).transpose(2, 1, 0, 3)),
    }
    if STAGE >= 2:
        arr["iota"] = f(np.broadcast_to(np.arange(P, dtype=np.float32), (P, P)))
        wq = x["peer_w_q"].reshape(L, KD, P, PH, 2, P).transpose(0, 4, 3, 2, 1, 5)
        keys = x["peer_keys"].transpose(0, 2, 1, 4, 3)[:, :, :, :, None, :]
        arr["wqk"] = f(np.concatenate([wq, keys], 4).reshape(L, 2 * PH, P, KD + 1, P))
        arr["uT"] = f(x["peer_u"].reshape(L, NK, NK, KD, P).transpose(0, 2, 4, 3, 1))
        arr["v"] = f(x["peer_v"])
    outs = {"yT": (P, KD, T), "new_state": (2, RH, P, P)}
    if STAGE >= 3:
        w = x["attn_w_qkv"][0]
        wq = w[:, :AH * HD].reshape(KD, P, 2, 2, 4, HD).transpose(2, 4, 1, 0, 3, 5).reshape(NQ, P, KD, P)
        wk = w[:, AH * HD:(AH + AKV) * HD].reshape(KD, P, NKV, P).transpose(2, 1, 0, 3)
        arr["wqk_att"] = f(np.concatenate([wq, wk], 0))
        arr["wv_att"] = f(w[:, (AH + AKV) * HD:].reshape(KD, P, AKV * HD).transpose(1, 0, 2))
        arr["qk_gain"] = f(np.stack([np.tile(x["attn_qn_w"][0], 2)] * NQ + [np.tile(x["attn_kn_w"][0], 2)] * NKV, 1))
        arr["cache_k"] = f(x["cache_k"][0, 0].reshape(P, NKV, P).transpose(2, 1, 0))
        arr["cache_v"] = f(x["cache_v"][0, 0])
        arr["sinks"] = f(np.broadcast_to(x["attn_sink"][0].reshape(2, 2, 4).transpose(0, 2, 1).reshape(AH), (P, AH)))
        arr["att_w_out"] = f(x["attn_w_out"][0].reshape(2, 2, 4, HD, D).transpose(0, 2, 1, 3, 4)
                             .reshape(NQ, P, KD, P).transpose(2, 1, 0, 3))
        arr.update(attention_constants())
        outs["new_k"], outs["new_v"] = (P, NKV, CTX), (CTX, AKV * HD)
    nc = bacc.Bacc("TRN2", target_bir_lowering=False, num_devices=1)
    aps = {n: nc.dram_tensor("in_" + n, v.shape, mybir.dt.from_np(v.dtype), kind="ExternalInput").ap()
           for n, v in arr.items()}
    for n, s in outs.items():
        aps[n] = nc.dram_tensor("out_" + n, s, F32, kind="ExternalOutput").ap()
    if STAGE >= 2:
        aps["v"] = aps["v"].rearrange("l (i j) d -> l j i d", j=NK)
    program(nc, aps, STAGE)
    r = run_bass_kernel_spmd(nc, [{"in_" + n: v for n, v in arr.items()}], core_ids=[0]).results[0]
    y = r["out_yT"].transpose(2, 1, 0).reshape(T, D)
    state = r["out_new_state"].reshape(1, 1, 2, RH, P, P)
    new_k = r["out_new_k"].transpose(2, 1, 0).reshape(1, 1, CTX, AKV, HD)
    new_v = r["out_new_v"].reshape(1, 1, CTX, AKV, HD)
    return (y[None, :CTX], y[None, CTX:], state, new_k, new_v)
```

```python
from contextlib import ExitStack

import numpy as np

import concourse.bass as bass
from concourse import mybir

P = 128
D = 1024
KD = D // P
CTX, LAT = 128, 512
T = CTX + LAT
NT = T // P
NMOD = 6
RH = 8
AH, AKV, HD = 16, 4, 64
HALFT = T // 2
BANK = 512
C0 = BANK - CTX
EPS = 1e-6
NEG = -1e30
LEVELS = 7
PH, NK, TK = 8, 128, 16
SCALE = HD ** -0.5

F32 = mybir.dt.float32
BF16 = mybir.dt.bfloat16
U32 = mybir.dt.uint32
I32 = mybir.dt.int32
ALU = mybir.AluOpType
ACT = mybir.ActivationFunctionType
AX = mybir.AxisListType.X
ds = bass.ds


def segments():
    return ((slice(0, CTX), slice(C0, BANK)), (slice(CTX, T), slice(BANK, BANK + LAT)))


class Modulation:
    PIECES = NMOD * D // 512

    def __init__(self, nc, ctx, cst, ada_w, adab_in, modT, tag):
        sb = lambda n, s: ctx.enter_context(nc.sbuf_tensor(n + tag, s, F32))
        sem = lambda n: nc.alloc_semaphore(n + tag)
        self.nc, self.cst, self.ada_w, self.adab_in, self.modT = nc, cst, ada_w, adab_in, modT
        self.wst = [sb(f"ada_wst{s}", [P, KD, 512]) for s in range(2)]
        self.rows = [sb(f"ada_rows{s}", [2, 512]) for s in range(2)]
        self.adab = sb("ada_bias", [P, NMOD * KD, 2])
        self.ps_rows = ctx.enter_context(nc.psum_tensor("ada_psr" + tag, [2, 512], F32))
        self.ps_cols = ctx.enter_context(nc.psum_tensor("ada_psc" + tag, [P, 4, 2], F32))
        self.w_in = [sem(f"ada_w_in{s}") for s in range(2)]
        self.b_in = sem("ada_b_in")
        self.rowp = sem("ada_rowp")
        self.rowc = sem("ada_rowc")
        self.colp = sem("ada_colp")
        self.colr = sem("ada_colr")

    def start(self, sp):
        sp.dma_start(self.adab[:], self.adab_in).then_inc(self.b_in, 16)

    def sp(self, sp, n, s):
        sp.wait_ge(self.rowp, n + 1)
        sp.dma_start(self.wst[s][:], self.ada_w[n]).then_inc(self.w_in[s], 16)

    def pe(self, pe, rnd, n, s):
        nc = self.nc
        pe.wait_ge(self.w_in[s], 16 * rnd + 16)
        for k in range(KD):
            last = nc.tensor.matmul(self.ps_rows[:], self.cst.cond[:, k, :], self.wst[s][:, k, :],
                                    start=(k == 0), stop=(k == KD - 1))
        last.then_inc(self.rowp, 1)
        pe.wait_ge(self.rowc, n + 1)
        pe.wait_ge(self.colr, n + 1)
        for m in range(4):
            last = nc.tensor.matmul(self.ps_cols[:, m, :], self.rows[s][:, P * m:P * m + P],
                                    self.cst.ident[0:2, 0:2], start=True, stop=True)
        last.then_inc(self.colp, 1)

    def act(self, act, n, s):
        act.wait_ge(self.rowp, n + 3)
        self.nc.scalar.activation(self.rows[s][:], self.ps_rows[:], ACT.Copy).then_inc(self.rowc, 1)

    def dve(self, dve, n):
        dve.wait_ge(self.colp, n + 1)
        at = ds(4 * n, 4)
        self.nc.vector.tensor_tensor(self.modT[:, at, :], self.ps_cols[:], self.adab[:, at, :],
                                     ALU.add).then_inc(self.colr, 1)


def modulation(nc, cst, ada_w, adab_in, modT, tag):
    with nc.cleanup_on_exit(), ExitStack() as ctx:
        mod = Modulation(nc, ctx, cst, ada_w, adab_in, modT, tag)
        block = ctx.enter_context(nc.Block())

        @block.sync
        def _(sp):
            mod.start(sp)
            with sp.Fori(0, mod.PIECES // 2) as i:
                for s in range(2):
                    mod.sp(sp, 2 * i + s, s)

        @block.tensor
        def _(pe):
            pe.sem_inc(mod.rowp, 2)
            with pe.Fori(0, mod.PIECES // 2) as i:
                for s in range(2):
                    mod.pe(pe, i, 2 * i + s, s)

        @block.scalar
        def _(act):
            with act.Fori(0, mod.PIECES // 2) as i:
                for s in range(2):
                    mod.act(act, 2 * i + s, s)

        @block.vector
        def _(dve):
            dve.sem_inc(mod.colr, 1)
            dve.wait_ge(mod.b_in, 16)
            with dve.Fori(0, mod.PIECES // 2) as i:
                for s in range(2):
                    mod.dve(dve, 2 * i + s)


class Norm:

    def __init__(self, nc, ctx, cst, tag, modT, which, sq, hT, sum_ps):
        sem = lambda n: nc.alloc_semaphore(n + tag)
        self.nc, self.cst, self.modT, self.which = nc, cst, modT, which
        self.sq, self.hT, self.sum_ps = sq, hT, sum_ps
        self.rstd = ctx.enter_context(nc.sbuf_tensor("rstd" + tag, [P, T], F32))
        self.gain = ctx.enter_context(nc.sbuf_tensor("gain" + tag, [P, KD, 2], F32))
        self.squares = sem("norm_squares")
        self.sums = sem("norm_sums")
        self.inv = sem("norm_inv")
        self.root = sem("norm_root")
        self.scaled = sem("norm_scaled")
        self.ready = sem("norm_ready")

    def act(self, act):
        nc = self.nc
        for k in range(KD):
            nc.scalar.activation(self.sq[:, k], self.cst.XT[:, k], ACT.Square).then_inc(self.squares, 1)
        act.wait_ge(self.inv, 1)
        nc.scalar.activation(self.rstd[:], self.rstd[:], ACT.Sqrt).then_inc(self.root, 1)
        shift = self.modT[:, 3 * self.which * KD:3 * self.which * KD + KD, :]
        for k in range(KD):
            act.wait_ge(self.scaled, k + 1)
            for c, tok in ((0, slice(0, CTX)), (1, slice(CTX, T))):
                nc.scalar.activation(self.hT[:, k, tok], self.hT[:, k, tok], ACT.Identity, bias=shift[:, k, c:c + 1])
            act.drain().then_inc(self.ready, 1)

    def pe(self, pe):
        nc = self.nc
        for k in range(KD):
            pe.wait_ge(self.squares, k + 1)
            for tok, col in segments():
                last = nc.tensor.matmul(self.sum_ps[:, col], self.cst.ones[:], self.sq[:, k, tok],
                                        start=(k == 0), stop=(k == KD - 1))
        last.then_inc(self.sums, 1)

    def dve(self, dve):
        nc, n0 = self.nc, (3 * self.which + 1) * KD
        nc.vector.scalar_tensor_tensor(self.gain[:], self.modT[:, n0:n0 + KD, :], 1.0,
                                       self.cst.normw[:, self.which], op0=ALU.add, op1=ALU.mult)
        dve.wait_ge(self.sums, 1)
        nc.vector.tensor_scalar(self.rstd[:], self.sum_ps[:, C0:C0 + T], 1.0 / D, EPS, ALU.mult, ALU.add)
        dve.drain()
        nc.vector.reciprocal(self.rstd[:], self.rstd[:]).then_inc(self.inv, 1)
        dve.wait_ge(self.root, 1)
        for k in range(KD):
            for c, tok in ((0, slice(0, CTX)), (1, slice(CTX, T))):
                nc.vector.scalar_tensor_tensor(self.hT[:, k, tok], self.cst.XT[:, k, tok], self.gain[:, k, c:c + 1],
                                               self.rstd[:, tok], op0=ALU.mult, op1=ALU.mult)
            dve.drain().then_inc(self.scaled, 1)


def out_projection(nc, cst, w_out, yT, modT, tag):
    with nc.cleanup_on_exit(), ExitStack() as ctx:
        sem = lambda n: nc.alloc_semaphore(n + tag)
        wst = ctx.enter_context(nc.sbuf_tensor("wo_st" + tag, [P, 4, KD, P], F32))
        ps = [ctx.enter_context(nc.psum_tensor(f"wo_ps{s}" + tag, [P, 2 * BANK], F32)) for s in range(2)]
        w_in = [sem(f"wo_in{s}") for s in range(4)]
        w_free, prod, psum_free = sem("wo_free"), sem("wo_prod"), sem("wo_psum_free")
        block = ctx.enter_context(nc.Block())

        @block.sync
        def _(sp):
            for m in range(KD):
                if m >= 4:
                    sp.wait_ge(prod, m - 3)
                sp.dma_start(wst[:, m % 4], w_out[m]).then_inc(w_in[m % 4], 16)

        @block.tensor
        def _(pe):
            for m in range(KD):
                pe.wait_ge(w_in[m % 4], 16 * (m // 4 + 1))
                if m >= 2:
                    pe.wait_ge(psum_free, m - 1)
                for k in range(KD):
                    for tok, col in segments():
                        last = nc.tensor.matmul(ps[m % 2][:, col], wst[:, m % 4, k, :], yT[:, k, tok],
                                                start=(k == 0), stop=(k == KD - 1))
                last.then_inc(prod, 1)

        @block.vector
        def _(dve):
            for m in range(KD):
                dve.wait_ge(prod, m + 1)
                for c, (tok, col) in enumerate(segments()):
                    last = nc.vector.scalar_tensor_tensor(cst.XT[:, m, tok], ps[m % 2][:, col],
                                                          modT[:, 2 * KD + m, c:c + 1], cst.XT[:, m, tok],
                                                          op0=ALU.mult, op1=ALU.add)
                last.then_inc(psum_free, 1)


def rec_mixer(nc, cst, modT, w_in_d, gn_in, masks_in, st_in, st_out, yT):
    Q_, FF_, FB_, G_, V_ = range(5)
    with nc.cleanup_on_exit(), ExitStack() as ctx:
        sb = lambda n, s, d=F32: ctx.enter_context(nc.sbuf_tensor(n, s, d))
        sem = lambda n: nc.alloc_semaphore(n)
        hT = sb("rec_hT", [P, KD, T])
        ms = sb("rec_ms", [P, RH, T])
        wst = sb("rec_wst", [P, 5, KD, P])
        masks = sb("rec_masks", [P, 2 * LEVELS, P], I32)
        gn = sb("rec_gn", [P, 1])
        z = [{n: sb(f"rec_{n}{s}", [P, T]) for n in ("q", "g", "f0", "f1", "k0", "k1", "v")} for s in range(2)]
        ksum = sb("rec_ksum", [P, T])
        ql = [sb(f"rec_ql{i}", [P, T]) for i in range(3)]
        kl = [sb(f"rec_kl{i}", [P, T]) for i in range(3)]
        qf = [sb(f"rec_qf{d}", [P, T]) for d in range(2)]
        kf = [sb(f"rec_kf{d}", [P, T]) for d in range(2)]
        tot = [sb(f"rec_tot{d}", [P, 2 * T]) for d in range(2)]
        acc = sb("rec_acc", [P, T])
        kt = [sb(f"rec_kt{d}", [P, NT, P]) for d in range(2)]
        st = sb("rec_st", [P, 2, 4, P])
        sto = sb("rec_sto", [P, 2, P])
        oT = sb("rec_oT", [P, T])
        osq = sb("rec_osq", [P, T])
        psA = [ctx.enter_context(nc.psum_tensor(f"rec_psA{s}", [P, 2 * BANK], F32)) for s in range(2)]
        psB = [ctx.enter_context(nc.psum_tensor(f"rec_psB{s}", [P, 2 * BANK], F32)) for s in range(2)]
        norm = Norm(nc, ctx, cst, "_rec", modT, 0, yT, hT, psA[0])
        small_in = sem("rec_small_in")
        wsem = [sem(f"rec_w_in{n}") for n in range(5)]
        proj = sem("rec_proj")
        psa_read = sem("rec_psa_read")
        zsem = sem("rec_z")
        zfree = sem("rec_zfree")
        lvl = sem("rec_lvl")
        full = sem("rec_full")
        psb_read = sem("rec_psb_read")
        accr = sem("rec_accr")
        ktr = sem("rec_ktr")
        st_ld = sem("rec_st_ld")
        st_rdy = sem("rec_st_rdy")
        st_sv = sem("rec_st_sv")
        osr = sem("rec_osr")
        otr = sem("rec_otr")
        seen = sem("rec_seen")
        fin = sem("rec_fin")
        NB = 20
        TR0, UU, OO, NN = 15, 17, 18, 19
        block = ctx.enter_context(nc.Block())

        @block.sync
        def _(sp):
            sp.dma_start(masks[:], masks_in).then_inc(small_in, 16)
            sp.dma_start(gn[:], gn_in).then_inc(small_in, 16)

            def head(h, first):
                for n in range(5):
                    if not first:
                        sp.wait_ge(proj, 5 * h + n - 4)
                    sp.dma_start(wst[:, n], w_in_d[h, n]).then_inc(wsem[n], 16)
                if not first:
                    sp.wait_ge(full, NB * h)
                    sp.wait_ge(accr, h)
                for d in range(2):
                    sp.dma_start(st[:, d, 0, :], st_in[d, h]).then_inc(st_ld, 16)

            def store(h):
                sp.wait_ge(st_rdy, h + 1)
                for d in range(2):
                    sp.dma_start(st_out[d, h], sto[:, d, :]).then_inc(st_sv, 16)

            head(0, True)
            with sp.Fori(1, RH) as h:
                head(h, False)
                store(h - 1)
            store(RH - 1)
            sp.wait_ge(st_sv, 32 * RH)

        @block.tensor
        def _(pe):
            norm.pe(pe)

            def project(h, n, first=False):
                pe.wait_ge(wsem[n], 16 * h + 16)
                pe.wait_ge(psa_read, 5 * h + max(n, 1))
                ps = psA[n % 2]
                if n == V_:
                    for t in range(NT):
                        for k in range(KD):
                            last = nc.tensor.matmul(ps[:, C0 + P * t:C0 + P * t + P], hT[:, k, P * t:P * t + P],
                                                    wst[:, n, k, :], start=(k == 0), stop=(k == KD - 1))
                else:
                    for k in range(KD):
                        if first:
                            pe.wait_ge(norm.ready, k + 1)
                        for tok, col in segments():
                            last = nc.tensor.matmul(ps[:, col], wst[:, n, k, :], hT[:, k, tok],
                                                    start=(k == 0), stop=(k == KD - 1))
                last.then_inc(proj, 1)

            def tiles(n, h, lhs, rhs, which=range(NT)):
                ps = psB[n % 2]
                for t in which:
                    a = slice(P * t, P * t + P)
                    last = nc.tensor.matmul(ps[:, C0 + P * t:C0 + P * t + P], lhs[:, a], rhs[:, a],
                                            start=True, stop=True)
                last.then_inc(full, 1)

            def head(h, s, nxt):
                zz = z[s]
                todo = [0, 1, 2, 3, 4] if nxt is not None else []
                for n in range(15):
                    if n in (4, 9) and todo:
                        project(nxt, todo.pop(0))
                    pe.wait_ge(psb_read, NB * h + n + 1)
                    pe.wait_ge(lvl, 15 * h + n + 1)
                    if n == 0:
                        tiles(0, h, ksum, zz["q"])
                        continue
                    d, l = divmod(n - 1, LEVELS)
                    i = (n - 1) % 3
                    tiles(n, h, zz[f"k{d}"] if l == 0 else kl[i], ql[i])
                for d in range(2):
                    n = TR0 + d
                    if d == 1 and todo:
                        project(nxt, todo.pop(0))
                    pe.wait_ge(psb_read, NB * h + n + 1)
                    pe.wait_ge(accr, 3 * h + d + 1)
                    for t in range(NT):
                        last = nc.tensor.transpose(psB[n % 2][:, C0 + P * t:C0 + P * t + P],
                                                   kf[d][:, P * t:P * t + P], cst.ident[:])
                    last.then_inc(full, 1)
                if todo:
                    project(nxt, todo.pop(0))
                n = UU
                pe.wait_ge(psb_read, NB * h + n + 1)
                pe.wait_ge(ktr, 2 * h + 2)
                for d in range(2):
                    for j in range(4):
                        t = (0 if j == 3 else j + 1) if d == 0 else (0 if j == 3 else 4 - j)
                        last = nc.tensor.matmul(psB[n % 2][:, BANK * d + P * j:BANK * d + P * j + P],
                                                kt[d][:, t, :], zz["v"][:, P * t:P * t + P], start=True, stop=True)
                last.then_inc(full, 1)
                if todo:
                    project(nxt, todo.pop(0))
                n = OO
                pe.wait_ge(psb_read, NB * h + n + 1)
                pe.wait_ge(accr, 3 * h + 3)
                for t in range(NT):
                    a, o = slice(P * t, P * t + P), psB[n % 2][:, C0 + P * t:C0 + P * t + P]
                    last = nc.tensor.matmul(o, zz["v"][:, a], acc[:, a], start=True, stop=(t == 0))
                    if t > 0:
                        nc.tensor.matmul(o, st[:, 0, t - 1, :], qf[0][:, a], start=False, stop=False)
                        last = nc.tensor.matmul(o, st[:, 1, 4 - t, :], qf[1][:, a], start=False, stop=True)
                last.then_inc(full, 1)
                n = NN
                pe.wait_ge(psb_read, NB * h + n + 1)
                pe.wait_ge(osr, h + 1)
                for tok, col in segments():
                    last = nc.tensor.matmul(psB[n % 2][:, col], cst.ones[:], osq[:, tok], start=True, stop=True)
                last.then_inc(full, 1)

            for n in range(5):
                project(0, n, n == 0)
            with pe.Fori(0, RH // 2 - 1) as i:
                head(2 * i, 0, 2 * i + 1)
                head(2 * i + 1, 1, 2 * i + 2)
            head(RH - 2, 0, RH - 1)
            head(RH - 1, 1, None)

        @block.scalar
        def _(act):
            act.sem_inc(psa_read, 1)
            norm.act(act)

            def evacuate(h, s):
                zz = z[s]
                act.wait_ge(zfree, h + 1)
                for n in range(5):
                    act.wait_ge(proj, 5 * h + n + 1)
                    src = psA[n % 2][:, C0:C0 + T]
                    if n in (Q_, G_):
                        dst = zz["q" if n == Q_ else "g"]
                        nc.scalar.activation(dst[:], src, ACT.Silu)
                    elif n in (FF_, FB_):
                        nc.scalar.activation(zz[f"f{n - FF_}"][:], src, ACT.Sigmoid)
                        nc.scalar.activation(zz[f"k{n - FF_}"][:], src, ACT.Sigmoid, scale=-1.0)
                    else:
                        nc.scalar.activation(zz["v"][:], src, ACT.Copy)
                    act.drain().then_inc(psa_read, 1)
                act.sem_inc(zsem, 1)

            def squares(h):
                act.wait_ge(otr, h + 1)
                nc.scalar.activation(osq[:], oT[:], ACT.Square).then_inc(osr, 1)

            evacuate(0, 0)
            with act.Fori(0, RH // 2 - 1) as i:
                evacuate(2 * i + 1, 1)
                squares(2 * i)
                evacuate(2 * i + 2, 0)
                squares(2 * i + 1)
            evacuate(RH - 1, 1)
            squares(RH - 2)
            squares(RH - 1)
            act.wait_ge(fin, 1)
            nc.scalar.activation(ms[:], ms[:], ACT.Sqrt).then_inc(fin, 1)

        @block.vector
        def _(dve):
            norm.dve(dve)
            dve.sem_inc(zfree, 2)
            dve.sem_inc(psb_read, 2)
            dve.wait_ge(small_in, 32)

            def build(h, s, n):
                zz = z[s]
                d, l = divmod(n - 1, LEVELS)
                i, H = (n - 1) % 3, 1 << l
                nb = T // H
                at = 2 * T - 2 * nb
                q_src, k_src = (ql[(i - 1) % 3], kl[(i - 1) % 3]) if l > 0 else (zz["q"], None)
                if n >= 4:
                    dve.wait_ge(full, NB * h + n - 2)
                if l == 0:
                    nc.vector.tensor_tensor(ql[i][:], zz["q"][:], zz[f"f{d}"][:], ALU.mult)
                else:
                    grow(d, l, q_src, ql[i], zz[f"k{d}"] if l == 1 else k_src, kl[i], zz)
                dve.drain().then_inc(lvl, 1)

            def grow(d, l, q_src, q_dst, k_src, k_dst, zz):
                H = 1 << l
                h2, nb = H // 2, T // H
                prev = zz[f"f{d}"][:] if l == 1 else tot[d][:, 2 * T - 4 * nb:2 * T - 2 * nb]
                pair = prev.rearrange("p (b e) -> p b e", e=2)
                if l < LEVELS:
                    nc.vector.tensor_tensor(tot[d][:, 2 * T - 2 * nb:2 * T - nb], pair[:, :, 0], pair[:, :, 1], ALU.mult)
                else:
                    nc.vector.tensor_tensor(tot[d][:, 2 * T - 2 * nb:2 * T - nb], pair[:, :, 0], pair[:, :, 1], ALU.mult)
                for src, dst, e in ((q_src, q_dst, 1 - d), (k_src, k_dst, d)):
                    sv = src[:].rearrange("p (b e x) -> p b e x", e=2, x=h2)
                    dv = dst[:].rearrange("p (b e x) -> p b e x", e=2, x=h2)
                    other = pair[:, :, 1 - e].unsqueeze(2).to_broadcast([P, nb, h2])
                    nc.vector.tensor_tensor(dv[:, :, e, :], sv[:, :, e, :], other, ALU.mult)
                    nc.vector.tensor_copy(dv[:, :, 1 - e, :], sv[:, :, 1 - e, :])

            def take(h, n):
                dve.wait_ge(full, NB * h + n + 1)
                dve.sem_inc(seen, 1)
                src = psB[n % 2][:, C0:C0 + T].rearrange("p (t x) -> p t x", x=P)
                dst = acc[:].rearrange("p (t x) -> p t x", x=P)
                if n == 0:
                    nc.vector.tensor_copy(dst, src).then_inc(psb_read, 1)
                else:
                    nc.vector.copy_predicated(dst, masks[:, n - 1, :].unsqueeze(1).to_broadcast([P, NT, P]),
                                              src).then_inc(psb_read, 1)
                dve.drain()

            def head(h, s, last):
                zz = z[s]
                dve.wait_ge(zsem, h + 1)
                nc.vector.tensor_tensor(ksum[:], zz["k0"][:], zz["k1"][:], ALU.add)
                dve.drain().then_inc(lvl, 1)
                for n in range(1, 15):
                    build(h, s, n)
                    take(h, n - 1)
                    if n % LEVELS == 0:
                        d = n // LEVELS - 1
                        i = (n - 1) % 3
                        grow(d, LEVELS, ql[i], qf[d], kl[i], kf[d], zz)
                        dve.drain().then_inc(accr, 1)
                take(h, 14)
                for d in range(2):
                    n = TR0 + d
                    dve.wait_ge(full, NB * h + n + 1)
                    nc.vector.tensor_copy(kt[d][:].rearrange("p t x -> p (t x)"),
                                          psB[n % 2][:, C0:C0 + T]).then_inc(psb_read, 1)
                    dve.drain().then_inc(ktr, 1)
                dve.wait_ge(full, NB * h + UU + 1)
                dve.wait_ge(st_ld, 32 * h + 32)
                if not (isinstance(h, int) and h == 0):
                    dve.wait_ge(st_sv, 32 * h)
                for d in range(2):
                    nc.vector.tensor_copy(sto[:, d, :], psB[UU % 2][:, BANK * d + 3 * P:BANK * d + 4 * P])
                for j in range(3):
                    for d in range(2):
                        t = j + 1 if d == 0 else 4 - j
                        decay = tot[d][:, 2 * T - 2 * NT + t:2 * T - 2 * NT + t + 1]
                        nc.vector.scalar_tensor_tensor(st[:, d, j + 1, :], st[:, d, j, :], decay,
                                                       psB[UU % 2][:, BANK * d + P * j:BANK * d + P * j + P],
                                                       op0=ALU.mult, op1=ALU.add)
                    dve.drain()
                dve.sem_inc(psb_read, 1)
                dve.sem_inc(st_rdy, 1)
                dve.sem_inc(accr, 1)
                dve.wait_ge(full, NB * h + OO + 1)
                nc.vector.tensor_copy(oT[:], psB[OO % 2][:, C0:C0 + T])
                nc.vector.tensor_tensor(yT[:, ds(h, 1), :].rearrange("p a t -> p (a t)"),
                                        psB[OO % 2][:, C0:C0 + T], zz["g"][:], ALU.mult)
                dve.drain()
                dve.sem_inc(otr, 1)
                dve.sem_inc(psb_read, 1)
                dve.sem_inc(zfree, 1)
                dve.wait_ge(full, NB * h + NN + 1)
                nc.vector.tensor_scalar(ms[:, ds(h, 1), :].rearrange("p a t -> p (a t)"),
                                        psB[NN % 2][:, C0:C0 + T], 1.0 / P, EPS, ALU.mult, ALU.add)
                dve.drain().then_inc(psb_read, 1)

            head(0, 0, False)
            head(1, 1, False)
            with dve.Fori(1, RH // 2) as i:
                head(2 * i, 0, False)
                head(2 * i + 1, 1, False)
            nc.vector.reciprocal(ms[:], ms[:]).then_inc(fin, 1)
            dve.wait_ge(fin, 2)
            nc.vector.scalar_tensor_tensor(yT[:], yT[:], gn[:, 0:1], ms[:], op0=ALU.mult, op1=ALU.mult)


def peer_scores(nc, cst, modT, wqk, h_hi, h_lo, vals, idxs, tag):
    NS = 2 * PH
    with nc.cleanup_on_exit(), ExitStack() as ctx:
        sb = lambda n, s, d=F32: ctx.enter_context(nc.sbuf_tensor(n + tag, s, d))
        sem = lambda n: nc.alloc_semaphore(n + tag)
        hT, sq = sb("ps_hT", [P, KD, T]), sb("ps_sq", [P, KD, T])
        wst = [sb(f"ps_wst{s}", [P, KD + 1, P]) for s in range(4)]
        qT = [sb(f"ps_qT{s}", [P, T]) for s in range(2)]
        sc = [sb(f"ps_sc{s}", [P, NT, P]) for s in range(2)]
        sc2 = sb("ps_sc2", [P, NT, P])
        v8, i8 = sb("ps_v8", [P, NT, TK]), sb("ps_i8", [P, NT, TK], U32)
        psA = [ctx.enter_context(nc.psum_tensor(f"ps_psA{s}" + tag, [P, 2 * BANK], F32)) for s in range(2)]
        psB = [ctx.enter_context(nc.psum_tensor(f"ps_psB{s}" + tag, [P, 2 * BANK], F32)) for s in range(2)]
        norm = Norm(nc, ctx, cst, "_ps" + tag, modT, 1, sq, hT, psA[0])
        w_in = [sem(f"ps_w_in{s}") for s in range(4)]
        qpr, qcp = sem("ps_qpr"), sem("ps_qcp")
        spr, scp = sem("ps_spr"), sem("ps_scp")
        top = sem("ps_top")
        qfree, sfree = sem("ps_qfree"), sem("ps_sfree")
        seen = sem("ps_seen")
        split = sem("ps_split")
        block = ctx.enter_context(nc.Block())

        @block.sync
        def _(sp):
            for s in range(4):
                sp.dma_start(wst[s][:], wqk[s]).then_inc(w_in[s], 16)
            with sp.Fori(1, NS // 4) as i:
                for s in range(4):
                    sp.wait_ge(spr, 4 * i + s - 3)
                    sp.dma_start(wst[s][:], wqk[4 * i + s]).then_inc(w_in[s], 16)

        @block.tensor
        def _(pe):
            norm.pe(pe)

            def query(i, s, first=False):
                n = 4 * i + s
                pe.wait_ge(w_in[s], 16 * i + 16)
                pe.wait_ge(qfree, n + 1)
                for k in range(KD):
                    if first:
                        pe.wait_ge(norm.ready, k + 1)
                    for tok, col in segments():
                        last = nc.tensor.matmul(psA[s % 2][:, col], wst[s][:, k, :], hT[:, k, tok],
                                                start=(k == 0), stop=(k == KD - 1))
                last.then_inc(qpr, 1)

            def score(i, s):
                n = 4 * i + s
                pe.wait_ge(qcp, n + 1)
                pe.wait_ge(sfree, n + 1)
                for t in range(NT):
                    last = nc.tensor.matmul(psB[s % 2][:, C0 + P * t:C0 + P * t + P], qT[s % 2][:, P * t:P * t + P],
                                            wst[s][:, KD, :], start=True, stop=True)
                last.then_inc(spr, 1)

            query(0, 0, True)
            with pe.Fori(0, NS // 4 - 1) as i:
                for s in range(4):
                    query(i + (s + 1) // 4, (s + 1) % 4)
                    score(i, s)
            for s in range(4):
                if s < 3:
                    query(NS // 4 - 1, s + 1)
                score(NS // 4 - 1, s)

        @block.scalar
        def _(act):
            act.sem_inc(qfree, 2)
            act.sem_inc(sfree, 2)
            norm.act(act)
            nc.scalar.activation(h_hi[:], hT[:], ACT.Copy).then_inc(split, 1)
            with act.Fori(0, NS // 2) as i:
                for s in range(2):
                    n = 2 * i + s
                    act.wait_ge(qpr, n + 1)
                    nc.scalar.activation(qT[s][:], psA[s][:, C0:C0 + T], ACT.Copy)
                    act.drain()
                    act.sem_inc(qcp, 1)
                    act.sem_inc(qfree, 1)
                    act.wait_ge(spr, n + 1)
                    act.wait_ge(top, n + 1)
                    nc.scalar.activation(sc[s][:].rearrange("p t x -> p (t x)"), psB[s][:, C0:C0 + T], ACT.Copy)
                    act.drain()
                    act.sem_inc(scp, 1)
                    act.sem_inc(sfree, 1)

        @block.vector
        def _(dve):
            norm.dve(dve)
            dve.sem_inc(top, 2)
            dve.wait_ge(split, 1)
            nc.vector.tensor_tensor(h_lo[:], hT[:], h_hi[:], ALU.subtract)
            with dve.Fori(0, NS // 2) as i:
                for s in range(2):
                    n = 2 * i + s
                    dve.wait_ge(scp, n + 1)
                    dve.sem_inc(seen, 1)
                    for t in range(NT):
                        nc.vector.max(v8[:, t, 0:8], sc[s][:, t, :])
                    dve.drain()
                    for t in range(NT):
                        nc.vector.max_index(i8[:, t, 0:8], v8[:, t, 0:8], sc[s][:, t, :])
                        nc.vector.match_replace(sc2[:, t, :], v8[:, t, 0:8], sc[s][:, t, :], -3e38)
                    dve.drain().then_inc(top, 1)
                    for t in range(NT):
                        nc.vector.max(v8[:, t, 8:16], sc2[:, t, :])
                    dve.drain()
                    for t in range(NT):
                        nc.vector.max_index(i8[:, t, 8:16], v8[:, t, 8:16], sc2[:, t, :])
                    dve.drain()
                    nc.vector.tensor_copy(vals[:, :, ds(n, 1), :].rearrange("p t a k -> p t (a k)"), v8[:])
                    nc.vector.tensor_copy(idxs[:, :, ds(n, 1), :].rearrange("p t a k -> p t (a k)"), i8[:])
                    dve.drain()


def peer_select(nc, cst, vals, idxs, picks, tag, ada=None):
    W = PH * TK
    with nc.cleanup_on_exit(), ExitStack() as ctx:
        sb = lambda n, s, d=F32: ctx.enter_context(nc.sbuf_tensor(n + tag, s, d))
        sem = lambda n: nc.alloc_semaphore(n + tag)
        vt, it = sb("sl_vt", [P, 2 * PH, TK]), sb("sl_it", [P, 2 * PH, TK])
        cand, cand2 = sb("sl_cand", [P, PH, TK, TK]), sb("sl_cand2", [P, PH, TK * TK])
        best, pos = sb("sl_best", [P, PH, TK]), sb("sl_pos", [P, PH, TK], U32)
        half = sb("sl_half", [P, 2, W], U32)
        halff = sb("sl_halff", [P, 2, W])
        eq = [sb(f"sl_eq{s}", [P, W, TK]) for s in range(2)]
        row = sb("sl_row", [P, 3, W])
        den = sb("sl_den", [P, PH])
        ps = ctx.enter_context(nc.psum_tensor("sl_ps" + tag, [P, 3, W], F32))
        ex_in, ex_out = sem("sl_ex_in"), sem("sl_ex_out")
        rows = sem("sl_rows")
        trs = sem("sl_trs")
        seen = sem("sl_seen")
        mod = Modulation(nc, ctx, cst, *ada, tag) if ada else None
        block = ctx.enter_context(nc.Block())

        if mod:
            @block.sync
            def _(sp):
                mod.start(sp)
                with sp.Fori(0, mod.PIECES // 2) as i:
                    for s in range(2):
                        mod.sp(sp, 2 * i + s, s)

        @block.scalar
        def _(act):
            if mod:
                for s in range(2):
                    mod.act(act, s, s)
            with act.Fori(0, NT) as t:
                if mod:
                    for s in range(2):
                        mod.act(act, 2 * t + 2 + s, s)
                act.wait_ge(ex_in, t + 1)
                nc.scalar.activation(row[:, 2, :], row[:, 2, :], ACT.Exp).then_inc(ex_out, 1)

        @block.tensor
        def _(pe):
            if mod:
                pe.sem_inc(mod.rowp, 2)
                for s in range(2):
                    mod.pe(pe, 0, s, s)
            with pe.Fori(0, NT) as t:
                if mod:
                    for s in range(2):
                        mod.pe(pe, t + 1, 2 * t + 2 + s, s)
                pe.wait_ge(rows, t + 1)
                for j in range(3):
                    last = nc.tensor.transpose(ps[:, j, :], row[:, j, :], cst.ident[:])
                last.then_inc(trs, 1)

        @block.vector
        def _(dve):
            if mod:
                dve.sem_inc(mod.colr, 1)
                dve.wait_ge(mod.b_in, 16)
                mod.dve(dve, 0)
                mod.dve(dve, 1)
            with dve.Fori(0, NT) as t:
                nc.vector.tensor_copy(vt[:], vals[:, ds(t, 1)].rearrange("p o a k -> p (o a) k"))
                nc.vector.tensor_copy(it[:], idxs[:, ds(t, 1)].rearrange("p o a k -> p (o a) k"))
                dve.drain()
                nc.vector.tensor_tensor(cand[:], vt[:, 0:PH, :].unsqueeze(3).to_broadcast([P, PH, TK, TK]),
                                        vt[:, PH:, :].unsqueeze(2).to_broadcast([P, PH, TK, TK]), ALU.add)
                dve.drain()
                c = cand[:].rearrange("p h a b -> p h (a b)")
                for h in range(PH):
                    nc.vector.max(best[:, h, 0:8], c[:, h, :])
                dve.drain()
                for h in range(PH):
                    nc.vector.max_index(pos[:, h, 0:8], best[:, h, 0:8], c[:, h, :])
                    nc.vector.match_replace(cand2[:, h, :], best[:, h, 0:8], c[:, h, :], -3e38)
                dve.drain()
                for h in range(PH):
                    nc.vector.max(best[:, h, 8:16], cand2[:, h, :])
                dve.drain()
                for h in range(PH):
                    nc.vector.max_index(pos[:, h, 8:16], best[:, h, 8:16], cand2[:, h, :])
                nc.vector.tensor_tensor(row[:, 2, :].rearrange("p (h k) -> p h k", k=TK), best[:],
                                        best[:, :, 0:1].to_broadcast([P, PH, TK]), ALU.subtract)
                dve.drain().then_inc(ex_in, 1)
                pf = pos[:].rearrange("p h k -> p (h k)")
                nc.vector.tensor_scalar(half[:, 0, :], pf, 4, None, ALU.logical_shift_right)
                nc.vector.tensor_scalar(half[:, 1, :], pf, 15, None, ALU.bitwise_and)
                dve.drain()
                nc.vector.tensor_copy(halff[:], half[:])
                dve.drain()
                for j in range(2):
                    nc.vector.tensor_tensor(eq[j][:], halff[:, j, :].unsqueeze(2).to_broadcast([P, W, TK]),
                                            cst.iota[:, 0:TK].unsqueeze(1).to_broadcast([P, W, TK]), ALU.is_equal)
                dve.drain()
                for j in range(2):
                    e4 = eq[j][:].rearrange("p (h k) a -> p h k a", k=TK)
                    nc.vector.tensor_tensor(e4, e4, it[:, PH * j:PH * j + PH, :].unsqueeze(2)
                                            .to_broadcast([P, PH, TK, TK]), ALU.mult)
                dve.drain()
                for j in range(2):
                    nc.vector.tensor_reduce(row[:, j, :], eq[j][:], AX, ALU.add)
                dve.wait_ge(ex_out, t + 1)
                nc.vector.tensor_reduce(den[:], row[:, 2, :].rearrange("p (h k) -> p h k", k=TK), AX, ALU.add)
                dve.drain()
                nc.vector.reciprocal(den[:], den[:])
                dve.drain()
                nc.vector.tensor_tensor(row[:, 2, :].rearrange("p (h k) -> p h k", k=TK),
                                        row[:, 2, :].rearrange("p (h k) -> p h k", k=TK),
                                        den[:].unsqueeze(2).to_broadcast([P, PH, TK]), ALU.mult)
                dve.drain().then_inc(rows, 1)
                if mod:
                    mod.dve(dve, 2 * t + 2)
                    mod.dve(dve, 2 * t + 3)
                dve.wait_ge(trs, t + 1)
                dve.sem_inc(seen, 1)
                nc.vector.tensor_copy(picks[:, :, ds(P * t, P)], ps[:])
                dve.drain()


def peer_gates(nc, cst, picks, gates, tag):
    TB, TU, TI = 32, 16, 8
    NBL, NU = T // TB, T // TU
    with nc.cleanup_on_exit(), ExitStack() as ctx:
        sb = lambda n, s, d=BF16: ctx.enter_context(nc.sbuf_tensor(n + tag, s, d))
        sem = lambda n: nc.alloc_semaphore(n + tag)
        keyrow = sb("gt_keyrow", [P, NK, TI])
        pk = sb("gt_pk", [P, 4, T])
        oh1 = [sb(f"gt_oh1{r}", [P, TU // TI, NK, TI]) for r in range(2)]
        oh2 = sb("gt_oh2", [P, TU // TI, NK, TI])
        ohh = [sb(f"gt_ohh{r}", [P, TU // TI, NK, TI]) for r in range(2)]
        ohl = [sb(f"gt_ohl{r}", [P, TU // TI, NK, TI]) for r in range(2)]
        gs = [sb(f"gt_gs{s}", [P, NK, TB], F32) for s in range(2)]
        ps = [ctx.enter_context(nc.psum_tensor(f"gt_ps{q}" + tag, [P, TI, NK], F32)) for q in range(4)]
        oh = sem("gt_oh")
        mm = sem("gt_mm")
        ev = sem("gt_ev")
        blk = sem("gt_blk")
        sv = [sem(f"gt_sv{s}") for s in range(2)]
        block = ctx.enter_context(nc.Block())

        @block.vector
        def _(dve):
            nc.vector.tensor_copy(keyrow[:], cst.iota[:].unsqueeze(2).to_broadcast([P, NK, TI]))
            nc.vector.tensor_copy(pk[:, 0:3], picks[:])
            dve.drain()
            nc.vector.tensor_tensor(pk[:, 3], picks[:, 2], pk[:, 2], ALU.subtract)
            dve.drain()
            keys = keyrow[:].unsqueeze(1).to_broadcast([P, TU // TI, NK, TI])
            with dve.Fori(0, NU // 2) as i:
                for r in range(2):
                    n = 2 * i + r
                    part = [pk[:, j, ds(2 * TU * i + TU * r, TU)].rearrange("p (g x) -> p g x", x=TI).unsqueeze(2)
                            .to_broadcast([P, TU // TI, NK, TI]) for j in range(4)]
                    nc.vector.tensor_tensor(oh2[:], part[1], keys, ALU.is_equal)
                    dve.wait_ge(mm, n + 1)
                    nc.vector.tensor_tensor(oh1[r][:], part[0], keys, ALU.is_equal)
                    dve.drain()
                    nc.vector.tensor_tensor(ohh[r][:], oh2[:], part[2], ALU.mult)
                    nc.vector.tensor_tensor(ohl[r][:], oh2[:], part[3], ALU.mult)
                    dve.drain().then_inc(oh, 1)

        @block.tensor
        def _(pe):
            pe.sem_inc(mm, 2)
            with pe.Fori(0, NU // 2) as i:
                for r in range(2):
                    n = 2 * i + r
                    pe.wait_ge(oh, n + 1)
                    for g in range(TU // TI):
                        pe.wait_ge(ev, 2 * n + g + 1)
                        for x in range(TI):
                            o = ps[2 * r + g][:, x, :]
                            nc.tensor.matmul(o, oh1[r][:, g, :, x], ohh[r][:, g, :, x], start=True, stop=False)
                            last = nc.tensor.matmul(o, oh1[r][:, g, :, x], ohl[r][:, g, :, x], start=False, stop=True)
                    last.then_inc(mm, 1)

        @block.scalar
        def _(act):
            act.sem_inc(ev, 4)

            def rows(i, s, first):
                if not first:
                    act.wait_ge(sv[s], 16 * i)
                for q in range(4):
                    if q % 2 == 0:
                        act.wait_ge(mm, 2 * (2 * i + s) + q // 2 + 3)
                    nc.scalar.activation(gs[s][:, :, 8 * q:8 * q + 8].rearrange("p j t -> p t j"), ps[q][:],
                                         ACT.Copy).then_inc(ev, 1)
                act.drain().then_inc(blk, 1)

            for s in range(2):
                rows(0, s, True)
            with act.Fori(1, NBL // 2) as i:
                for s in range(2):
                    rows(i, s, False)

        @block.sync
        def _(sp):
            with sp.Fori(0, NBL // 2) as i:
                for s in range(2):
                    sp.wait_ge(blk, 2 * i + s + 1)
                    sp.dma_start(gates[:, ds(2 * i + s, 1)].rearrange("p o j t -> p (o j t)"),
                                 gs[s][:].rearrange("p j t -> p (j t)")).then_inc(sv[s], 16)
            for s in range(2):
                sp.wait_ge(sv[s], 16 * (NBL // 2))


def peer_experts(nc, cst, modT, uT, v, gates, h_hi, h_lo, tag):
    J, TB = 4, 32
    NG = NK // J
    with nc.cleanup_on_exit(), ExitStack() as ctx:
        sb = lambda n, s, d=F32: ctx.enter_context(nc.sbuf_tensor(n + tag, s, d))
        sem = lambda n: nc.alloc_semaphore(n + tag)
        pst = lambda n: ctx.enter_context(nc.psum_tensor(n + tag, [P, 2, BANK], F32))
        facc = sb("ex_facc", [P, KD, T])
        ust = [sb(f"ex_ust{s}", [P, KD, P]) for s in range(2)]
        vst = [sb(f"ex_vst{s}", [P, KD, P]) for s in range(2)]
        gst = [sb(f"ex_gst{s}", [P, T // TB, J, TB]) for s in range(2)]
        u_hi = [sb(f"ex_uhi{s}", [P, KD, P], BF16) for s in range(2)]
        u_lo = [sb(f"ex_ulo{s}", [P, KD, P], BF16) for s in range(2)]
        v_hi = [sb(f"ex_vhi{s}", [P, J, KD, P], BF16) for s in range(2)]
        v_lo = [sb(f"ex_vlo{s}", [P, J, KD, P], BF16) for s in range(2)]
        ge = [sb(f"ex_ge{s}", [P, T]) for s in range(2)]
        gh = sb("ex_gh", [P, T])
        g_hi = [sb(f"ex_ghi{s}", [P, J, T], BF16) for s in range(2)]
        g_lo = [sb(f"ex_glo{s}", [P, J, T], BF16) for s in range(2)]
        psH = [pst(f"ex_psH{s}") for s in range(2)]
        psV = [pst(f"ex_psV{s}") for s in range(2)]
        u_in = [sem(f"ex_u_in{s}") for s in range(2)]
        v_in = [sem(f"ex_v_in{s}") for s in range(2)]
        g_in = [sem(f"ex_g_in{s}") for s in range(2)]
        uh, ul = sem("ex_uh"), sem("ex_ul")
        vh, vl = sem("ex_vh"), sem("ex_vl")
        hp, hg, hr = sem("ex_hp"), sem("ex_hg"), sem("ex_hr")
        vp, vr = sem("ex_vp"), sem("ex_vr")
        block = ctx.enter_context(nc.Block())
        seg = [slice(0, HALFT), slice(HALFT, T)]

        @block.sync
        def _(sp):
            def group(g, first, s):
                if first < 2:
                    pass
                else:
                    sp.wait_ge(hr, J * g - J)
                sp.dma_start(gst[s][:], gates[:, :, ds(J * g, J), :]).then_inc(g_in[s], 16)
                for q in range(J):
                    n = J * g + q
                    if first > 0 or q >= 2:
                        sp.wait_ge(ul, n - 1)
                    sp.dma_start(ust[q % 2][:], uT[n]).then_inc(u_in[q % 2], 16)
                    if first > 0 or q >= 2:
                        sp.wait_ge(vl, n - 1)
                    sp.dma_start(vst[q % 2][:].rearrange("p k x -> p (k x)"), v[n]).then_inc(v_in[q % 2], 16)

            group(0, 0, 0)
            group(1, 1, 1)
            with sp.Fori(1, NG // 2) as i:
                group(2 * i, 2, 0)
                group(2 * i + 1, 2, 1)

        @block.tensor
        def _(pe):
            def hidden(g, q, first):
                n, s = J * g + q, q % 2
                pe.wait_ge(ul, n + 1)
                if first and q < 2:
                    pass
                else:
                    pe.wait_ge(hg, n - 1)
                prods = [(a, b, k) for k in range(KD) for a, b in ((u_hi, h_hi), (u_hi, h_lo), (u_lo, h_hi))]
                for m, (a, b, k) in enumerate(prods):
                    for x in range(2):
                        last = nc.tensor.matmul(psH[s][:, x, 0:HALFT], a[s][:, k, :], b[:, k, seg[x]],
                                                start=(m == 0), stop=(m == len(prods) - 1))
                last.then_inc(hp, 1)

            def output(g, k, s, first):
                if k == 0:
                    pe.wait_ge(hr, J * g + J)
                    pe.wait_ge(vl, J * g + J)
                if not (first and k < 2):
                    pe.wait_ge(vr, KD * g + k - 1)
                prods = [(a, b, q) for q in range(J) for a, b in ((v_hi, g_hi), (v_hi, g_lo), (v_lo, g_hi))]
                for m, (a, b, q) in enumerate(prods):
                    for x in range(2):
                        last = nc.tensor.matmul(psV[k % 2][:, x, 0:HALFT], a[s][:, q, k, :], b[s][:, q, seg[x]],
                                                start=(m == 0), stop=(m == len(prods) - 1))
                last.then_inc(vp, 1)

            def group(g, s, second):
                for q in range(J):
                    hidden(g, q, False)
                    output(g - 1, 2 * q, 1 - s, second)
                    output(g - 1, 2 * q + 1, 1 - s, second)

            for q in range(J):
                hidden(0, q, True)
            group(1, 1, True)
            with pe.Fori(1, NG // 2) as i:
                group(2 * i, 0, False)
                group(2 * i + 1, 1, False)
            for k in range(KD):
                output(NG - 1, k, 1, False)

        @block.scalar
        def _(act):
            def take_u(g, q, first):
                n, s = J * g + q, q % 2
                rnd = (n - s) // 2 if isinstance(n, int) else 2 * g + q // 2
                act.wait_ge(u_in[s], 16 * rnd + 16)
                if not first:
                    act.wait_ge(hp, n - 1)
                nc.scalar.activation(u_hi[s][:], ust[s][:], ACT.Copy).then_inc(uh, 1)

            def take_v(g, q, s, first):
                act.wait_ge(v_in[q % 2], 16 * (2 * g + q // 2) + 16)
                if not first:
                    act.wait_ge(vp, KD * g - KD)
                nc.scalar.activation(v_hi[s][:, q], vst[q % 2][:], ACT.Copy).then_inc(vh, 1)

            def gelu(g, q, first):
                n, s = J * g + q, q % 2
                act.wait_ge(hp, n + 1)
                if not first:
                    act.wait_ge(hr, n - 1)
                nc.scalar.activation(ge[s][:].rearrange("p (a x) -> p a x", a=2), psH[s][:, :, 0:HALFT],
                                     ACT.Gelu).then_inc(hg, 1)

            def group(g, s, first, last):
                for q in range(J):
                    if q < J - 1:
                        take_u(g, q + 1, first == 0 and q < 1)
                    elif not last:
                        take_u(g + 1, 0, False)
                    gelu(g, q, first == 0 and q < 2)
                    take_v(g, q, s, first < 2)

            take_u(0, 0, True)
            group(0, 0, 0, False)
            group(1, 1, 1, False)
            with act.Fori(1, NG // 2 - 1) as i:
                group(2 * i, 0, 2, False)
                group(2 * i + 1, 1, 2, False)
            group(NG - 2, 0, 2, False)
            group(NG - 1, 1, 2, True)

        @block.vector
        def _(dve):
            def take_u(g, q):
                n, s = J * g + q, q % 2
                dve.wait_ge(uh, n + 1)
                nc.vector.tensor_tensor(u_lo[s][:], ust[s][:], u_hi[s][:], ALU.subtract).then_inc(ul, 1)

            def take_v(g, q, s):
                dve.wait_ge(vh, J * g + q + 1)
                nc.vector.tensor_tensor(v_lo[s][:, q], vst[q % 2][:], v_hi[s][:, q], ALU.subtract).then_inc(vl, 1)

            def gate(g, q, s, first):
                n = J * g + q
                if q == 0:
                    dve.wait_ge(g_in[s], 16 * ((g - s) // 2 if isinstance(g, int) else g // 2) + 16)
                dve.wait_ge(hg, n + 1)
                nc.vector.tensor_tensor(gh[:].rearrange("p (b t) -> p b t", t=TB),
                                        ge[q % 2][:].rearrange("p (b t) -> p b t", t=TB), gst[s][:, :, q, :], ALU.mult)
                dve.drain()
                if not first:
                    dve.wait_ge(vp, KD * g - KD)
                nc.vector.tensor_copy(g_hi[s][:, q], gh[:])
                dve.drain()
                nc.vector.tensor_tensor(g_lo[s][:, q], gh[:], g_hi[s][:, q], ALU.subtract)
                dve.drain().then_inc(hr, 1)

            def add_up(g, k):
                dve.wait_ge(vp, KD * g + k + 1)
                dst = facc[:, k, :].rearrange("p (a x) -> p a x", a=2)
                nc.vector.tensor_tensor(dst, psV[k % 2][:, :, 0:HALFT], dst, ALU.add).then_inc(vr, 1)

            def group(g, s, first, last):
                for q in range(J):
                    if q < J - 1:
                        take_u(g, q + 1)
                    elif not last:
                        take_u(g + 1, 0)
                    gate(g, q, s, first < 2)
                    take_v(g, q, s)
                    if first > 0:
                        add_up(g - 1, 2 * q)
                        add_up(g - 1, 2 * q + 1)

            nc.vector.memset(facc[:], 0.0)
            dve.drain()
            take_u(0, 0)
            group(0, 0, 0, False)
            group(1, 1, 1, False)
            with dve.Fori(1, NG // 2 - 1) as i:
                group(2 * i, 0, 2, False)
                group(2 * i + 1, 1, 2, False)
            group(NG - 2, 0, 2, False)
            group(NG - 1, 1, 2, True)
            for k in range(KD):
                add_up(NG - 1, k)
            dve.drain()
            for k in range(KD):
                for c, tok in ((0, slice(0, CTX)), (1, slice(CTX, T))):
                    nc.vector.scalar_tensor_tensor(cst.XT[:, k, tok], facc[:, k, tok], modT[:, 5 * KD + k, c:c + 1],
                                                   cst.XT[:, k, tok], op0=ALU.mult, op1=ALU.add)
            dve.drain()


def peer(nc, cst, modT, wqk, uT, v, gates, tag, ada=None):
    with ExitStack() as ctx:
        h_hi = ctx.enter_context(nc.sbuf_tensor("h_hi" + tag, [P, KD, T], BF16))
        h_lo = ctx.enter_context(nc.sbuf_tensor("h_lo" + tag, [P, KD, T], BF16))
        with ExitStack() as c1:
            vals = c1.enter_context(nc.sbuf_tensor("vals" + tag, [P, NT, 2 * PH, TK], F32))
            idxs = c1.enter_context(nc.sbuf_tensor("idxs" + tag, [P, NT, 2 * PH, TK], F32))
            picks = c1.enter_context(nc.sbuf_tensor("picks" + tag, [P, 3, T], F32))
            peer_scores(nc, cst, modT, wqk, h_hi, h_lo, vals, idxs, tag)
            peer_select(nc, cst, vals, idxs, picks, tag, ada)
            peer_gates(nc, cst, picks, gates, tag)
        peer_experts(nc, cst, modT, uT, v, gates, h_hi, h_lo, tag)


NQ, NKV = AH * HD // P, AKV * HD // P
KC0 = 2 * P
KCOLS = 2 * P + LAT


def attn_project(nc, cst, modT, a, zT, ktp, vp):
    NZ = NQ + NKV
    with nc.cleanup_on_exit(), ExitStack() as ctx:
        sb = lambda n, s, d=F32: ctx.enter_context(nc.sbuf_tensor(n, s, d))
        sem = lambda n: nc.alloc_semaphore(n)
        hT = sb("ap_hT", [P, KD, T])
        wst = [sb(f"ap_wst{s}", [P, KD, P]) for s in range(2)]
        wv = sb("ap_wv", [P, KD, AKV * HD])
        sqz = [sb(f"ap_sqz{s}", [P, T]) for s in range(2)]
        rs = [sb(f"ap_rs{s}", [P, T]) for s in range(2)]
        turn = sb("ap_turn", [P, LAT])
        cos, sin = sb("ap_cos", [P, LAT]), sb("ap_sin", [P, LAT])
        heads, rot = sb("ap_heads", [P, P]), sb("ap_rot", [P, P])
        gain = sb("ap_gain", [P, NZ])
        vctx = sb("ap_vctx", [P, AKV * HD])
        psA = [ctx.enter_context(nc.psum_tensor(f"ap_psA{s}", [P, 2 * BANK], F32)) for s in range(2)]
        psB = ctx.enter_context(nc.psum_tensor("ap_psB", [P, 2 * BANK], F32))
        psR = [ctx.enter_context(nc.psum_tensor(f"ap_psR{s}", [P, LAT], F32)) for s in range(2)]
        norm = Norm(nc, ctx, cst, "_ap", modT, 0, zT[:, 0:KD, :], hT, psA[0])
        w_in = [sem(f"ap_w_in{s}") for s in range(2)]
        c_in = sem("ap_c_in")
        v_in = sem("ap_v_in")
        cleared = sem("ap_cleared")
        cache_in = sem("ap_cache_in")
        pr = sem("ap_pr")
        zc = sem("ap_zc")
        sm = sem("ap_sm")
        iv = sem("ap_iv")
        rt = sem("ap_rt")
        nz = sem("ap_nz")
        tn = sem("ap_tn")
        ro = sem("ap_ro")
        vpr = sem("ap_vpr")
        outr, outs = sem("ap_outr"), sem("ap_outs")
        def values(t):
            return psA[t // 4][:, 256 * (t % 4):256 * (t % 4) + 256]

        block = ctx.enter_context(nc.Block())

        @block.sync
        def _(sp):
            for s in range(2):
                sp.dma_start(wst[s][:], a["wqk_att"][s]).then_inc(w_in[s], 16)
            for dst, name in ((heads, "heads"), (rot, "rot"), (gain, "qk_gain"), (cos, "cos"), (sin, "sin")):
                sp.dma_start(dst[:], a[name]).then_inc(c_in, 16)
            sp.dma_start(wv[:], a["wv_att"]).then_inc(v_in, 16)
            sp.wait_ge(cleared, 1)
            for p in range(NKV):
                for h in range(2):
                    c = slice(HD * h, HD * h + HD)
                    sp.dma_start(ktp[c, p, h, 0:P], a["cache_k"][c, p, :]).then_inc(cache_in, 16)
                    sp.dma_start(vp[:, p, h, 0, c], a["cache_v"][:, 2 * p + h, :]).then_inc(cache_in, 16)
            with sp.Fori(1, NZ // 2) as i:
                for s in range(2):
                    sp.wait_ge(pr, 2 * i + s - 1)
                    sp.dma_start(wst[s][:], a["wqk_att"][2 * i + s]).then_inc(w_in[s], 16)
            sp.wait_ge(outr, 1)
            sp.dma_start(a["new_k"], zT[:, NQ:NZ, 0:CTX]).then_inc(outs, 16)
            sp.wait_ge(outr, 2)
            sp.dma_start(a["new_v"], vctx[:]).then_inc(outs, 16)
            sp.wait_ge(outs, 32)
            sp.wait_ge(cache_in, 64 * NKV)

        @block.tensor
        def _(pe):
            norm.pe(pe)
            pe.wait_ge(c_in, 80)

            def project(i, s, first=False):
                n = 2 * i + s
                pe.wait_ge(w_in[s], 16 * i + 16)
                pe.wait_ge(zc, n + 1)
                for k in range(KD):
                    if first:
                        pe.wait_ge(norm.ready, k + 1)
                    for tok, col in segments():
                        last = nc.tensor.matmul(psA[s][:, col], wst[s][:, k, :], hT[:, k, tok],
                                                start=(k == 0), stop=(k == KD - 1))
                last.then_inc(pr, 1)

            def sums(n, s, first=False):
                pe.wait_ge(zc, n + 3)
                if not first:
                    pe.wait_ge(iv, n)
                for tok, col in segments():
                    last = nc.tensor.matmul(psB[:, col], heads[:], sqz[s][:, tok], start=True, stop=True)
                last.then_inc(sm, 1)

            def turned(n, s):
                pe.wait_ge(nz, n + 1)
                pe.wait_ge(ro, n + 1)
                nc.tensor.matmul(psR[s][:], rot[:], zT[:, ds(n, 1), CTX:T].rearrange("p o t -> p (o t)"),
                                 start=True, stop=True).then_inc(tn, 1)

            project(0, 0, True)
            project(0, 1)
            sums(0, 0, True)
            with pe.Fori(1, NZ // 2) as i:
                for s in range(2):
                    project(i, s)
                    sums(2 * i + s - 1, 1 - s)
                    turned(2 * i + s - 2, s)
            sums(NZ - 1, 1)
            turned(NZ - 2, 0)
            turned(NZ - 1, 1)
            pe.wait_ge(v_in, 16)
            for t in range(NT):
                for k in range(KD):
                    last = nc.tensor.matmul(values(t), hT[:, k, P * t:P * t + P], wv[:, k, :],
                                            start=(k == 0), stop=(k == KD - 1))
            last.then_inc(vpr, 1)

        @block.scalar
        def _(act):
            act.sem_inc(zc, 2)
            norm.act(act)

            def take(n, s):
                act.wait_ge(pr, n + 1)
                src = psA[s][:, C0:C0 + T]
                nc.scalar.activation(zT[:, ds(n, 1), :].rearrange("p o t -> p (o t)"), src, ACT.Copy)
                nc.scalar.activation(sqz[s][:], src, ACT.Square)
                act.drain().then_inc(zc, 1)

            def root(n, s):
                act.wait_ge(iv, n + 1)
                nc.scalar.activation(rs[s][:], rs[s][:], ACT.Sqrt).then_inc(rt, 1)

            take(0, 0)
            take(1, 1)
            root(0, 0)
            with act.Fori(1, NZ // 2) as i:
                for s in range(2):
                    n = 2 * i + s
                    act.wait_ge(sm, n - 1)
                    take(n, s)
                    root(n - 1, 1 - s)
            root(NZ - 1, 1)

        @block.vector
        def _(dve):
            nc.vector.memset(ktp[:], 0.0)
            nc.vector.memset(vp[:], 0.0)
            dve.drain().then_inc(cleared, 1)
            norm.dve(dve)
            dve.sem_inc(ro, 2)
            dve.wait_ge(c_in, 80)

            def inverse(n, s):
                dve.wait_ge(sm, n + 1)
                nc.vector.tensor_scalar(rs[s][:], psB[:, C0:C0 + T], 1.0 / HD, EPS, ALU.mult, ALU.add)
                dve.drain()
                nc.vector.reciprocal(rs[s][:], rs[s][:])
                dve.drain().then_inc(iv, 1)

            def normalise(n, s):
                z = zT[:, ds(n, 1), :].rearrange("p o t -> p (o t)")
                dve.wait_ge(rt, n + 1)
                nc.vector.scalar_tensor_tensor(z, z, gain[:, ds(n, 1)], rs[s][:], op0=ALU.mult, op1=ALU.mult)
                dve.drain().then_inc(nz, 1)

            def rotate(n, s):
                z = zT[:, ds(n, 1), CTX:T].rearrange("p o t -> p (o t)")
                dve.wait_ge(tn, n + 1)
                nc.vector.tensor_tensor(turn[:], psR[s][:], sin[:], ALU.mult)
                nc.vector.tensor_tensor(z, z, cos[:], ALU.mult)
                dve.drain()
                nc.vector.tensor_tensor(z, z, turn[:], ALU.add)
                dve.drain().then_inc(ro, 1)

            inverse(0, 0)
            normalise(0, 0)
            with dve.Fori(1, NZ // 2) as i:
                for s in range(2):
                    n = 2 * i + s
                    rotate(n - 2, s)
                    inverse(n - 1, 1 - s)
                    normalise(n - 1, 1 - s)
            inverse(NZ - 1, 1)
            normalise(NZ - 1, 1)
            rotate(NZ - 2, 0)
            rotate(NZ - 1, 1)
            dve.sem_inc(outr, 1)
            for p in range(NKV):
                for h in range(2):
                    c = slice(HD * h, HD * h + HD)
                    nc.vector.tensor_copy(ktp[c, p, h, P:KCOLS], zT[c, NQ + p, :])
            dve.wait_ge(vpr, 1)
            nc.vector.tensor_copy(vctx[:], values(0))
            for t in range(NT):
                for p in range(NKV):
                    for h in range(2):
                        o = 2 * HD * p + HD * h
                        nc.vector.tensor_copy(vp[:, p, h, t + 1, HD * h:HD * h + HD], values(t)[:, o:o + HD])
            dve.drain().then_inc(outr, 1)


def attention(nc, cst, a, zT, ktp, vp, yT):
    units = [(c, b, h) for c in range(2) for b in range(NT) for h in range(2)]
    NU = len(units)

    def keys(b):
        if b == 0:
            return [1]
        return [0] + [2 + j for j in range(max(0, b - 2), min(NT - 2, b) + 1)]

    KIND = {0: 1, 1: 0, 2: 1, 3: 1, 4: 2}
    with nc.cleanup_on_exit(), ExitStack() as ctx:
        sb = lambda n, s, d=F32: ctx.enter_context(nc.sbuf_tensor(n, s, d))
        sem = lambda n: nc.alloc_semaphore(n)
        mask = sb("at_mask", [P, 3, 4 * P])
        sink = sb("at_sink", [P, AH])
        qs = [sb(f"at_qs{s}", [P, T]) for s in range(2)]
        ss = [sb(f"at_s{i}", [P, 4 * P]) for i in range(4)]
        pt = [sb(f"at_pt{i}", [P, 4, P]) for i in range(2)]
        nm, den, es = sb("at_nm", [P, NU]), sb("at_den", [P, NU]), sb("at_es", [P, NU])
        mx = sb("at_mx", [P, NU])
        psS = [ctx.enter_context(nc.psum_tensor(f"at_psS{i}", [P, 4 * P], F32)) for i in range(4)]
        psT = [ctx.enter_context(nc.psum_tensor(f"at_psT{i}", [P, 4, P], F32)) for i in range(2)]
        psO = ctx.enter_context(nc.psum_tensor("at_psO", [P, 2 * BANK], F32))
        c_in = sem("at_c_in")
        qr = sem("at_qr")
        sf = sem("at_sf")
        mr = sem("at_mr")
        er = sem("at_er")
        wr = sem("at_wr")
        tf = sem("at_tf")
        tr = sem("at_tr")
        of = sem("at_of")
        orr = sem("at_or")
        block = ctx.enter_context(nc.Block())

        def runs(eng, one):
            for p in range(NKV):
                with eng.Fori(0, 2) as i:
                    one(p, i + 2 * p)

        @block.sync
        def _(sp):
            sp.dma_start(mask[:], a["win_mask"]).then_inc(c_in, 16)
            sp.dma_start(sink[:], a["sinks"]).then_inc(c_in, 16)

        @block.tensor
        def _(pe):
            pe.sem_inc(tf, 4)
            pe.sem_inc(of, 2)

            def one(p, r):
                def score(v):
                    c, b, h = units[v]
                    pe.wait_ge(mr, NU * r + v + 1)
                    q, out = qs[c][:, P * b:P * b + P], psS[v % 4]
                    ks = keys(b)
                    if b == 0:
                        last = nc.tensor.matmul(out[:, 0:P], q, ktp[:, p, h, P:2 * P], start=True, stop=True)
                    else:
                        nc.tensor.matmul(out[:, 0:P], q, ktp[:, p, h, 0:P], start=True, stop=True)
                        n = len(ks) - 1
                        last = nc.tensor.matmul(out[:, P:P + n * P], q, ktp[:, p, h, P * ks[1]:P * ks[1] + n * P],
                                                start=True, stop=True)
                    last.then_inc(sf, 1)

                def turn(v):
                    pe.wait_ge(wr, NU * r + v + 1)
                    pe.wait_ge(tr, NU * r + v + 1)
                    for j in range(len(keys(units[v][1]))):
                        last = nc.tensor.transpose(psT[v % 2][:, j, :], ss[v % 4][:, P * j:P * j + P], cst.ident[:])
                    last.then_inc(tf, 1)

                def output(v):
                    c, b, h = units[v]
                    pe.wait_ge(tr, NU * r + v + 3)
                    if b == 0 and h == 0:
                        pe.wait_ge(orr, 2 * r + c + 1)
                    ks = keys(b)
                    for j, kt in enumerate(ks):
                        last = nc.tensor.matmul(psO[:, C0 + P * b:C0 + P * b + P], vp[:, p, h, kt, :], pt[v % 2][:, j, :],
                                                start=(h == 0 and j == 0), stop=(h == 1 and j == len(ks) - 1))
                    last.then_inc(of, 1)

                pe.wait_ge(qr, r + 1)
                for v in range(NU + 3):
                    if v < NU:
                        score(v)
                    if 2 <= v < NU + 2:
                        turn(v - 2)
                    if v >= 3:
                        output(v - 3)

            runs(pe, one)

        @block.scalar
        def _(act):
            act.sem_inc(tr, 2)
            act.wait_ge(c_in, 32)

            def one(p, r):
                def exps(v):
                    c, b, h = units[v]
                    w = P * len(keys(b))
                    act.wait_ge(mr, NU * r + v + 5)
                    nc.scalar.activation(ss[v % 4][:, 0:w], ss[v % 4][:, 0:w], ACT.Exp, bias=nm[:, v:v + 1],
                                         accum_out=den[:, v:v + 1])
                    nc.scalar.activation(es[:, v:v + 1], sink[:, ds(4 * r + 2 * c + h, 1)], ACT.Exp, bias=nm[:, v:v + 1])
                    act.drain().then_inc(er, 1)

                def move(v):
                    n = len(keys(units[v][1]))
                    act.wait_ge(tf, NU * r + v + 5)
                    act.wait_ge(of, NU * r + v + 1)
                    nc.scalar.activation(pt[v % 2][:, 0:n, :], psT[v % 2][:, 0:n, :], ACT.Copy).then_inc(tr, 1)

                for c in range(2):
                    nc.scalar.activation(qs[c][:], zT[:, ds(2 * r + c, 1), :].rearrange("p o t -> p (o t)"), ACT.Copy)
                act.drain().then_inc(qr, 1)
                for v in range(NU + 2):
                    if v < NU:
                        exps(v)
                    if v >= 2:
                        move(v - 2)

            runs(act, one)

        @block.vector
        def _(dve):
            dve.sem_inc(mr, 4)
            dve.sem_inc(orr, 1)
            dve.wait_ge(c_in, 32)

            def one(p, r):
                def scores(v):
                    c, b, h = units[v]
                    w = P * len(keys(b))
                    m = mask[:, 1, 0:w] if b == 0 else mask[:, KIND[b], 0:w]
                    dve.wait_ge(sf, NU * r + v + 1)
                    dve.wait_ge(tf, NU * r + v + 1)
                    nc.vector.scalar_tensor_tensor(ss[v % 4][:, 0:w], psS[v % 4][:, 0:w], SCALE, m,
                                                   op0=ALU.mult, op1=ALU.add)
                    dve.drain()
                    nc.vector.tensor_reduce(mx[:, v:v + 1], ss[v % 4][:, 0:w], AX, ALU.max)
                    dve.drain()
                    nc.vector.tensor_scalar(nm[:, v:v + 1], mx[:, v:v + 1], sink[:, ds(4 * r + 2 * c + h, 1)], -1.0,
                                            ALU.max, ALU.mult)
                    dve.drain().then_inc(mr, 1)

                def weights(v):
                    w = P * len(keys(units[v][1]))
                    dve.wait_ge(er, NU * r + v + 1)
                    nc.vector.tensor_tensor(den[:, v:v + 1], den[:, v:v + 1], es[:, v:v + 1], ALU.add)
                    dve.drain()
                    nc.vector.reciprocal(den[:, v:v + 1], den[:, v:v + 1])
                    dve.drain()
                    nc.vector.tensor_scalar(ss[v % 4][:, 0:w], ss[v % 4][:, 0:w], den[:, v:v + 1], None, ALU.mult)
                    dve.drain().then_inc(wr, 1)

                def out(c):
                    dve.wait_ge(of, NU * r + 10 * c + 12)
                    nc.vector.tensor_scalar(yT[:, ds(2 * r + c, 1), :].rearrange("p o t -> p (o t)"),
                                            psO[:, C0:C0 + T], 1.0, None, ALU.mult)
                    dve.drain().then_inc(orr, 1)

                for v in range(NU + 1):
                    if v < NU:
                        scores(v)
                    if v >= 1:
                        weights(v - 1)
                    if v == 12:
                        out(0)
                out(1)

            runs(dve, one)


class Const:
    pass


def program(nc, a, stage):
    with ExitStack() as ctx:
        sb = lambda n, s, d=F32: ctx.enter_context(nc.sbuf_tensor(n, s, d))
        cst = Const()
        cst.XT = sb("XT", [P, KD, T])
        cst.cond = sb("cond", [P, KD, 2])
        cst.ones = sb("ones", [P, P])
        cst.ident = sb("ident", [P, P])
        cst.normw = None
        normw = [sb(f"normw{l}", [P, 2, KD, 2]) for l in range(2)]
        cst.iota = sb("iota", [P, P])
        mods = [sb(f"modT{l}", [P, NMOD * KD, 2]) for l in range(2)]
        with ExitStack() as c1:
            ld = c1.enter_context(nc.semaphore("first_in"))
            sil = c1.enter_context(nc.semaphore("first_silu"))
            block = c1.enter_context(nc.Block())

            @block.sync
            def _(sp):
                sp.dma_start(cst.cond[:], a["cond"]).then_inc(ld, 16)
                sp.dma_start(cst.XT[:], a["xT"]).then_inc(ld, 16)
                sp.dma_start(cst.ident[:], a["ident"]).then_inc(ld, 16)
                for l in range(2):
                    sp.dma_start(normw[l][:], a["normw"][l]).then_inc(ld, 16)
                sp.dma_start(cst.iota[:], a["iota"]).then_inc(ld, 16)
                sp.wait_ge(ld, 96)

            @block.scalar
            def _(act):
                act.wait_ge(ld, 96)
                nc.scalar.activation(cst.cond[:], cst.cond[:], ACT.Silu).then_inc(sil, 1)
                act.wait_ge(sil, 1)

            @block.vector
            def _(dve):
                nc.vector.memset(cst.ones[:], 1.0)
                dve.drain()

        modulation(nc, cst, a["ada_w"][0], a["ada_b"][0], mods[0], "_0")
        cst.normw = normw[0]
        with ExitStack() as c1:
            yT = c1.enter_context(nc.sbuf_tensor("yT", [P, KD, T], F32))
            rec_mixer(nc, cst, mods[0], a["rec_w_in"], a["rec_gn"], a["masks"], a["state"], a["new_state"], yT)
            out_projection(nc, cst, a["rec_w_out"], yT, mods[0], "_rec")
        if stage >= 2:
            gates = nc.dram_tensor("gates", [P, T // 32, NK, 32], F32, kind="Internal").ap()
            peer(nc, cst, mods[0], a["wqk"][0], a["uT"][0], a["v"][0], gates, "_p0",
                 (a["ada_w"][1], a["ada_b"][1], mods[1]))
        if stage >= 3:
            cst.normw = normw[1]
            with ExitStack() as c1:
                zT = c1.enter_context(nc.sbuf_tensor("zT", [P, NQ + NKV, T], F32))
                ktp = c1.enter_context(nc.sbuf_tensor("ktp", [P, NKV, 2, KCOLS], F32))
                vp = c1.enter_context(nc.sbuf_tensor("vp", [P, NKV, 2, NT + 1, P], F32))
                attn_project(nc, cst, mods[1], a, zT, ktp, vp)
                yT = c1.enter_context(nc.sbuf_tensor("yTa", [P, KD, T], F32))
                attention(nc, cst, a, zT, ktp, vp, yT)
                out_projection(nc, cst, a["att_w_out"], yT, mods[1], "_att")
            peer(nc, cst, mods[1], a["wqk"][1], a["uT"][1], a["v"][1], gates, "_p1")
        with ExitStack() as c1:
            sv = c1.enter_context(nc.semaphore("last_out"))
            block = c1.enter_context(nc.Block())

            @block.sync
            def _(sp):
                sp.dma_start(a["yT"], cst.XT[:]).then_inc(sv, 16)
                sp.wait_ge(sv, 16)


STAGE = 3


def level_masks():
    m = np.zeros((P, 2 * LEVELS, P), np.int32)
    s, t = np.arange(P)[:, None], np.arange(P)[None, :]
    for l in range(LEVELS):
        same = (s >> (l + 1)) == (t >> (l + 1))
        hs, ht = (s >> l) & 1, (t >> l) & 1
        m[:, l, :] = same & (hs == 0) & (ht == 1)
        m[:, LEVELS + l, :] = same & (hs == 1) & (ht == 0)
    return m


def attention_constants():
    p, t = np.arange(P), np.arange(LAT)
    nf, grid = HD // 4, 64
    e, part = p % 32, (p % HD) // 32
    freqs = np.float32(10000.0) ** (-np.arange(nf, dtype=np.float32) / np.float32(nf))
    place = np.where(part[:, None] == 0, t[None, :] // grid, t[None, :] % grid).astype(np.float32)
    angle = place * freqs[e % nf][:, None]
    rot = np.zeros((P, P), np.float32)
    for m in range(P):
        if m % 32 < nf:
            rot[m + nf, m] = -1.0
        else:
            rot[m - nf, m] = 1.0
    q, k = np.arange(P)[:, None], np.arange(P)[None, :]
    left, right, none = np.where(k >= q, 0, NEG), np.where(k <= q, 0, NEG), np.zeros((P, P))
    mask = np.stack([np.concatenate(r, 1) for r in ((none, none, right, none), (none, left, none, right),
                                                    (none, left, none, none))], 1)
    return {"cos": np.cos(angle).astype(np.float32), "sin": np.sin(angle).astype(np.float32), "rot": rot,
            "heads": (p[:, None] // HD == p[None, :] // HD).astype(np.float32), "win_mask": mask.astype(np.float32)}


def kernel(**inputs):
    import concourse.bacc as bacc
    from concourse.bass_utils import run_bass_kernel_spmd

    x = {n: np.asarray(v) for n, v in inputs.items()}
    L = x["ada_w"].shape[0]
    f = np.ascontiguousarray
    tok = np.concatenate([x["x_prompt"][0], x["x_sample"][0]], 0)
    cond = np.stack([x["c_ctx"], x["c"][0]], -1)
    arr = {
        "xT": f(tok.reshape(T, KD, P).transpose(2, 1, 0)),
        "cond": f(cond.reshape(KD, P, 2).transpose(1, 0, 2)),
        "ident": np.eye(P, dtype=np.float32),
        "normw": f(np.repeat(x["norm_w"].reshape(L, 2, KD, P).transpose(0, 3, 1, 2)[..., None], 2, -1)),
        "ada_w": f(x["ada_w"].reshape(L, KD, P, 12, 512).transpose(0, 3, 2, 1, 4)),
        "ada_b": f(np.repeat(x["ada_b"].reshape(L, NMOD * KD, P).transpose(0, 2, 1)[..., None], 2, -1)),
        "rec_w_in": f(x["rec_w_in"][0].reshape(KD, P, 5, RH, P)[:, :, [0, 1, 2, 4, 3]].transpose(3, 2, 1, 0, 4)),
        "rec_gn": f(x["rec_gn_w"].reshape(P, 1)),
        "masks": level_masks(),
        "state": f(x["state_rec"][0, 0]),
        "rec_w_out": f(x["rec_w_out"][0].reshape(KD, P, KD, P).transpose(2, 1, 0, 3)),
    }
    if STAGE >= 2:
        arr["iota"] = f(np.broadcast_to(np.arange(P, dtype=np.float32), (P, P)))
        wq = x["peer_w_q"].reshape(L, KD, P, PH, 2, P).transpose(0, 4, 3, 2, 1, 5)
        keys = x["peer_keys"].transpose(0, 2, 1, 4, 3)[:, :, :, :, None, :]
        arr["wqk"] = f(np.concatenate([wq, keys], 4).reshape(L, 2 * PH, P, KD + 1, P))
        arr["uT"] = f(x["peer_u"].reshape(L, NK, NK, KD, P).transpose(0, 2, 4, 3, 1))
        arr["v"] = f(x["peer_v"])
    outs = {"yT": (P, KD, T), "new_state": (2, RH, P, P)}
    if STAGE >= 3:
        w = x["attn_w_qkv"][0]
        wq = w[:, :AH * HD].reshape(KD, P, 2, 2, 4, HD).transpose(2, 4, 1, 0, 3, 5).reshape(NQ, P, KD, P)
        wk = w[:, AH * HD:(AH + AKV) * HD].reshape(KD, P, NKV, P).transpose(2, 1, 0, 3)
        arr["wqk_att"] = f(np.concatenate([wq, wk], 0))
        arr["wv_att"] = f(w[:, (AH + AKV) * HD:].reshape(KD, P, AKV * HD).transpose(1, 0, 2))
        arr["qk_gain"] = f(np.stack([np.tile(x["attn_qn_w"][0], 2)] * NQ + [np.tile(x["attn_kn_w"][0], 2)] * NKV, 1))
        arr["cache_k"] = f(x["cache_k"][0, 0].reshape(P, NKV, P).transpose(2, 1, 0))
        arr["cache_v"] = f(x["cache_v"][0, 0])
        arr["sinks"] = f(np.broadcast_to(x["attn_sink"][0].reshape(2, 2, 4).transpose(0, 2, 1).reshape(AH), (P, AH)))
        arr["att_w_out"] = f(x["attn_w_out"][0].reshape(2, 2, 4, HD, D).transpose(0, 2, 1, 3, 4)
                             .reshape(NQ, P, KD, P).transpose(2, 1, 0, 3))
        arr.update(attention_constants())
        outs["new_k"], outs["new_v"] = (P, NKV, CTX), (CTX, AKV * HD)
    nc = bacc.Bacc("TRN2", target_bir_lowering=False, num_devices=1)
    aps = {n: nc.dram_tensor("in_" + n, v.shape, mybir.dt.from_np(v.dtype), kind="ExternalInput").ap()
           for n, v in arr.items()}
    for n, s in outs.items():
        aps[n] = nc.dram_tensor("out_" + n, s, F32, kind="ExternalOutput").ap()
    if STAGE >= 2:
        aps["v"] = aps["v"].rearrange("l (i j) d -> l j i d", j=NK)
    program(nc, aps, STAGE)
    r = run_bass_kernel_spmd(nc, [{"in_" + n: v for n, v in arr.items()}], core_ids=[0]).results[0]
    y = r["out_yT"].transpose(2, 1, 0).reshape(T, D)
    state = r["out_new_state"].reshape(1, 1, 2, RH, P, P)
    new_k = r["out_new_k"].transpose(2, 1, 0).reshape(1, 1, CTX, AKV, HD)
    new_v = r["out_new_v"].reshape(1, 1, CTX, AKV, HD)
    return (y[None, :CTX], y[None, CTX:], state, new_k, new_v)
```

```python
from contextlib import ExitStack

import numpy as np

import concourse.bass as bass
from concourse import mybir

P = 128
D = 1024
KD = D // P
CTX, LAT = 128, 512
T = CTX + LAT
NT = T // P
NMOD = 6
RH = 8
AH, AKV, HD = 16, 4, 64
HALFT = T // 2
BANK = 512
C0 = BANK - CTX
EPS = 1e-6
NEG = -1e30
LEVELS = 7
PH, NK, TK = 8, 128, 16
SCALE = HD ** -0.5

F32 = mybir.dt.float32
BF16 = mybir.dt.bfloat16
U32 = mybir.dt.uint32
I32 = mybir.dt.int32
ALU = mybir.AluOpType
ACT = mybir.ActivationFunctionType
AX = mybir.AxisListType.X
ds = bass.ds


def segments():
    return ((slice(0, CTX), slice(C0, BANK)), (slice(CTX, T), slice(BANK, BANK + LAT)))


class Modulation:
    PIECES = NMOD * D // 512

    def __init__(self, nc, ctx, cst, ada_w, adab_in, modT, tag):
        sb = lambda n, s: ctx.enter_context(nc.sbuf_tensor(n + tag, s, F32))
        sem = lambda n: nc.alloc_semaphore(n + tag)
        self.nc, self.cst, self.ada_w, self.adab_in, self.modT = nc, cst, ada_w, adab_in, modT
        self.wst = [sb(f"ada_wst{s}", [P, KD, 512]) for s in range(2)]
        self.rows = [sb(f"ada_rows{s}", [2, 512]) for s in range(2)]
        self.adab = sb("ada_bias", [P, NMOD * KD, 2])
        self.ps_rows = ctx.enter_context(nc.psum_tensor("ada_psr" + tag, [2, 512], F32))
        self.ps_cols = [ctx.enter_context(nc.psum_tensor(f"ada_psc{s}" + tag, [P, 4, 2], F32)) for s in range(2)]
        self.w_in = [sem(f"ada_w_in{s}") for s in range(2)]
        self.b_in = sem("ada_b_in")
        self.rowp = sem("ada_rowp")
        self.rowc = sem("ada_rowc")
        self.colp = sem("ada_colp")
        self.colr = sem("ada_colr")

    def start(self, sp):
        sp.dma_start(self.adab[:], self.adab_in).then_inc(self.b_in, 16)

    def sp(self, sp, n, s):
        sp.wait_ge(self.rowp, n + 1)
        sp.dma_start(self.wst[s][:], self.ada_w[n]).then_inc(self.w_in[s], 16)

    def pe(self, pe, rnd, n, s):
        nc = self.nc
        pe.wait_ge(self.w_in[s], 16 * rnd + 16)
        for k in range(KD):
            last = nc.tensor.matmul(self.ps_rows[:], self.cst.cond[:, k, :], self.wst[s][:, k, :],
                                    start=(k == 0), stop=(k == KD - 1))
        last.then_inc(self.rowp, 1)
        pe.wait_ge(self.rowc, n + 1)
        pe.wait_ge(self.colr, n + 1)
        for m in range(4):
            last = nc.tensor.matmul(self.ps_cols[s][:, m, :], self.rows[s][:, P * m:P * m + P],
                                    self.cst.ident[0:2, 0:2], start=True, stop=True)
        last.then_inc(self.colp, 1)

    def act(self, act, n, s):
        act.wait_ge(self.rowp, n + 3)
        self.nc.scalar.activation(self.rows[s][:], self.ps_rows[:], ACT.Copy).then_inc(self.rowc, 1)

    def dve(self, dve, n, s):
        dve.wait_ge(self.colp, n + 1)
        at = ds(4 * n, 4)
        self.nc.vector.tensor_tensor(self.modT[:, at, :], self.ps_cols[s][:], self.adab[:, at, :],
                                     ALU.add).then_inc(self.colr, 1)


def modulation(nc, cst, ada_w, adab_in, modT, tag):
    with nc.cleanup_on_exit(), ExitStack() as ctx:
        mod = Modulation(nc, ctx, cst, ada_w, adab_in, modT, tag)
        block = ctx.enter_context(nc.Block())

        @block.sync
        def _(sp):
            mod.start(sp)
            with sp.Fori(0, mod.PIECES // 2) as i:
                for s in range(2):
                    mod.sp(sp, 2 * i + s, s)

        @block.tensor
        def _(pe):
            pe.sem_inc(mod.rowp, 2)
            with pe.Fori(0, mod.PIECES // 2) as i:
                for s in range(2):
                    mod.pe(pe, i, 2 * i + s, s)

        @block.scalar
        def _(act):
            with act.Fori(0, mod.PIECES // 2) as i:
                for s in range(2):
                    mod.act(act, 2 * i + s, s)

        @block.vector
        def _(dve):
            dve.sem_inc(mod.colr, 2)
            dve.wait_ge(mod.b_in, 16)
            with dve.Fori(0, mod.PIECES // 2) as i:
                for s in range(2):
                    mod.dve(dve, 2 * i + s, s)


class Norm:

    def __init__(self, nc, ctx, cst, tag, modT, which, sq, hT, sum_ps):
        sem = lambda n: nc.alloc_semaphore(n + tag)
        self.nc, self.cst, self.modT, self.which = nc, cst, modT, which
        self.sq, self.hT, self.sum_ps = sq, hT, sum_ps
        self.rstd = ctx.enter_context(nc.sbuf_tensor("rstd" + tag, [P, T], F32))
        self.gain = ctx.enter_context(nc.sbuf_tensor("gain" + tag, [P, KD, 2], F32))
        self.squares = sem("norm_squares")
        self.sums = sem("norm_sums")
        self.inv = sem("norm_inv")
        self.root = sem("norm_root")
        self.scaled = sem("norm_scaled")
        self.ready = sem("norm_ready")

    def act(self, act):
        nc = self.nc
        for k in range(KD):
            nc.scalar.activation(self.sq[:, k], self.cst.XT[:, k], ACT.Square).then_inc(self.squares, 1)
        act.wait_ge(self.inv, 1)
        nc.scalar.activation(self.rstd[:], self.rstd[:], ACT.Sqrt).then_inc(self.root, 1)
        shift = self.modT[:, 3 * self.which * KD:3 * self.which * KD + KD, :]
        for k in range(KD):
            act.wait_ge(self.scaled, k + 1)
            for c, tok in ((0, slice(0, CTX)), (1, slice(CTX, T))):
                nc.scalar.activation(self.hT[:, k, tok], self.hT[:, k, tok], ACT.Identity, bias=shift[:, k, c:c + 1])
            act.drain().then_inc(self.ready, 1)

    def pe(self, pe):
        nc = self.nc
        for k in range(KD):
            pe.wait_ge(self.squares, k + 1)
            for tok, col in segments():
                last = nc.tensor.matmul(self.sum_ps[:, col], self.cst.ones[:], self.sq[:, k, tok],
                                        start=(k == 0), stop=(k == KD - 1))
        last.then_inc(self.sums, 1)

    def dve(self, dve):
        nc, n0 = self.nc, (3 * self.which + 1) * KD
        nc.vector.scalar_tensor_tensor(self.gain[:], self.modT[:, n0:n0 + KD, :], 1.0,
                                       self.cst.normw[:, self.which], op0=ALU.add, op1=ALU.mult)
        dve.wait_ge(self.sums, 1)
        nc.vector.tensor_scalar(self.rstd[:], self.sum_ps[:, C0:C0 + T], 1.0 / D, EPS, ALU.mult, ALU.add)
        dve.drain()
        nc.vector.reciprocal(self.rstd[:], self.rstd[:]).then_inc(self.inv, 1)
        dve.wait_ge(self.root, 1)
        for k in range(KD):
            for c, tok in ((0, slice(0, CTX)), (1, slice(CTX, T))):
                nc.vector.scalar_tensor_tensor(self.hT[:, k, tok], self.cst.XT[:, k, tok], self.gain[:, k, c:c + 1],
                                               self.rstd[:, tok], op0=ALU.mult, op1=ALU.mult)
            dve.drain().then_inc(self.scaled, 1)


def out_projection(nc, cst, w_out, yT, modT, tag):
    with nc.cleanup_on_exit(), ExitStack() as ctx:
        sem = lambda n: nc.alloc_semaphore(n + tag)
        wst = ctx.enter_context(nc.sbuf_tensor("wo_st" + tag, [P, 4, KD, P], F32))
        ps = [ctx.enter_context(nc.psum_tensor(f"wo_ps{s}" + tag, [P, 2 * BANK], F32)) for s in range(2)]
        w_in = [sem(f"wo_in{s}") for s in range(4)]
        w_free, prod, psum_free = sem("wo_free"), sem("wo_prod"), sem("wo_psum_free")
        block = ctx.enter_context(nc.Block())

        @block.sync
        def _(sp):
            for m in range(KD):
                if m >= 4:
                    sp.wait_ge(prod, m - 3)
                sp.dma_start(wst[:, m % 4], w_out[m]).then_inc(w_in[m % 4], 16)

        @block.tensor
        def _(pe):
            for m in range(KD):
                pe.wait_ge(w_in[m % 4], 16 * (m // 4 + 1))
                if m >= 2:
                    pe.wait_ge(psum_free, m - 1)
                for k in range(KD):
                    for tok, col in segments():
                        last = nc.tensor.matmul(ps[m % 2][:, col], wst[:, m % 4, k, :], yT[:, k, tok],
                                                start=(k == 0), stop=(k == KD - 1))
                last.then_inc(prod, 1)

        @block.vector
        def _(dve):
            for m in range(KD):
                dve.wait_ge(prod, m + 1)
                for c, (tok, col) in enumerate(segments()):
                    last = nc.vector.scalar_tensor_tensor(cst.XT[:, m, tok], ps[m % 2][:, col],
                                                          modT[:, 2 * KD + m, c:c + 1], cst.XT[:, m, tok],
                                                          op0=ALU.mult, op1=ALU.add)
                last.then_inc(psum_free, 1)


def rec_mixer(nc, cst, modT, w_in_d, gn_in, masks_in, st_in, st_out, yT):
    Q_, FF_, FB_, G_, V_ = range(5)
    with nc.cleanup_on_exit(), ExitStack() as ctx:
        sb = lambda n, s, d=F32: ctx.enter_context(nc.sbuf_tensor(n, s, d))
        sem = lambda n: nc.alloc_semaphore(n)
        hT = sb("rec_hT", [P, KD, T])
        ms = sb("rec_ms", [P, RH, T])
        wst = sb("rec_wst", [P, 5, KD, P])
        masks = sb("rec_masks", [P, 2 * LEVELS, P], I32)
        gn = sb("rec_gn", [P, 1])
        z = [{n: sb(f"rec_{n}{s}", [P, T]) for n in ("q", "g", "f0", "f1", "k0", "k1", "v")} for s in range(2)]
        ksum = sb("rec_ksum", [P, T])
        ql = [sb(f"rec_ql{i}", [P, T]) for i in range(3)]
        kl = [sb(f"rec_kl{i}", [P, T]) for i in range(3)]
        qf = [sb(f"rec_qf{d}", [P, T]) for d in range(2)]
        kf = [sb(f"rec_kf{d}", [P, T]) for d in range(2)]
        tot = [sb(f"rec_tot{d}", [P, 2 * T]) for d in range(2)]
        acc = sb("rec_acc", [P, T])
        kt = [sb(f"rec_kt{d}", [P, NT, P]) for d in range(2)]
        st = sb("rec_st", [P, 2, 4, P])
        sto = sb("rec_sto", [P, 2, P])
        oT = sb("rec_oT", [P, T])
        osq = sb("rec_osq", [P, T])
        psA = [ctx.enter_context(nc.psum_tensor(f"rec_psA{s}", [P, 2 * BANK], F32)) for s in range(2)]
        psB = [ctx.enter_context(nc.psum_tensor(f"rec_psB{s}", [P, 2 * BANK], F32)) for s in range(2)]
        norm = Norm(nc, ctx, cst, "_rec", modT, 0, yT, hT, psA[0])
        small_in = sem("rec_small_in")
        wsem = [sem(f"rec_w_in{n}") for n in range(5)]
        proj = sem("rec_proj")
        psa_read = sem("rec_psa_read")
        zsem = sem("rec_z")
        zfree = sem("rec_zfree")
        lvl = sem("rec_lvl")
        full = sem("rec_full")
        psb_read = sem("rec_psb_read")
        accr = sem("rec_accr")
        ktr = sem("rec_ktr")
        st_ld = sem("rec_st_ld")
        st_rdy = sem("rec_st_rdy")
        st_sv = sem("rec_st_sv")
        osr = sem("rec_osr")
        otr = sem("rec_otr")
        seen = sem("rec_seen")
        fin = sem("rec_fin")
        NB = 20
        TR0, UU, OO, NN = 15, 17, 18, 19
        block = ctx.enter_context(nc.Block())

        @block.sync
        def _(sp):
            sp.dma_start(masks[:], masks_in).then_inc(small_in, 16)
            sp.dma_start(gn[:], gn_in).then_inc(small_in, 16)

            def head(h, first):
                for n in range(5):
                    if not first:
                        sp.wait_ge(proj, 5 * h + n - 4)
                    sp.dma_start(wst[:, n], w_in_d[h, n]).then_inc(wsem[n], 16)
                if not first:
                    sp.wait_ge(full, NB * h)
                    sp.wait_ge(accr, h)
                for d in range(2):
                    sp.dma_start(st[:, d, 0, :], st_in[d, h]).then_inc(st_ld, 16)

            def store(h):
                sp.wait_ge(st_rdy, h + 1)
                for d in range(2):
                    sp.dma_start(st_out[d, h], sto[:, d, :]).then_inc(st_sv, 16)

            head(0, True)
            with sp.Fori(1, RH) as h:
                head(h, False)
                store(h - 1)
            store(RH - 1)
            sp.wait_ge(st_sv, 32 * RH)

        @block.tensor
        def _(pe):
            norm.pe(pe)

            def project(h, n, quarters=range(4), first=False):
                ps = psA[n % 2]
                if n == V_:
                    prods = [(ps[:, C0 + P * t:C0 + P * t + P], hT[:, k, P * t:P * t + P], wst[:, n, k, :], k)
                             for t in range(NT) for k in range(KD)]
                else:
                    prods = [(ps[:, col], wst[:, n, k, :], hT[:, k, tok], k) for k in range(KD) for tok, col in segments()]
                for f in quarters:
                    if f == 0:
                        pe.wait_ge(wsem[n], 16 * h + 16)
                        pe.wait_ge(psa_read, 5 * h + max(n, 1))
                    for m in range(f * len(prods) // 4, (f + 1) * len(prods) // 4):
                        out, lhs, rhs, k = prods[m]
                        if first and m % len(segments()) == 0:
                            pe.wait_ge(norm.ready, k + 1)
                        last = nc.tensor.matmul(out, lhs, rhs, start=(k == 0), stop=(k == KD - 1))
                    if f == 3:
                        last.then_inc(proj, 1)

            def tiles(n, h, lhs, rhs, which=range(NT)):
                ps = psB[n % 2]
                for t in which:
                    a = slice(P * t, P * t + P)
                    last = nc.tensor.matmul(ps[:, C0 + P * t:C0 + P * t + P], lhs[:, a], rhs[:, a],
                                            start=True, stop=True)
                last.then_inc(full, 1)

            def head(h, s, nxt):
                zz = z[s]

                def piece(n):
                    if nxt is not None:
                        project(nxt, n // 4, [n % 4])

                for n in range(15):
                    piece(n)
                    pe.wait_ge(psb_read, NB * h + n + 1)
                    pe.wait_ge(lvl, 15 * h + n + 1)
                    if n == 0:
                        tiles(0, h, ksum, zz["q"])
                        continue
                    d, l = divmod(n - 1, LEVELS)
                    i = (n - 1) % 3
                    tiles(n, h, zz[f"k{d}"] if l == 0 else kl[i], ql[i])
                for d in range(2):
                    n = TR0 + d
                    piece(n)
                    pe.wait_ge(psb_read, NB * h + n + 1)
                    pe.wait_ge(accr, 3 * h + d + 1)
                    for t in range(NT):
                        last = nc.tensor.transpose(psB[n % 2][:, C0 + P * t:C0 + P * t + P],
                                                   kf[d][:, P * t:P * t + P], cst.ident[:])
                    last.then_inc(full, 1)
                n = UU
                piece(n)
                pe.wait_ge(psb_read, NB * h + n + 1)
                pe.wait_ge(ktr, 2 * h + 2)
                for d in range(2):
                    for j in range(4):
                        t = (0 if j == 3 else j + 1) if d == 0 else (0 if j == 3 else 4 - j)
                        last = nc.tensor.matmul(psB[n % 2][:, BANK * d + P * j:BANK * d + P * j + P],
                                                kt[d][:, t, :], zz["v"][:, P * t:P * t + P], start=True, stop=True)
                last.then_inc(full, 1)
                n = OO
                piece(n)
                pe.wait_ge(psb_read, NB * h + n + 1)
                pe.wait_ge(accr, 3 * h + 3)
                for t in range(NT):
                    a, o = slice(P * t, P * t + P), psB[n % 2][:, C0 + P * t:C0 + P * t + P]
                    last = nc.tensor.matmul(o, zz["v"][:, a], acc[:, a], start=True, stop=(t == 0))
                    if t > 0:
                        nc.tensor.matmul(o, st[:, 0, t - 1, :], qf[0][:, a], start=False, stop=False)
                        last = nc.tensor.matmul(o, st[:, 1, 4 - t, :], qf[1][:, a], start=False, stop=True)
                last.then_inc(full, 1)
                n = NN
                piece(n)
                pe.wait_ge(psb_read, NB * h + n + 1)
                pe.wait_ge(osr, h + 1)
                for tok, col in segments():
                    last = nc.tensor.matmul(psB[n % 2][:, col], cst.ones[:], osq[:, tok], start=True, stop=True)
                last.then_inc(full, 1)

            for n in range(5):
                project(0, n, first=(n == 0))
            with pe.Fori(0, RH // 2 - 1) as i:
                head(2 * i, 0, 2 * i + 1)
                head(2 * i + 1, 1, 2 * i + 2)
            head(RH - 2, 0, RH - 1)
            head(RH - 1, 1, None)

        @block.scalar
        def _(act):
            act.sem_inc(psa_read, 1)
            norm.act(act)

            def evacuate(h, s, parts):
                zz = z[s]
                for n in parts:
                    if n == 0:
                        act.wait_ge(zfree, h + 1)
                    act.wait_ge(proj, 5 * h + n + 1)
                    src = psA[n % 2][:, C0:C0 + T]
                    if n in (Q_, G_):
                        dst = zz["q" if n == Q_ else "g"]
                        nc.scalar.activation(dst[:], src, ACT.Silu)
                    elif n in (FF_, FB_):
                        nc.scalar.activation(zz[f"f{n - FF_}"][:], src, ACT.Sigmoid)
                        nc.scalar.activation(zz[f"k{n - FF_}"][:], src, ACT.Sigmoid, scale=-1.0)
                    else:
                        nc.scalar.activation(zz["v"][:], src, ACT.Copy)
                    act.drain().then_inc(psa_read, 1)
                if V_ in parts:
                    act.sem_inc(zsem, 1)

            def squares(h):
                act.wait_ge(otr, h + 1)
                nc.scalar.activation(osq[:], oT[:], ACT.Square).then_inc(osr, 1)

            def both(h, s):
                evacuate(h, s, [Q_, FF_, FB_, G_])
                squares(h - 1)
                evacuate(h, s, [V_])

            evacuate(0, 0, range(5))
            with act.Fori(0, RH // 2 - 1) as i:
                both(2 * i + 1, 1)
                both(2 * i + 2, 0)
            both(RH - 1, 1)
            squares(RH - 1)
            act.wait_ge(fin, 1)
            nc.scalar.activation(ms[:], ms[:], ACT.Sqrt).then_inc(fin, 1)

        @block.vector
        def _(dve):
            norm.dve(dve)
            dve.sem_inc(zfree, 2)
            dve.sem_inc(psb_read, 2)
            dve.wait_ge(small_in, 32)

            def build(h, s, n):
                zz = z[s]
                d, l = divmod(n - 1, LEVELS)
                i, H = (n - 1) % 3, 1 << l
                nb = T // H
                at = 2 * T - 2 * nb
                q_src, k_src = (ql[(i - 1) % 3], kl[(i - 1) % 3]) if l > 0 else (zz["q"], None)
                if n >= 4:
                    dve.wait_ge(full, NB * h + n - 2)
                if l == 0:
                    nc.vector.tensor_tensor(ql[i][:], zz["q"][:], zz[f"f{d}"][:], ALU.mult)
                else:
                    grow(d, l, q_src, ql[i], zz[f"k{d}"] if l == 1 else k_src, kl[i], zz)
                dve.drain().then_inc(lvl, 1)

            def grow(d, l, q_src, q_dst, k_src, k_dst, zz):
                H = 1 << l
                h2, nb = H // 2, T // H
                prev = zz[f"f{d}"][:] if l == 1 else tot[d][:, 2 * T - 4 * nb:2 * T - 2 * nb]
                pair = prev.rearrange("p (b e) -> p b e", e=2)
                nc.vector.tensor_tensor(tot[d][:, 2 * T - 2 * nb:2 * T - nb], pair[:, :, 0], pair[:, :, 1], ALU.mult)
                for src, dst, e in ((q_src, q_dst, 1 - d), (k_src, k_dst, d)):
                    sv = src[:].rearrange("p (b e x) -> p b e x", e=2, x=h2)
                    dv = dst[:].rearrange("p (b e x) -> p b e x", e=2, x=h2)
                    other = pair[:, :, 1 - e].unsqueeze(2).to_broadcast([P, nb, h2])
                    nc.vector.tensor_tensor(dv[:, :, e, :], sv[:, :, e, :], other, ALU.mult)
                    nc.vector.tensor_copy(dv[:, :, 1 - e, :], sv[:, :, 1 - e, :])

            def take(h, n):
                dve.wait_ge(full, NB * h + n + 1)
                dve.sem_inc(seen, 1)
                src = psB[n % 2][:, C0:C0 + T].rearrange("p (t x) -> p t x", x=P)
                dst = acc[:].rearrange("p (t x) -> p t x", x=P)
                if n == 0:
                    nc.vector.tensor_copy(dst, src).then_inc(psb_read, 1)
                else:
                    nc.vector.copy_predicated(dst, masks[:, n - 1, :].unsqueeze(1).to_broadcast([P, NT, P]),
                                              src).then_inc(psb_read, 1)
                dve.drain()

            def head(h, s, last):
                zz = z[s]
                dve.wait_ge(zsem, h + 1)
                nc.vector.tensor_tensor(ksum[:], zz["k0"][:], zz["k1"][:], ALU.add)
                dve.drain().then_inc(lvl, 1)
                for n in range(1, 15):
                    build(h, s, n)
                    take(h, n - 1)
                    if n % LEVELS == 0:
                        d = n // LEVELS - 1
                        i = (n - 1) % 3
                        grow(d, LEVELS, ql[i], qf[d], kl[i], kf[d], zz)
                        dve.drain().then_inc(accr, 1)
                take(h, 14)
                for d in range(2):
                    n = TR0 + d
                    dve.wait_ge(full, NB * h + n + 1)
                    nc.vector.tensor_copy(kt[d][:].rearrange("p t x -> p (t x)"),
                                          psB[n % 2][:, C0:C0 + T]).then_inc(psb_read, 1)
                    dve.drain().then_inc(ktr, 1)
                dve.wait_ge(full, NB * h + UU + 1)
                dve.wait_ge(st_ld, 32 * h + 32)
                if not (isinstance(h, int) and h == 0):
                    dve.wait_ge(st_sv, 32 * h)
                for d in range(2):
                    nc.vector.tensor_copy(sto[:, d, :], psB[UU % 2][:, BANK * d + 3 * P:BANK * d + 4 * P])
                for j in range(3):
                    for d in range(2):
                        t = j + 1 if d == 0 else 4 - j
                        decay = tot[d][:, 2 * T - 2 * NT + t:2 * T - 2 * NT + t + 1]
                        nc.vector.scalar_tensor_tensor(st[:, d, j + 1, :], st[:, d, j, :], decay,
                                                       psB[UU % 2][:, BANK * d + P * j:BANK * d + P * j + P],
                                                       op0=ALU.mult, op1=ALU.add)
                    dve.drain()
                dve.sem_inc(psb_read, 1)
                dve.sem_inc(st_rdy, 1)
                dve.sem_inc(accr, 1)
                dve.wait_ge(full, NB * h + OO + 1)
                nc.vector.tensor_copy(oT[:], psB[OO % 2][:, C0:C0 + T])
                nc.vector.tensor_tensor(yT[:, ds(h, 1), :].rearrange("p a t -> p (a t)"),
                                        psB[OO % 2][:, C0:C0 + T], zz["g"][:], ALU.mult)
                dve.drain()
                dve.sem_inc(otr, 1)
                dve.sem_inc(psb_read, 1)
                dve.sem_inc(zfree, 1)
                dve.wait_ge(full, NB * h + NN + 1)
                nc.vector.tensor_scalar(ms[:, ds(h, 1), :].rearrange("p a t -> p (a t)"),
                                        psB[NN % 2][:, C0:C0 + T], 1.0 / P, EPS, ALU.mult, ALU.add)
                dve.drain().then_inc(psb_read, 1)

            head(0, 0, False)
            head(1, 1, False)
            with dve.Fori(1, RH // 2) as i:
                head(2 * i, 0, False)
                head(2 * i + 1, 1, False)
            nc.vector.reciprocal(ms[:], ms[:]).then_inc(fin, 1)
            dve.wait_ge(fin, 2)
            nc.vector.scalar_tensor_tensor(yT[:], yT[:], gn[:, 0:1], ms[:], op0=ALU.mult, op1=ALU.mult)


def peer_scores(nc, cst, modT, wqk, h_hi, h_lo, vals, idxs, tag):
    NS = 2 * PH
    with nc.cleanup_on_exit(), ExitStack() as ctx:
        sb = lambda n, s, d=F32: ctx.enter_context(nc.sbuf_tensor(n + tag, s, d))
        sem = lambda n: nc.alloc_semaphore(n + tag)
        hT, sq = sb("ps_hT", [P, KD, T]), sb("ps_sq", [P, KD, T])
        wst = [sb(f"ps_wst{s}", [P, KD + 1, P]) for s in range(4)]
        qT = [sb(f"ps_qT{s}", [P, T]) for s in range(2)]
        sc = [sb(f"ps_sc{s}", [P, NT, P]) for s in range(2)]
        sc2 = sb("ps_sc2", [P, NT, P])
        v8, i8 = sb("ps_v8", [P, NT, TK]), sb("ps_i8", [P, NT, TK], U32)
        psA = [ctx.enter_context(nc.psum_tensor(f"ps_psA{s}" + tag, [P, 2 * BANK], F32)) for s in range(2)]
        psB = [ctx.enter_context(nc.psum_tensor(f"ps_psB{s}" + tag, [P, 2 * BANK], F32)) for s in range(2)]
        norm = Norm(nc, ctx, cst, "_ps" + tag, modT, 1, sq, hT, psA[0])
        w_in = [sem(f"ps_w_in{s}") for s in range(4)]
        qpr, qcp = sem("ps_qpr"), sem("ps_qcp")
        spr, scp = sem("ps_spr"), sem("ps_scp")
        top = sem("ps_top")
        qfree, sfree = sem("ps_qfree"), sem("ps_sfree")
        seen = sem("ps_seen")
        split = sem("ps_split")
        block = ctx.enter_context(nc.Block())

        @block.sync
        def _(sp):
            for s in range(4):
                sp.dma_start(wst[s][:], wqk[s]).then_inc(w_in[s], 16)
            with sp.Fori(1, NS // 4) as i:
                for s in range(4):
                    sp.wait_ge(spr, 4 * i + s - 3)
                    sp.dma_start(wst[s][:], wqk[4 * i + s]).then_inc(w_in[s], 16)

        @block.tensor
        def _(pe):
            norm.pe(pe)

            def query(i, s, first=False):
                n = 4 * i + s
                pe.wait_ge(w_in[s], 16 * i + 16)
                pe.wait_ge(qfree, n + 1)
                for k in range(KD):
                    if first:
                        pe.wait_ge(norm.ready, k + 1)
                    for tok, col in segments():
                        last = nc.tensor.matmul(psA[s % 2][:, col], wst[s][:, k, :], hT[:, k, tok],
                                                start=(k == 0), stop=(k == KD - 1))
                last.then_inc(qpr, 1)

            def score(i, s):
                n = 4 * i + s
                pe.wait_ge(qcp, n + 1)
                pe.wait_ge(sfree, n + 1)
                for t in range(NT):
                    last = nc.tensor.matmul(psB[s % 2][:, C0 + P * t:C0 + P * t + P], qT[s % 2][:, P * t:P * t + P],
                                            wst[s][:, KD, :], start=True, stop=True)
                last.then_inc(spr, 1)

            query(0, 0, True)
            with pe.Fori(0, NS // 4 - 1) as i:
                for s in range(4):
                    query(i + (s + 1) // 4, (s + 1) % 4)
                    score(i, s)
            for s in range(4):
                if s < 3:
                    query(NS // 4 - 1, s + 1)
                score(NS // 4 - 1, s)

        @block.scalar
        def _(act):
            act.sem_inc(qfree, 2)
            act.sem_inc(sfree, 2)
            norm.act(act)
            nc.scalar.activation(h_hi[:], hT[:], ACT.Copy).then_inc(split, 1)
            with act.Fori(0, NS // 2) as i:
                for s in range(2):
                    n = 2 * i + s
                    act.wait_ge(qpr, n + 1)
                    nc.scalar.activation(qT[s][:], psA[s][:, C0:C0 + T], ACT.Copy)
                    act.drain()
                    act.sem_inc(qcp, 1)
                    act.sem_inc(qfree, 1)
                    act.wait_ge(spr, n + 1)
                    act.wait_ge(top, n + 1)
                    nc.scalar.activation(sc[s][:].rearrange("p t x -> p (t x)"), psB[s][:, C0:C0 + T], ACT.Copy)
                    act.drain()
                    act.sem_inc(scp, 1)
                    act.sem_inc(sfree, 1)

        @block.vector
        def _(dve):
            norm.dve(dve)
            dve.sem_inc(top, 2)
            dve.wait_ge(split, 1)
            nc.vector.tensor_tensor(h_lo[:], hT[:], h_hi[:], ALU.subtract)
            with dve.Fori(0, NS // 2) as i:
                for s in range(2):
                    n = 2 * i + s
                    dve.wait_ge(scp, n + 1)
                    dve.sem_inc(seen, 1)
                    for t in range(NT):
                        nc.vector.max(v8[:, t, 0:8], sc[s][:, t, :])
                    dve.drain()
                    for t in range(NT):
                        nc.vector.max_index(i8[:, t, 0:8], v8[:, t, 0:8], sc[s][:, t, :])
                        nc.vector.match_replace(sc2[:, t, :], v8[:, t, 0:8], sc[s][:, t, :], -3e38)
                    dve.drain().then_inc(top, 1)
                    for t in range(NT):
                        nc.vector.max(v8[:, t, 8:16], sc2[:, t, :])
                    dve.drain()
                    for t in range(NT):
                        nc.vector.max_index(i8[:, t, 8:16], v8[:, t, 8:16], sc2[:, t, :])
                    dve.drain()
                    nc.vector.tensor_copy(vals[:, :, ds(n, 1), :].rearrange("p t a k -> p t (a k)"), v8[:])
                    nc.vector.tensor_copy(idxs[:, :, ds(n, 1), :].rearrange("p t a k -> p t (a k)"), i8[:])
                    dve.drain()


class EarlyHidden:

    def __init__(self, nc, ctx, uT, h_hi, h_lo, hid, base, ps_slots, tag):
        sb = lambda n, s, d=F32: ctx.enter_context(nc.sbuf_tensor(n + tag, s, d))
        sem = lambda n: nc.alloc_semaphore(n + tag)
        self.nc, self.uT, self.h_hi, self.h_lo, self.hid, self.base = nc, uT, h_hi, h_lo, hid, base
        self.nps = ps_slots
        self.ust = [sb(f"eh_ust{s}", [P, KD, P]) for s in range(2)]
        self.u_hi = [sb(f"eh_uhi{s}", [P, KD, P], BF16) for s in range(2)]
        self.u_lo = [sb(f"eh_ulo{s}", [P, KD, P], BF16) for s in range(2)]
        self.ge = [sb(f"eh_ge{s}", [P, T]) for s in range(2)]
        self.psH = [ctx.enter_context(nc.psum_tensor(f"eh_psH{s}" + tag, [P, 2, BANK], F32))
                    for s in range(ps_slots)]
        self.u_in = [sem(f"eh_u_in{s}") for s in range(2)]
        self.uh = sem("eh_uh")
        self.ul = sem("eh_ul")
        self.hp = sem("eh_hp")
        self.hg = sem("eh_hg")
        self.sv = [sem(f"eh_sv{s}") for s in range(2)]

    def start_act(self, act):
        act.sem_inc(self.hg, self.nps)
        for s in range(2):
            act.sem_inc(self.sv[s], 16)

    def start_pe(self, pe):
        pe.sem_inc(self.hp, 2)

    def start_pool(self, pool):
        pool.sem_inc(self.ul, 2)

    def sp(self, sp, m, s):
        sp.wait_ge(self.ul, m + 1)
        sp.dma_start(self.ust[s][:], self.uT[self.base + m]).then_inc(self.u_in[s], 16)

    def take_high(self, act, m, rnd, s):
        act.wait_ge(self.u_in[s], 16 * rnd + 16)
        act.wait_ge(self.hp, m + 1)
        self.nc.scalar.activation(self.u_hi[s][:], self.ust[s][:], ACT.Copy).then_inc(self.uh, 1)

    def take_low(self, pool, m, s):
        pool.wait_ge(self.uh, m + 1)
        self.nc.gpsimd.tensor_tensor(self.u_lo[s][:], self.ust[s][:], self.u_hi[s][:],
                                     ALU.subtract).then_inc(self.ul, 1)

    def pe(self, pe, m, s):
        pe.wait_ge(self.ul, m + 3)
        pe.wait_ge(self.hg, m + 1)
        hidden_products(self.nc, self.psH[s % self.nps], self.u_hi[s], self.u_lo[s],
                        self.h_hi, self.h_lo).then_inc(self.hp, 1)

    def gelu(self, act, m, rnd, s):
        act.wait_ge(self.hp, m + 3)
        act.wait_ge(self.sv[s], 16 * rnd + 16)
        self.nc.scalar.activation(self.ge[s][:].rearrange("p (a x) -> p a x", a=2),
                                  self.psH[s % self.nps][:, :, 0:HALFT], ACT.Gelu).then_inc(self.hg, 1)
        act.drain()
        act.dma_start(self.hid[self.base + m], self.ge[s][:]).then_inc(self.sv[s], 16)

    def loop_sp(self, sp, tiles):
        with sp.Fori(0, tiles // 2) as i:
            for s in range(2):
                self.sp(sp, 2 * i + s, s)

    def loop_pool(self, pool, tiles):
        self.start_pool(pool)
        with pool.Fori(0, tiles // 2) as i:
            for s in range(2):
                self.take_low(pool, 2 * i + s, s)

    def finish(self, act, tiles):
        for s in range(2):
            act.wait_ge(self.sv[s], 16 * (tiles // 2) + 16)


def hidden_products(nc, ps, hi, lo, h_hi, h_lo):
    prods = [(a, b, k) for k in range(KD) for a, b in ((hi, h_hi), (hi, h_lo), (lo, h_hi))]
    for m, (a, b, k) in enumerate(prods):
        for x in range(2):
            last = nc.tensor.matmul(ps[:, x, 0:HALFT], a[:, k, :], b[:, k, HALFT * x:HALFT * x + HALFT],
                                    start=(m == 0), stop=(m == len(prods) - 1))
    return last


def peer_select(nc, cst, vals, idxs, picks, early, before, per, tag, ada=None):
    W = PH * TK
    with nc.cleanup_on_exit(), ExitStack() as ctx:
        sb = lambda n, s, d=F32: ctx.enter_context(nc.sbuf_tensor(n + tag, s, d))
        sem = lambda n: nc.alloc_semaphore(n + tag)
        vt, it = sb("sl_vt", [P, 2 * PH, TK]), sb("sl_it", [P, 2 * PH, TK])
        cand, cand2 = sb("sl_cand", [P, PH, TK, TK]), sb("sl_cand2", [P, PH, TK * TK])
        best, pos = sb("sl_best", [P, PH, TK]), sb("sl_pos", [P, PH, TK], U32)
        half = sb("sl_half", [P, 2, W], U32)
        halff = sb("sl_halff", [P, 2, W])
        eq = [sb(f"sl_eq{s}", [P, W, TK]) for s in range(2)]
        ex = sb("sl_ex", [P, W])
        row = sb("sl_row", [P, 3, W])
        den = sb("sl_den", [P, PH])
        ps = ctx.enter_context(nc.psum_tensor("sl_ps" + tag, [P, 3, W], F32))
        ex_in, ex_out = sem("sl_ex_in"), sem("sl_ex_out")
        rows = sem("sl_rows")
        trs = sem("sl_trs")
        taken = sem("sl_taken")
        eh = EarlyHidden(nc, ctx, *early, 2, "_sl" + tag)
        mod = Modulation(nc, ctx, cst, *ada, tag) if ada else None
        tiles = before + per * NT
        block = ctx.enter_context(nc.Block())

        @block.sync
        def _(sp):
            for s in range(2):
                eh.sp(sp, s, s)
            if mod:
                mod.start(sp)
                for s in range(2):
                    mod.sp(sp, s, s)
            for m in range(2, before):
                eh.sp(sp, m, m % 2)
            with sp.Fori(0, NT) as t:
                for x in range(per):
                    eh.sp(sp, before + per * t + x, x % 2)
                    if mod:
                        mod.sp(sp, 2 * t + 2 + x, x)

        @block.gpsimd
        def _(pool):
            eh.loop_pool(pool, tiles)

        @block.scalar
        def _(act):
            def step(m, rnd, s):
                eh.gelu(act, m - 1, rnd - 1 + s, 1 - s)
                eh.take_high(act, m + 1, rnd + s, 1 - s)

            eh.start_act(act)
            act.sem_inc(taken, 1)
            for s in range(2):
                eh.take_high(act, s, 0, s)
            if mod:
                for s in range(2):
                    mod.act(act, s, s)
            for m in range(1, before - 1):
                step(m, m // 2, m % 2)
            with act.Fori(0, NT) as t:
                for x in range(per):
                    m0 = before - 1 + x
                    step(m0 + per * t, m0 // 2 + per // 2 * t, m0 % 2)
                    if mod:
                        mod.act(act, 2 * t + 2 + x, x)
                    if x == 1:
                        act.wait_ge(ex_in, t + 1)
                        nc.scalar.activation(ex[:], ex[:], ACT.Exp).then_inc(ex_out, 1)
                act.wait_ge(trs, t + 2)
                nc.scalar.activation(picks[:, :, ds(P * t, P)], ps[:], ACT.Copy).then_inc(taken, 1)
            for m in (tiles - 2, tiles - 1):
                eh.gelu(act, m, m // 2, m % 2)
            eh.finish(act, tiles)

        @block.tensor
        def _(pe):
            eh.start_pe(pe)
            pe.sem_inc(trs, 1)
            if mod:
                pe.sem_inc(mod.rowp, 2)
                for s in range(2):
                    mod.pe(pe, 0, s, s)
            for m in range(before):
                eh.pe(pe, m, m % 2)
            with pe.Fori(0, NT) as t:
                for x in range(per):
                    if mod:
                        mod.pe(pe, t + 1, 2 * t + 2 + x, x)
                    if x == per - 1:
                        pe.wait_ge(rows, t + 1)
                        pe.wait_ge(taken, t + 1)
                        for j in range(3):
                            last = nc.tensor.transpose(ps[:, j, :], row[:, j, :], cst.ident[:])
                        last.then_inc(trs, 1)
                    eh.pe(pe, before + per * t + x, x % 2)

        @block.vector
        def _(dve):
            if mod:
                dve.sem_inc(mod.colr, 2)
                dve.wait_ge(mod.b_in, 16)
                for s in range(2):
                    mod.dve(dve, s, s)
            with dve.Fori(0, NT) as t:
                nc.vector.tensor_copy(vt[:], vals[:, ds(t, 1)].rearrange("p o a k -> p (o a) k"))
                nc.vector.tensor_copy(it[:], idxs[:, ds(t, 1)].rearrange("p o a k -> p (o a) k"))
                dve.drain()
                nc.vector.tensor_tensor(cand[:], vt[:, 0:PH, :].unsqueeze(3).to_broadcast([P, PH, TK, TK]),
                                        vt[:, PH:, :].unsqueeze(2).to_broadcast([P, PH, TK, TK]), ALU.add)
                dve.drain()
                c = cand[:].rearrange("p h a b -> p h (a b)")
                for h in range(PH):
                    nc.vector.max(best[:, h, 0:8], c[:, h, :])
                dve.drain()
                for h in range(PH):
                    nc.vector.max_index(pos[:, h, 0:8], best[:, h, 0:8], c[:, h, :])
                    nc.vector.match_replace(cand2[:, h, :], best[:, h, 0:8], c[:, h, :], -3e38)
                dve.drain()
                for h in range(PH):
                    nc.vector.max(best[:, h, 8:16], cand2[:, h, :])
                dve.drain()
                for h in range(PH):
                    nc.vector.max_index(pos[:, h, 8:16], best[:, h, 8:16], cand2[:, h, :])
                nc.vector.tensor_tensor(ex[:].rearrange("p (h k) -> p h k", k=TK), best[:],
                                        best[:, :, 0:1].to_broadcast([P, PH, TK]), ALU.subtract)
                dve.drain().then_inc(ex_in, 1)
                pf = pos[:].rearrange("p h k -> p (h k)")
                nc.vector.tensor_scalar(half[:, 0, :], pf, 4, None, ALU.logical_shift_right)
                nc.vector.tensor_scalar(half[:, 1, :], pf, 15, None, ALU.bitwise_and)
                dve.drain()
                nc.vector.tensor_copy(halff[:], half[:])
                dve.drain()
                for j in range(2):
                    nc.vector.tensor_tensor(eq[j][:], halff[:, j, :].unsqueeze(2).to_broadcast([P, W, TK]),
                                            cst.iota[:, 0:TK].unsqueeze(1).to_broadcast([P, W, TK]), ALU.is_equal)
                dve.drain()
                for j in range(2):
                    e4 = eq[j][:].rearrange("p (h k) a -> p h k a", k=TK)
                    nc.vector.tensor_tensor(e4, e4, it[:, PH * j:PH * j + PH, :].unsqueeze(2)
                                            .to_broadcast([P, PH, TK, TK]), ALU.mult)
                dve.drain()
                dve.wait_ge(trs, t + 1)
                for j in range(2):
                    nc.vector.tensor_reduce(row[:, j, :], eq[j][:], AX, ALU.add)
                dve.wait_ge(ex_out, t + 1)
                nc.vector.tensor_reduce(den[:], ex[:].rearrange("p (h k) -> p h k", k=TK), AX, ALU.add)
                dve.drain()
                nc.vector.reciprocal(den[:], den[:])
                dve.drain()
                nc.vector.tensor_tensor(row[:, 2, :].rearrange("p (h k) -> p h k", k=TK),
                                        ex[:].rearrange("p (h k) -> p h k", k=TK),
                                        den[:].unsqueeze(2).to_broadcast([P, PH, TK]), ALU.mult)
                dve.drain().then_inc(rows, 1)
                if mod:
                    for s in range(2):
                        mod.dve(dve, 2 * t + 2 + s, s)


def peer_gates(nc, cst, picks, gates, early, tag):
    TB, TU, TI = 32, 16, 8
    NBL, NU = T // TB, T // TU
    with nc.cleanup_on_exit(), ExitStack() as ctx:
        sb = lambda n, s, d=BF16: ctx.enter_context(nc.sbuf_tensor(n + tag, s, d))
        sem = lambda n: nc.alloc_semaphore(n + tag)
        keyrow = sb("gt_keyrow", [P, NK, TI])
        pk = sb("gt_pk", [P, 4, T])
        oh1 = [sb(f"gt_oh1{r}", [P, TU // TI, NK, TI]) for r in range(4)]
        oh2 = sb("gt_oh2", [P, TU // TI, NK, TI])
        ohh = [sb(f"gt_ohh{r}", [P, TU // TI, NK, TI]) for r in range(4)]
        ohl = [sb(f"gt_ohl{r}", [P, TU // TI, NK, TI]) for r in range(4)]
        gs = [sb(f"gt_gs{s}", [P, NK, TB], F32) for s in range(2)]
        ps = [ctx.enter_context(nc.psum_tensor(f"gt_ps{q}" + tag, [P, TI, NK], F32)) for q in range(3)]
        SLOT = [c % 3 for c in range(8)]
        LAST = [-2, -1, -3, 0, 1, 2, 3, 4]
        oh = sem("gt_oh")
        mm = sem("gt_mm")
        ev = sem("gt_ev")
        sv = [sem(f"gt_sv{s}") for s in range(2)]
        eh = EarlyHidden(nc, ctx, *early, 1, "_gt" + tag)
        block = ctx.enter_context(nc.Block())

        @block.vector
        def _(dve):
            nc.vector.tensor_copy(keyrow[:], cst.iota[:].unsqueeze(2).to_broadcast([P, NK, TI]))
            nc.vector.tensor_copy(pk[:, 0:3], picks[:])
            dve.drain()
            nc.vector.tensor_tensor(pk[:, 3], picks[:, 2], pk[:, 2], ALU.subtract)
            dve.drain()
            keys = keyrow[:].unsqueeze(1).to_broadcast([P, TU // TI, NK, TI])
            with dve.Fori(0, NU // 4) as i:
                for r in range(4):
                    n = 4 * i + r
                    part = [pk[:, j, ds(4 * TU * i + TU * r, TU)].rearrange("p (g x) -> p g x", x=TI).unsqueeze(2)
                            .to_broadcast([P, TU // TI, NK, TI]) for j in range(4)]
                    nc.vector.tensor_tensor(oh2[:], part[1], keys, ALU.is_equal)
                    dve.wait_ge(mm, n + 1)
                    nc.vector.tensor_tensor(oh1[r][:], part[0], keys, ALU.is_equal)
                    dve.drain()
                    nc.vector.tensor_tensor(ohh[r][:], oh2[:], part[2], ALU.mult)
                    nc.vector.tensor_tensor(ohl[r][:], oh2[:], part[3], ALU.mult)
                    dve.drain().then_inc(oh, 1)

        @block.tensor
        def _(pe):
            pe.sem_inc(mm, 4)
            eh.start_pe(pe)
            with pe.Fori(0, NBL // 2) as i:
                for r in range(4):
                    pe.wait_ge(oh, 4 * i + r + 1)
                    for g in range(2):
                        c = 2 * r + g
                        pe.wait_ge(ev, 8 * i + LAST[c] + 4)
                        for x in range(TI):
                            o = ps[SLOT[c]][:, x, :]
                            nc.tensor.matmul(o, oh1[r][:, g, :, x], ohh[r][:, g, :, x], start=True, stop=False)
                            last = nc.tensor.matmul(o, oh1[r][:, g, :, x], ohl[r][:, g, :, x],
                                                    start=False, stop=True)
                    last.then_inc(mm, 1)
                    if r % 2 == 1:
                        eh.pe(pe, 2 * i + r // 2, r // 2)

        @block.gpsimd
        def _(pool):
            eh.loop_pool(pool, NBL)

        @block.scalar
        def _(act):
            act.sem_inc(ev, 3)
            eh.start_act(act)

            def rows(i, s, first):
                if not first:
                    act.wait_ge(sv[s], 16 * i)
                for q in range(4):
                    if q % 2 == 0:
                        act.wait_ge(mm, 2 * (2 * i + s) + q // 2 + 5)
                    nc.scalar.activation(gs[s][:, :, 8 * q:8 * q + 8].rearrange("p j t -> p t j"),
                                         ps[SLOT[4 * s + q]][:], ACT.Copy).then_inc(ev, 1)
                act.drain()
                act.dma_start(gates[:, ds(2 * i + s, 1)].rearrange("p o j t -> p (o j t)"),
                              gs[s][:].rearrange("p j t -> p (j t)")).then_inc(sv[s], 16)

            def step(i, s, first=False, last=False):
                b = 2 * i + s
                if not (first and s == 0):
                    eh.gelu(act, b - 1, i - 1 + s, 1 - s)
                rows(i, s, first)
                if not (last and s == 1):
                    eh.take_high(act, b + 1, i + s, 1 - s)

            eh.take_high(act, 0, 0, 0)
            for s in range(2):
                step(0, s, first=True)
            with act.Fori(1, NBL // 2 - 1) as i:
                for s in range(2):
                    step(i, s)
            for s in range(2):
                step(NBL // 2 - 1, s, last=True)
            eh.gelu(act, NBL - 1, NBL // 2 - 1, 1)
            eh.finish(act, NBL)

        @block.sync
        def _(sp):
            eh.loop_sp(sp, NBL)
            for s in range(2):
                sp.wait_ge(sv[s], 16 * (NBL // 2))


def peer_experts(nc, cst, modT, uT, v, gates, hid, early, h_hi, h_lo, tag):
    J, TB = 4, 32
    NG = NK // J
    with nc.cleanup_on_exit(), ExitStack() as ctx:
        sb = lambda n, s, d=F32: ctx.enter_context(nc.sbuf_tensor(n + tag, s, d))
        sem = lambda n: nc.alloc_semaphore(n + tag)
        pst = lambda n: ctx.enter_context(nc.psum_tensor(n + tag, [P, 2, BANK], F32))
        facc = sb("ex_facc", [P, KD, T])
        ust = [sb(f"ex_ust{s}", [P, KD, P]) for s in range(2)]
        vst = [sb(f"ex_vst{s}", [P, KD, P]) for s in range(2)]
        gst = [sb(f"ex_gst{s}", [P, T // TB, J, TB]) for s in range(2)]
        est = [sb(f"ex_est{s}", [P, J, T]) for s in range(2)]
        u_hi = [sb(f"ex_uhi{s}", [P, KD, P], BF16) for s in range(2)]
        u_lo = [sb(f"ex_ulo{s}", [P, KD, P], BF16) for s in range(2)]
        v_hi = [sb(f"ex_vhi{s}", [P, J, KD, P], BF16) for s in range(2)]
        v_lo = [sb(f"ex_vlo{s}", [P, J, KD, P], BF16) for s in range(2)]
        ge = [sb(f"ex_ge{s}", [P, T]) for s in range(2)]
        gh = sb("ex_gh", [P, T])
        g_hi = [sb(f"ex_ghi{s}", [P, J, T], BF16) for s in range(2)]
        g_lo = [sb(f"ex_glo{s}", [P, J, T], BF16) for s in range(2)]
        psH = [pst(f"ex_psH{s}") for s in range(2)]
        psV = [pst(f"ex_psV{s}") for s in range(2)]
        u_in = [sem(f"ex_u_in{s}") for s in range(2)]
        v_in = [sem(f"ex_v_in{s}") for s in range(2)]
        g_in = [sem(f"ex_g_in{s}") for s in range(2)]
        uh, ul = sem("ex_uh"), sem("ex_ul")
        vh, vl = sem("ex_vh"), sem("ex_vl")
        hp, hg = sem("ex_hp"), sem("ex_hg")
        hr = sem("ex_hr")
        vp, vr = sem("ex_vp"), sem("ex_vr")
        block = ctx.enter_context(nc.Block())
        late = NG - early
        rounds = (late - 1) // 2

        def g_in_count(g, s, is_early):
            late_s = (late + 1 - s) // 2
            return 16 * (g - s) + 32 - 16 * late_s if is_early else 8 * (g - s) + 16

        @block.sync
        def _(sp):
            def group(g, s, is_early):
                for q in range(J):
                    n = J * g + q
                    if not is_early:
                        sp.wait_ge(ul, n + 1)
                        sp.dma_start(ust[q % 2][:], uT[n]).then_inc(u_in[q % 2], 16)
                    sp.wait_ge(vl, n + 1)
                    sp.dma_start(vst[q % 2][:].rearrange("p k x -> p (k x)"), v[n]).then_inc(v_in[q % 2], 16)
                    if q == 0:
                        sp.wait_ge(hr, J * g + J)
                        sp.dma_start(gst[s][:], gates[:, :, ds(J * g, J), :]).then_inc(g_in[s], 16)
                        if is_early:
                            sp.dma_start(est[s][:], hid[ds(J * (g - late), J)].rearrange("j p t -> p j t")
                                         ).then_inc(g_in[s], 16)

            group(0, 0, False)
            with sp.Fori(0, rounds) as i:
                group(2 * i + 1, 1, False)
                group(2 * i + 2, 0, False)
            with sp.Fori(rounds, NG // 2 - 1) as i:
                group(2 * i + 1, 1, True)
                group(2 * i + 2, 0, True)
            group(NG - 1, 1, True)

        @block.tensor
        def _(pe):
            def hidden(g, q):
                n, s = J * g + q, q % 2
                pe.wait_ge(ul, n + 3)
                pe.wait_ge(hg, n + 1)
                hidden_products(nc, psH[s], u_hi[s], u_lo[s], h_hi, h_lo).then_inc(hp, 1)

            def output(g, k, s):
                if k == 0:
                    pe.wait_ge(hr, J * g + 3 * J)
                    pe.wait_ge(vl, J * g + J + 2)
                pe.wait_ge(vr, KD * g + k + 1)
                prods = [(a, b, q) for q in range(J) for a, b in ((v_hi, g_hi), (v_hi, g_lo), (v_lo, g_hi))]
                for m, (a, b, q) in enumerate(prods):
                    for x in range(2):
                        last = nc.tensor.matmul(psV[k % 2][:, x, 0:HALFT], a[s][:, q, k, :],
                                                b[s][:, q, HALFT * x:HALFT * x + HALFT],
                                                start=(m == 0), stop=(m == len(prods) - 1))
                last.then_inc(vp, 1)

            def group(g, s, is_early):
                for q in range(J):
                    if not is_early:
                        hidden(g, q)
                    output(g - 1, 2 * q, 1 - s)
                    output(g - 1, 2 * q + 1, 1 - s)

            pe.sem_inc(hp, 2)
            pe.sem_inc(vp, 2 * KD)
            for q in range(J):
                hidden(0, q)
            with pe.Fori(0, rounds) as i:
                group(2 * i + 1, 1, False)
                group(2 * i + 2, 0, False)
            with pe.Fori(rounds, NG // 2 - 1) as i:
                group(2 * i + 1, 1, True)
                group(2 * i + 2, 0, True)
            group(NG - 1, 1, True)
            for k in range(KD):
                output(NG - 1, k, 1)

        @block.scalar
        def _(act):
            def take_u(g, q):
                s = q % 2
                act.wait_ge(u_in[s], 16 * (2 * g + q // 2) + 16)
                act.wait_ge(hp, J * g + q + 1)
                nc.scalar.activation(u_hi[s][:], ust[s][:], ACT.Copy).then_inc(uh, 1)

            def take_v(g, q, s):
                act.wait_ge(v_in[q % 2], 16 * (2 * g + q // 2) + 16)
                act.wait_ge(vp, KD * g + KD)
                nc.scalar.activation(v_hi[s][:, q], vst[q % 2][:], ACT.Copy).then_inc(vh, 1)

            def gelu(g, q):
                n, s = J * g + q, q % 2
                act.wait_ge(hp, n + 3)
                act.wait_ge(hr, n + 2 * J - 1)
                nc.scalar.activation(ge[s][:].rearrange("p (a x) -> p a x", a=2), psH[s][:, :, 0:HALFT],
                                     ACT.Gelu).then_inc(hg, 1)

            def group(g, s, is_early, last=False):
                for q in range(J):
                    if not is_early:
                        if q < J - 1:
                            take_u(g, q + 1)
                        elif not last:
                            take_u(g + 1, 0)
                        gelu(g, q)
                    take_v(g, q, s)

            act.sem_inc(hg, 2)
            take_u(0, 0)
            group(0, 0, False)
            with act.Fori(0, rounds - 1) as i:
                group(2 * i + 1, 1, False)
                group(2 * i + 2, 0, False)
            group(late - 2, 1, False)
            group(late - 1, 0, False, last=True)
            with act.Fori(rounds, NG // 2 - 1) as i:
                group(2 * i + 1, 1, True)
                group(2 * i + 2, 0, True)
            group(NG - 1, 1, True)

        @block.vector
        def _(dve):
            def take_u(g, q):
                s = q % 2
                dve.wait_ge(uh, J * g + q + 1)
                nc.vector.tensor_tensor(u_lo[s][:], ust[s][:], u_hi[s][:], ALU.subtract).then_inc(ul, 1)

            def take_v(g, q, s):
                dve.wait_ge(vh, J * g + q + 1)
                nc.vector.tensor_tensor(v_lo[s][:, q], vst[q % 2][:], v_hi[s][:, q], ALU.subtract).then_inc(vl, 1)

            def gate(g, q, s, is_early):
                if q == 0:
                    dve.wait_ge(g_in[s], g_in_count(g, s, is_early))
                if is_early:
                    src = est[s][:, q, :]
                else:
                    src = ge[q % 2][:]
                    dve.wait_ge(hg, J * g + q + 3)
                nc.vector.tensor_tensor(gh[:].rearrange("p (b t) -> p b t", t=TB),
                                        src.rearrange("p (b t) -> p b t", t=TB), gst[s][:, :, q, :], ALU.mult)
                dve.drain()
                dve.wait_ge(vp, KD * g + KD)
                nc.vector.tensor_copy(g_hi[s][:, q], gh[:])
                dve.drain()
                nc.vector.tensor_tensor(g_lo[s][:, q], gh[:], g_hi[s][:, q], ALU.subtract)
                dve.drain().then_inc(hr, 1)

            def add_up(g, k):
                dve.wait_ge(vp, KD * g + k + 1 + 2 * KD)
                dst = facc[:, k, :].rearrange("p (a x) -> p a x", a=2)
                nc.vector.tensor_tensor(dst, psV[k % 2][:, :, 0:HALFT], dst, ALU.add).then_inc(vr, 1)

            def group(g, s, is_early, first=False, last=False):
                for q in range(J):
                    if not is_early:
                        if q < J - 1:
                            take_u(g, q + 1)
                        elif not last:
                            take_u(g + 1, 0)
                    gate(g, q, s, is_early)
                    take_v(g, q, s)
                    if not first:
                        add_up(g - 1, 2 * q)
                        add_up(g - 1, 2 * q + 1)

            dve.sem_inc(ul, 2)
            dve.sem_inc(vl, 2)
            dve.sem_inc(hr, 2 * J)
            dve.sem_inc(vr, 2)
            take_u(0, 0)
            nc.vector.memset(facc[:], 0.0)
            group(0, 0, False, first=True)
            with dve.Fori(0, rounds - 1) as i:
                group(2 * i + 1, 1, False)
                group(2 * i + 2, 0, False)
            group(late - 2, 1, False)
            group(late - 1, 0, False, last=True)
            with dve.Fori(rounds, NG // 2 - 1) as i:
                group(2 * i + 1, 1, True)
                group(2 * i + 2, 0, True)
            group(NG - 1, 1, True)
            for k in range(KD):
                add_up(NG - 1, k)
            dve.drain()
            for k in range(KD):
                for c, tok in ((0, slice(0, CTX)), (1, slice(CTX, T))):
                    nc.vector.scalar_tensor_tensor(cst.XT[:, k, tok], facc[:, k, tok], modT[:, 5 * KD + k, c:c + 1],
                                                   cst.XT[:, k, tok], op0=ALU.mult, op1=ALU.add)
            dve.drain()


def peer(nc, cst, modT, wqk, uT, v, gates, hid, tag, ada=None):
    before, per = (6, 2) if ada else (4, 4)
    picked = before + per * NT
    early_u = uT[NK - picked - T // 32:]
    with ExitStack() as ctx:
        h_hi = ctx.enter_context(nc.sbuf_tensor("h_hi" + tag, [P, KD, T], BF16))
        h_lo = ctx.enter_context(nc.sbuf_tensor("h_lo" + tag, [P, KD, T], BF16))
        with ExitStack() as c1:
            vals = c1.enter_context(nc.sbuf_tensor("vals" + tag, [P, NT, 2 * PH, TK], F32))
            idxs = c1.enter_context(nc.sbuf_tensor("idxs" + tag, [P, NT, 2 * PH, TK], F32))
            picks = c1.enter_context(nc.sbuf_tensor("picks" + tag, [P, 3, T], F32))
            peer_scores(nc, cst, modT, wqk, h_hi, h_lo, vals, idxs, tag)
            peer_select(nc, cst, vals, idxs, picks, (early_u, h_hi, h_lo, hid, 0), before, per, tag, ada)
            peer_gates(nc, cst, picks, gates, (early_u, h_hi, h_lo, hid, picked), tag)
        peer_experts(nc, cst, modT, uT, v, gates, hid, (picked + T // 32) // 4, h_hi, h_lo, tag)


NQ, NKV = AH * HD // P, AKV * HD // P
KC0 = 2 * P
KCOLS = 2 * P + LAT


def attn_project(nc, cst, modT, a, zT, ktp, vp):
    NZ = NQ + NKV
    with nc.cleanup_on_exit(), ExitStack() as ctx:
        sb = lambda n, s, d=F32: ctx.enter_context(nc.sbuf_tensor(n, s, d))
        sem = lambda n: nc.alloc_semaphore(n)
        hT = sb("ap_hT", [P, KD, T])
        wst = [sb(f"ap_wst{s}", [P, KD, P]) for s in range(2)]
        wv = sb("ap_wv", [P, KD, AKV * HD])
        sqz = [sb(f"ap_sqz{s}", [P, T]) for s in range(2)]
        rs = [sb(f"ap_rs{s}", [P, T]) for s in range(2)]
        turn = sb("ap_turn", [P, LAT])
        cos, sin = sb("ap_cos", [P, LAT]), sb("ap_sin", [P, LAT])
        heads, rot = sb("ap_heads", [P, P]), sb("ap_rot", [P, P])
        gain = sb("ap_gain", [P, NZ])
        vctx = sb("ap_vctx", [P, AKV * HD])
        psA = [ctx.enter_context(nc.psum_tensor(f"ap_psA{s}", [P, 2 * BANK], F32)) for s in range(2)]
        psB = ctx.enter_context(nc.psum_tensor("ap_psB", [P, 2 * BANK], F32))
        psR = [ctx.enter_context(nc.psum_tensor(f"ap_psR{s}", [P, LAT], F32)) for s in range(2)]
        norm = Norm(nc, ctx, cst, "_ap", modT, 0, zT[:, 0:KD, :], hT, psA[0])
        w_in = [sem(f"ap_w_in{s}") for s in range(2)]
        c_in = sem("ap_c_in")
        v_in = sem("ap_v_in")
        cleared = sem("ap_cleared")
        cache_in = sem("ap_cache_in")
        pr = sem("ap_pr")
        zc = sem("ap_zc")
        sm = sem("ap_sm")
        iv = sem("ap_iv")
        rt = sem("ap_rt")
        nz = sem("ap_nz")
        tn = sem("ap_tn")
        ro = sem("ap_ro")
        vpr = sem("ap_vpr")
        kr, vr = sem("ap_kr"), sem("ap_vr")
        outs = sem("ap_outs")
        def values(t):
            return psA[t // 4][:, 256 * (t % 4):256 * (t % 4) + 256]

        block = ctx.enter_context(nc.Block())

        @block.sync
        def _(sp):
            for s in range(2):
                sp.dma_start(wst[s][:], a["wqk_att"][s]).then_inc(w_in[s], 16)
            for dst, name in ((heads, "heads"), (rot, "rot"), (gain, "qk_gain"), (cos, "cos"), (sin, "sin")):
                sp.dma_start(dst[:], a[name]).then_inc(c_in, 16)
            sp.dma_start(wv[:], a["wv_att"]).then_inc(v_in, 16)
            sp.wait_ge(cleared, 1)
            for p in range(NKV):
                for h in range(2):
                    c = slice(HD * h, HD * h + HD)
                    sp.dma_start(ktp[c, p, h, 0:P], a["cache_k"][c, p, :]).then_inc(cache_in, 16)
                    sp.dma_start(vp[:, p, h, 0, c], a["cache_v"][:, 2 * p + h, :]).then_inc(cache_in, 16)
            with sp.Fori(1, NZ // 2) as i:
                for s in range(2):
                    sp.wait_ge(pr, 2 * i + s - 1)
                    sp.dma_start(wst[s][:], a["wqk_att"][2 * i + s]).then_inc(w_in[s], 16)
            sp.wait_ge(kr, 1)
            sp.dma_start(a["new_k"], zT[:, NQ:NZ, 0:CTX]).then_inc(outs, 16)
            sp.wait_ge(vr, 1)
            sp.dma_start(a["new_v"], vctx[:]).then_inc(outs, 16)
            sp.wait_ge(outs, 32)
            sp.wait_ge(cache_in, 64 * NKV)

        @block.tensor
        def _(pe):
            norm.pe(pe)
            pe.wait_ge(c_in, 80)

            def project(i, s, first=False):
                n = 2 * i + s
                pe.wait_ge(w_in[s], 16 * i + 16)
                pe.wait_ge(zc, n + 1)
                for k in range(KD):
                    if first:
                        pe.wait_ge(norm.ready, k + 1)
                    for tok, col in segments():
                        last = nc.tensor.matmul(psA[s][:, col], wst[s][:, k, :], hT[:, k, tok],
                                                start=(k == 0), stop=(k == KD - 1))
                last.then_inc(pr, 1)

            def sums(n, s, first=False):
                pe.wait_ge(zc, n + 3)
                if not first:
                    pe.wait_ge(iv, n)
                for tok, col in segments():
                    last = nc.tensor.matmul(psB[:, col], heads[:], sqz[s][:, tok], start=True, stop=True)
                last.then_inc(sm, 1)

            def turned(n, s):
                pe.wait_ge(nz, n + 1)
                pe.wait_ge(ro, n + 1)
                nc.tensor.matmul(psR[s][:], rot[:], zT[:, ds(n, 1), CTX:T].rearrange("p o t -> p (o t)"),
                                 start=True, stop=True).then_inc(tn, 1)

            project(0, 0, True)
            project(0, 1)
            sums(0, 0, True)
            with pe.Fori(1, NZ // 2) as i:
                for s in range(2):
                    project(i, s)
                    sums(2 * i + s - 1, 1 - s)
                    turned(2 * i + s - 2, s)
            pe.wait_ge(v_in, 16)

            def value(t):
                for k in range(KD):
                    last = nc.tensor.matmul(values(t), hT[:, k, P * t:P * t + P], wv[:, k, :],
                                            start=(k == 0), stop=(k == KD - 1))
                last.then_inc(vpr, 1)

            for t in range(4):
                value(t)
            sums(NZ - 1, 1)
            turned(NZ - 2, 0)
            value(4)
            turned(NZ - 1, 1)

        @block.scalar
        def _(act):
            act.sem_inc(zc, 2)
            norm.act(act)

            def take(n, s):
                act.wait_ge(pr, n + 1)
                src = psA[s][:, C0:C0 + T]
                nc.scalar.activation(zT[:, ds(n, 1), :].rearrange("p o t -> p (o t)"), src, ACT.Copy)
                nc.scalar.activation(sqz[s][:], src, ACT.Square)
                act.drain().then_inc(zc, 1)

            def root(n, s):
                act.wait_ge(iv, n + 1)
                nc.scalar.activation(rs[s][:], rs[s][:], ACT.Sqrt).then_inc(rt, 1)

            take(0, 0)
            take(1, 1)
            root(0, 0)
            with act.Fori(1, NZ // 2) as i:
                for s in range(2):
                    n = 2 * i + s
                    act.wait_ge(sm, n - 1)
                    take(n, s)
                    root(n - 1, 1 - s)
            act.wait_ge(vpr, 4)
            nc.scalar.activation(vctx[:], values(0), ACT.Copy).then_inc(vr, 1)
            act.wait_ge(cleared, 1)

            def spread(t):
                act.wait_ge(vpr, 4 if t < 4 else 5)
                v = values(t).rearrange("p (a h x) -> p a h x", h=2, x=HD)
                for h in range(2):
                    nc.scalar.activation(vp[:, :, h, t + 1, HD * h:HD * h + HD], v[:, :, h, :], ACT.Copy)

            for t in range(3):
                spread(t)
            root(NZ - 1, 1)
            for t in range(3, NT):
                spread(t)
            act.drain()

        @block.vector
        def _(dve):
            nc.vector.memset(ktp[:], 0.0)
            nc.vector.memset(vp[:], 0.0)
            dve.drain().then_inc(cleared, 1)
            norm.dve(dve)
            dve.sem_inc(ro, 2)
            dve.wait_ge(c_in, 80)

            def inverse(n, s):
                dve.wait_ge(sm, n + 1)
                nc.vector.tensor_scalar(rs[s][:], psB[:, C0:C0 + T], 1.0 / HD, EPS, ALU.mult, ALU.add)
                dve.drain()
                nc.vector.reciprocal(rs[s][:], rs[s][:])
                dve.drain().then_inc(iv, 1)

            def normalise(n, s):
                z = zT[:, ds(n, 1), :].rearrange("p o t -> p (o t)")
                dve.wait_ge(rt, n + 1)
                nc.vector.scalar_tensor_tensor(z, z, gain[:, ds(n, 1)], rs[s][:], op0=ALU.mult, op1=ALU.mult)
                dve.drain().then_inc(nz, 1)

            def rotate(n, s):
                z = zT[:, ds(n, 1), CTX:T].rearrange("p o t -> p (o t)")
                dve.wait_ge(tn, n + 1)
                nc.vector.tensor_tensor(turn[:], psR[s][:], sin[:], ALU.mult)
                nc.vector.tensor_tensor(z, z, cos[:], ALU.mult)
                dve.drain()
                nc.vector.tensor_tensor(z, z, turn[:], ALU.add)
                dve.drain().then_inc(ro, 1)

            inverse(0, 0)
            normalise(0, 0)
            with dve.Fori(1, NZ // 2) as i:
                for s in range(2):
                    n = 2 * i + s
                    rotate(n - 2, s)
                    inverse(n - 1, 1 - s)
                    normalise(n - 1, 1 - s)
            inverse(NZ - 1, 1)
            normalise(NZ - 1, 1)
            rotate(NZ - 2, 0)
            rotate(NZ - 1, 1)
            dve.sem_inc(kr, 1)
            for p in range(NKV):
                for h in range(2):
                    c = slice(HD * h, HD * h + HD)
                    nc.vector.tensor_copy(ktp[c, p, h, P:KCOLS], zT[c, NQ + p, :])
            dve.drain()


def attention(nc, cst, a, zT, ktp, vp, yT):
    units = [(c, b, h) for c in range(2) for b in range(NT) for h in range(2)]
    NU = len(units)

    def keys(b):
        if b == 0:
            return [1]
        return [0] + [2 + j for j in range(max(0, b - 2), min(NT - 2, b) + 1)]

    KIND = {0: 1, 1: 0, 2: 1, 3: 1, 4: 2}
    with nc.cleanup_on_exit(), ExitStack() as ctx:
        sb = lambda n, s, d=F32: ctx.enter_context(nc.sbuf_tensor(n, s, d))
        sem = lambda n: nc.alloc_semaphore(n)
        mask = sb("at_mask", [P, 3, 4 * P])
        sink = sb("at_sink", [P, AH])
        qs = [sb(f"at_qs{s}", [P, T]) for s in range(2)]
        ss = [sb(f"at_s{i}", [P, 4 * P]) for i in range(4)]
        pt = [sb(f"at_pt{i}", [P, 4, P]) for i in range(2)]
        nm, den, es = sb("at_nm", [P, NU]), sb("at_den", [P, NU]), sb("at_es", [P, NU])
        mx = sb("at_mx", [P, NU])
        psS = [ctx.enter_context(nc.psum_tensor(f"at_psS{i}", [P, 4 * P], F32)) for i in range(4)]
        psT = [ctx.enter_context(nc.psum_tensor(f"at_psT{i}", [P, 4, P], F32)) for i in range(2)]
        psO = ctx.enter_context(nc.psum_tensor("at_psO", [P, 2 * BANK], F32))
        c_in = sem("at_c_in")
        qr = sem("at_qr")
        sf = sem("at_sf")
        mr = sem("at_mr")
        er = sem("at_er")
        wr = sem("at_wr")
        tf = sem("at_tf")
        tr = sem("at_tr")
        of = sem("at_of")
        orr = sem("at_or")
        block = ctx.enter_context(nc.Block())

        def runs(eng, one):
            for p in range(NKV):
                with eng.Fori(0, 2) as i:
                    one(p, i + 2 * p)

        @block.sync
        def _(sp):
            sp.dma_start(mask[:], a["win_mask"]).then_inc(c_in, 16)
            sp.dma_start(sink[:], a["sinks"]).then_inc(c_in, 16)

        @block.tensor
        def _(pe):
            pe.sem_inc(tf, 4)
            pe.sem_inc(of, 2)

            def one(p, r):
                def score(v):
                    c, b, h = units[v]
                    pe.wait_ge(mr, NU * r + v + 1)
                    q, out = qs[c][:, P * b:P * b + P], psS[v % 4]
                    ks = keys(b)
                    if b == 0:
                        last = nc.tensor.matmul(out[:, 0:P], q, ktp[:, p, h, P:2 * P], start=True, stop=True)
                    else:
                        nc.tensor.matmul(out[:, 0:P], q, ktp[:, p, h, 0:P], start=True, stop=True)
                        n = len(ks) - 1
                        last = nc.tensor.matmul(out[:, P:P + n * P], q, ktp[:, p, h, P * ks[1]:P * ks[1] + n * P],
                                                start=True, stop=True)
                    last.then_inc(sf, 1)

                def turn(v):
                    pe.wait_ge(wr, NU * r + v + 1)
                    pe.wait_ge(tr, NU * r + v + 1)
                    for j in range(len(keys(units[v][1]))):
                        last = nc.tensor.transpose(psT[v % 2][:, j, :], ss[v % 4][:, P * j:P * j + P], cst.ident[:])
                    last.then_inc(tf, 1)

                def output(v):
                    c, b, h = units[v]
                    pe.wait_ge(tr, NU * r + v + 3)
                    if b == 0 and h == 0:
                        pe.wait_ge(orr, 2 * r + c + 1)
                    ks = keys(b)
                    for j, kt in enumerate(ks):
                        last = nc.tensor.matmul(psO[:, C0 + P * b:C0 + P * b + P], vp[:, p, h, kt, :], pt[v % 2][:, j, :],
                                                start=(h == 0 and j == 0), stop=(h == 1 and j == len(ks) - 1))
                    last.then_inc(of, 1)

                pe.wait_ge(qr, r + 1)
                for v in range(NU + 4):
                    if v < NU:
                        score(v)
                    if 3 <= v < NU + 3:
                        turn(v - 3)
                    if v >= 4:
                        output(v - 4)

            runs(pe, one)

        @block.scalar
        def _(act):
            act.sem_inc(tr, 2)
            act.wait_ge(c_in, 32)

            def one(p, r):
                def exps(v):
                    c, b, h = units[v]
                    w = P * len(keys(b))
                    act.wait_ge(mr, NU * r + v + 5)
                    nc.scalar.activation(ss[v % 4][:, 0:w], ss[v % 4][:, 0:w], ACT.Exp, bias=nm[:, v:v + 1],
                                         accum_out=den[:, v:v + 1])
                    nc.scalar.activation(es[:, v:v + 1], sink[:, ds(4 * r + 2 * c + h, 1)], ACT.Exp, bias=nm[:, v:v + 1])
                    act.drain().then_inc(er, 1)

                def move(v):
                    n = len(keys(units[v][1]))
                    act.wait_ge(tf, NU * r + v + 5)
                    act.wait_ge(of, NU * r + v + 1)
                    nc.scalar.activation(pt[v % 2][:, 0:n, :], psT[v % 2][:, 0:n, :], ACT.Copy).then_inc(tr, 1)

                for c in range(2):
                    nc.scalar.activation(qs[c][:], zT[:, ds(2 * r + c, 1), :].rearrange("p o t -> p (o t)"), ACT.Copy)
                act.drain().then_inc(qr, 1)
                for v in range(NU + 3):
                    if v >= 3:
                        move(v - 3)
                    if v < NU:
                        exps(v)

            runs(act, one)

        @block.vector
        def _(dve):
            dve.sem_inc(mr, 4)
            dve.sem_inc(orr, 1)
            dve.wait_ge(c_in, 32)

            def one(p, r):
                def step(v):
                    first, second = v < NU, v >= 2
                    if first:
                        c, b, h = units[v]
                        w = P * len(keys(b))
                        m = mask[:, 1, 0:w] if b == 0 else mask[:, KIND[b], 0:w]
                        dve.wait_ge(sf, NU * r + v + 1)
                        dve.wait_ge(tf, NU * r + v + 1)
                        nc.vector.scalar_tensor_tensor(ss[v % 4][:, 0:w], psS[v % 4][:, 0:w], SCALE, m,
                                                       op0=ALU.mult, op1=ALU.add)
                    if second:
                        u = v - 2
                        wu = P * len(keys(units[u][1]))
                        dve.wait_ge(er, NU * r + u + 1)
                        nc.vector.tensor_tensor(den[:, u:u + 1], den[:, u:u + 1], es[:, u:u + 1], ALU.add)
                    dve.drain()
                    if second:
                        nc.vector.reciprocal(den[:, u:u + 1], den[:, u:u + 1])
                    if first:
                        nc.vector.tensor_reduce(mx[:, v:v + 1], ss[v % 4][:, 0:w], AX, ALU.max)
                    dve.drain()
                    if first:
                        nc.vector.tensor_scalar(nm[:, v:v + 1], mx[:, v:v + 1], sink[:, ds(4 * r + 2 * c + h, 1)],
                                                -1.0, ALU.max, ALU.mult)
                    if second:
                        nc.vector.tensor_scalar(ss[u % 4][:, 0:wu], ss[u % 4][:, 0:wu], den[:, u:u + 1], None, ALU.mult)
                    dve.drain()
                    if first:
                        dve.sem_inc(mr, 1)
                    if second:
                        dve.sem_inc(wr, 1)

                def out(c):
                    dve.wait_ge(of, NU * r + 10 * c + 12)
                    nc.vector.tensor_scalar(yT[:, ds(2 * r + c, 1), :].rearrange("p o t -> p (o t)"),
                                            psO[:, C0:C0 + T], 1.0, None, ALU.mult)
                    dve.drain().then_inc(orr, 1)

                for v in range(NU + 2):
                    step(v)
                    if v == 13:
                        out(0)
                out(1)

            runs(dve, one)


class Const:
    pass


def program(nc, a):
    with ExitStack() as ctx:
        sb = lambda n, s, d=F32: ctx.enter_context(nc.sbuf_tensor(n, s, d))
        cst = Const()
        cst.XT = sb("XT", [P, KD, T])
        cst.cond = sb("cond", [P, KD, 2])
        cst.ones = sb("ones", [P, P])
        cst.ident = sb("ident", [P, P])
        cst.normw = None
        normw = [sb(f"normw{l}", [P, 2, KD, 2]) for l in range(2)]
        cst.iota = sb("iota", [P, P])
        mods = [sb(f"modT{l}", [P, NMOD * KD, 2]) for l in range(2)]
        with ExitStack() as c1:
            ld = c1.enter_context(nc.semaphore("first_in"))
            sil = c1.enter_context(nc.semaphore("first_silu"))
            block = c1.enter_context(nc.Block())

            @block.sync
            def _(sp):
                sp.dma_start(cst.cond[:], a["cond"]).then_inc(ld, 16)
                sp.dma_start(cst.XT[:], a["xT"]).then_inc(ld, 16)
                sp.dma_start(cst.ident[:], a["ident"]).then_inc(ld, 16)
                for l in range(2):
                    sp.dma_start(normw[l][:], a["normw"][l]).then_inc(ld, 16)
                sp.dma_start(cst.iota[:], a["iota"]).then_inc(ld, 16)
                sp.wait_ge(ld, 96)

            @block.scalar
            def _(act):
                act.wait_ge(ld, 96)
                nc.scalar.activation(cst.cond[:], cst.cond[:], ACT.Silu).then_inc(sil, 1)
                act.wait_ge(sil, 1)

            @block.vector
            def _(dve):
                nc.vector.memset(cst.ones[:], 1.0)
                dve.drain()

        modulation(nc, cst, a["ada_w"][0], a["ada_b"][0], mods[0], "_0")
        cst.normw = normw[0]
        with ExitStack() as c1:
            yT = c1.enter_context(nc.sbuf_tensor("yT", [P, KD, T], F32))
            rec_mixer(nc, cst, mods[0], a["rec_w_in"], a["rec_gn"], a["masks"], a["state"], a["new_state"], yT)
            out_projection(nc, cst, a["rec_w_out"], yT, mods[0], "_rec")
        gates = nc.dram_tensor("gates", [P, T // 32, NK, 32], F32, kind="Internal").ap()
        hid = nc.dram_tensor("hidden", [NK // 2, P, T], F32, kind="Internal").ap()
        peer(nc, cst, mods[0], a["wqk"][0], a["uT"][0], a["v"][0], gates, hid, "_p0",
             (a["ada_w"][1], a["ada_b"][1], mods[1]))
        cst.normw = normw[1]
        with ExitStack() as c1:
            zT = c1.enter_context(nc.sbuf_tensor("zT", [P, NQ + NKV, T], F32))
            ktp = c1.enter_context(nc.sbuf_tensor("ktp", [P, NKV, 2, KCOLS], F32))
            vp = c1.enter_context(nc.sbuf_tensor("vp", [P, NKV, 2, NT + 1, P], F32))
            attn_project(nc, cst, mods[1], a, zT, ktp, vp)
            yT = c1.enter_context(nc.sbuf_tensor("yTa", [P, KD, T], F32))
            attention(nc, cst, a, zT, ktp, vp, yT)
            out_projection(nc, cst, a["att_w_out"], yT, mods[1], "_att")
        peer(nc, cst, mods[1], a["wqk"][1], a["uT"][1], a["v"][1], gates, hid, "_p1")
        with ExitStack() as c1:
            sv = c1.enter_context(nc.semaphore("last_out"))
            block = c1.enter_context(nc.Block())

            @block.sync
            def _(sp):
                sp.dma_start(a["yT"], cst.XT[:]).then_inc(sv, 16)
                sp.wait_ge(sv, 16)


def level_masks():
    m = np.zeros((P, 2 * LEVELS, P), np.int32)
    s, t = np.arange(P)[:, None], np.arange(P)[None, :]
    for l in range(LEVELS):
        same = (s >> (l + 1)) == (t >> (l + 1))
        hs, ht = (s >> l) & 1, (t >> l) & 1
        m[:, l, :] = same & (hs == 0) & (ht == 1)
        m[:, LEVELS + l, :] = same & (hs == 1) & (ht == 0)
    return m


def attention_constants():
    p, t = np.arange(P), np.arange(LAT)
    nf, grid = HD // 4, 64
    e, part = p % 32, (p % HD) // 32
    freqs = np.float32(10000.0) ** (-np.arange(nf, dtype=np.float32) / np.float32(nf))
    place = np.where(part[:, None] == 0, t[None, :] // grid, t[None, :] % grid).astype(np.float32)
    angle = place * freqs[e % nf][:, None]
    rot = np.zeros((P, P), np.float32)
    for m in range(P):
        if m % 32 < nf:
            rot[m + nf, m] = -1.0
        else:
            rot[m - nf, m] = 1.0
    q, k = np.arange(P)[:, None], np.arange(P)[None, :]
    left, right, none = np.where(k >= q, 0, NEG), np.where(k <= q, 0, NEG), np.zeros((P, P))
    mask = np.stack([np.concatenate(r, 1) for r in ((none, none, right, none), (none, left, none, right),
                                                    (none, left, none, none))], 1)
    return {"cos": np.cos(angle).astype(np.float32), "sin": np.sin(angle).astype(np.float32), "rot": rot,
            "heads": (p[:, None] // HD == p[None, :] // HD).astype(np.float32), "win_mask": mask.astype(np.float32)}


def kernel(**inputs):
    import concourse.bacc as bacc
    from concourse.bass_utils import run_bass_kernel_spmd

    x = {n: np.asarray(v) for n, v in inputs.items()}
    L = x["ada_w"].shape[0]
    f = np.ascontiguousarray
    tok = np.concatenate([x["x_prompt"][0], x["x_sample"][0]], 0)
    cond = np.stack([x["c_ctx"], x["c"][0]], -1)
    arr = {
        "xT": f(tok.reshape(T, KD, P).transpose(2, 1, 0)),
        "cond": f(cond.reshape(KD, P, 2).transpose(1, 0, 2)),
        "ident": np.eye(P, dtype=np.float32),
        "normw": f(np.repeat(x["norm_w"].reshape(L, 2, KD, P).transpose(0, 3, 1, 2)[..., None], 2, -1)),
        "ada_w": f(x["ada_w"].reshape(L, KD, P, 12, 512).transpose(0, 3, 2, 1, 4)),
        "ada_b": f(np.repeat(x["ada_b"].reshape(L, NMOD * KD, P).transpose(0, 2, 1)[..., None], 2, -1)),
        "rec_w_in": f(x["rec_w_in"][0].reshape(KD, P, 5, RH, P)[:, :, [0, 1, 2, 4, 3]].transpose(3, 2, 1, 0, 4)),
        "rec_gn": f(x["rec_gn_w"].reshape(P, 1)),
        "masks": level_masks(),
        "state": f(x["state_rec"][0, 0]),
        "rec_w_out": f(x["rec_w_out"][0].reshape(KD, P, KD, P).transpose(2, 1, 0, 3)),
    }
    arr["iota"] = f(np.broadcast_to(np.arange(P, dtype=np.float32), (P, P)))
    wq = x["peer_w_q"].reshape(L, KD, P, PH, 2, P).transpose(0, 4, 3, 2, 1, 5)
    keys = x["peer_keys"].transpose(0, 2, 1, 4, 3)[:, :, :, :, None, :]
    arr["wqk"] = f(np.concatenate([wq, keys], 4).reshape(L, 2 * PH, P, KD + 1, P))
    arr["uT"] = f(x["peer_u"].reshape(L, NK, NK, KD, P).transpose(0, 2, 4, 3, 1))
    arr["v"] = f(x["peer_v"])
    outs = {"yT": (P, KD, T), "new_state": (2, RH, P, P)}
    w = x["attn_w_qkv"][0]
    wq = w[:, :AH * HD].reshape(KD, P, 2, 2, 4, HD).transpose(2, 4, 1, 0, 3, 5).reshape(NQ, P, KD, P)
    wk = w[:, AH * HD:(AH + AKV) * HD].reshape(KD, P, NKV, P).transpose(2, 1, 0, 3)
    arr["wqk_att"] = f(np.concatenate([wq, wk], 0))
    arr["wv_att"] = f(w[:, (AH + AKV) * HD:].reshape(KD, P, AKV * HD).transpose(1, 0, 2))
    arr["qk_gain"] = f(np.stack([np.tile(x["attn_qn_w"][0], 2)] * NQ + [np.tile(x["attn_kn_w"][0], 2)] * NKV, 1))
    arr["cache_k"] = f(x["cache_k"][0, 0].reshape(P, NKV, P).transpose(2, 1, 0))
    arr["cache_v"] = f(x["cache_v"][0, 0])
    arr["sinks"] = f(np.broadcast_to(x["attn_sink"][0].reshape(2, 2, 4).transpose(0, 2, 1).reshape(AH), (P, AH)))
    arr["att_w_out"] = f(x["attn_w_out"][0].reshape(2, 2, 4, HD, D).transpose(0, 2, 1, 3, 4)
                         .reshape(NQ, P, KD, P).transpose(2, 1, 0, 3))
    arr.update(attention_constants())
    outs["new_k"], outs["new_v"] = (P, NKV, CTX), (CTX, AKV * HD)
    nc = bacc.Bacc("TRN2", target_bir_lowering=False, num_devices=1)
    aps = {n: nc.dram_tensor("in_" + n, v.shape, mybir.dt.from_np(v.dtype), kind="ExternalInput").ap()
           for n, v in arr.items()}
    for n, s in outs.items():
        aps[n] = nc.dram_tensor("out_" + n, s, F32, kind="ExternalOutput").ap()
    aps["v"] = aps["v"].rearrange("l (i j) d -> l j i d", j=NK)
    program(nc, aps)
    r = run_bass_kernel_spmd(nc, [{"in_" + n: v for n, v in arr.items()}], core_ids=[0]).results[0]
    y = r["out_yT"].transpose(2, 1, 0).reshape(T, D)
    state = r["out_new_state"].reshape(1, 1, 2, RH, P, P)
    new_k = r["out_new_k"].transpose(2, 1, 0).reshape(1, 1, CTX, AKV, HD)
    new_v = r["out_new_v"].reshape(1, 1, CTX, AKV, HD)
    return (y[None, :CTX], y[None, CTX:], state, new_k, new_v)
```
